# Optimizing a Trainium2 kernel written in Bass

```python
import math
import jax
import jax.numpy as jnp
from jax import lax
import numpy as np

D_MODEL = 1024
BATCH = 1
SEQ = 512
DEPTH = 2

CHUNK = 64
HEAD_DIM = 64
NORM_EPS = 1e-6
D_FF = 2816
A_HEADS = 4
A_LEFT_CHUNKS = 8
A_REL_PAST = 128
A_REL_SIZE = CHUNK + A_REL_PAST
B_HEADS = 4
B_CONV = 4
C_Q_HEADS = 8
C_KV_HEADS = 2
C_WINDOW = 128
C_WINDOW_CHUNKS = C_WINDOW // CHUNK
ROPE_THETA = 10000.0
N_BRANCH = 3
N_ADA = 9
A_W = A_HEADS * HEAD_DIM
B_W = B_HEADS * HEAD_DIM
C_QW = C_Q_HEADS * HEAD_DIM
C_KVW = C_KV_HEADS * HEAD_DIM
IN_SIZES = (A_W, A_W, A_W, 3 * B_W, B_W, B_HEADS, B_HEADS, C_QW, C_KVW, C_KVW, N_BRANCH * D_MODEL)
IN_TOTAL = 3 * A_W + 4 * B_W + 2 * B_HEADS + C_QW + 2 * C_KVW + N_BRANCH * D_MODEL
F32 = jnp.float32

kernel_name = 'hybrid_chunk_causal_encoder_block'

def _rmsnorm(x, g):
    xf = x.astype(F32)
    y = xf * lax.rsqrt(jnp.mean(xf * xf, axis=-1, keepdims=True) + NORM_EPS)
    return (y * g.astype(F32)).astype(x.dtype)

def _l2norm(x):
    return x * lax.rsqrt(jnp.sum(x * x, axis=-1, keepdims=True) + NORM_EPS)

def _modulate(h, shift, scale):
    return h * (1.0 + scale) + shift

def _swiglu(h, w_in, w_out):
    gate, up = jnp.split(h @ w_in, 2, axis=-1)
    return (jax.nn.silu(gate) * up) @ w_out

def _split_cols(t, sizes):
    out, start = [], 0
    for s in sizes:
        out.append(t[..., start:start + s])
        start += s
    return out

def _rope(t, pos):
    half = HEAD_DIM // 2
    inv_freq = ROPE_THETA ** (-jnp.arange(half, dtype=F32) / half)
    ang = pos.astype(F32)[:, None] * inv_freq[None, :]
    cos = jnp.cos(ang)[None, :, None, :]
    sin = jnp.sin(ang)[None, :, None, :]
    t1 = t[..., :half].astype(F32)
    t2 = t[..., half:].astype(F32)
    return jnp.concatenate([t1 * cos - t2 * sin, t2 * cos + t1 * sin], axis=-1).astype(t.dtype)

def _chunk_band(t, n_prev):
    nc = t.shape[1]
    pad = [(0, 0)] * t.ndim
    pad[1] = (n_prev, 0)
    tp = jnp.pad(t, pad)
    return jnp.concatenate([tp[:, o:o + nc] for o in range(n_prev + 1)], axis=2)

def _band_valid(nc, n_prev):
    band = (n_prev + 1) * CHUNK
    return (jnp.arange(nc)[:, None] * CHUNK + jnp.arange(band)[None, :]) >= n_prev * CHUNK

def _chunked_relpos_attention(q, k, v, rel_bias):
    b_, s_, _ = q.shape
    nc = s_ // CHUNK
    band = (A_LEFT_CHUNKS + 1) * CHUNK
    q = q.reshape(b_, nc, CHUNK, A_HEADS, HEAD_DIM)
    k = _chunk_band(k.reshape(b_, nc, CHUNK, A_HEADS, HEAD_DIM), A_LEFT_CHUNKS)
    v = _chunk_band(v.reshape(b_, nc, CHUNK, A_HEADS, HEAD_DIM), A_LEFT_CHUNKS)
    s = jnp.einsum('bnqhd,bnkhd->bnhqk', q, k).astype(F32) * (HEAD_DIM ** -0.5)
    rel = A_LEFT_CHUNKS * CHUNK + jnp.arange(CHUNK)[:, None] - jnp.arange(band)[None, :]
    idx = jnp.clip(rel, -(CHUNK - 1), A_REL_PAST) + (CHUNK - 1)
    bias = rel_bias.astype(F32)[:, idx]
    valid = _band_valid(nc, A_LEFT_CHUNKS)
    s = jnp.where(valid[None, :, None, None, :], s + bias[None, None], -jnp.inf)
    p = jax.nn.softmax(s, axis=-1).astype(v.dtype)
    o = jnp.einsum('bnhqk,bnkhd->bnqhd', p, v)
    return o.reshape(b_, s_, A_W)

def _causal_depthwise_conv(x, w):
    ch = x.shape[-1]
    return lax.conv_general_dilated(
        x, w.reshape(B_CONV, 1, ch), window_strides=(1,), padding=[(B_CONV - 1, 0)],
        dimension_numbers=('NWC', 'WIO', 'NWC'), feature_group_count=ch)

def _delta_step(state, xs):
    q_n, k_n, u_n, w_n, gc_n, intra_n = xs
    v_new = u_n - jnp.einsum('bhcd,bhde->bhce', w_n, state)
    o = (jnp.einsum('bhcd,bhde->bhce', q_n * jnp.exp(gc_n)[..., None], state)
         + jnp.einsum('bhcj,bhje->bhce', intra_n, v_new))
    g_last = gc_n[..., -1:]
    k_dec = k_n * jnp.exp(g_last - gc_n)[..., None]
    state = state * jnp.exp(g_last)[..., None] + jnp.einsum('bhcd,bhce->bhde', k_dec, v_new)
    return state, o

def _gated_deltanet(qkv, z, a, b, conv_w, a_log, dt_bias, norm_g):
    b_, s_, _ = qkv.shape
    nc = s_ // CHUNK
    qkv = jax.nn.silu(_causal_depthwise_conv(qkv, conv_w))
    q, k, v = jnp.split(qkv.astype(F32), 3, axis=-1)
    q = _l2norm(q.reshape(b_, s_, B_HEADS, HEAD_DIM)) * (HEAD_DIM ** -0.5)
    k = _l2norm(k.reshape(b_, s_, B_HEADS, HEAD_DIM))
    v = v.reshape(b_, s_, B_HEADS, HEAD_DIM)
    beta = jax.nn.sigmoid(b.astype(F32))
    g = -jnp.exp(a_log.astype(F32)) * jax.nn.softplus(a.astype(F32) + dt_bias.astype(F32))

    def to_chunks(t):
        return jnp.moveaxis(t.reshape((b_, nc, CHUNK) + t.shape[2:]), 3, 1)

    q, k, v, beta, g = to_chunks(q), to_chunks(k), to_chunks(v), to_chunks(beta), to_chunks(g)
    gc = jnp.cumsum(g, axis=-1)
    pos = jnp.arange(CHUNK)
    incl = pos[:, None] >= pos[None, :]
    strict = pos[:, None] > pos[None, :]
    decay = jnp.exp(jnp.where(incl, gc[..., :, None] - gc[..., None, :], -jnp.inf))
    kb = k * beta[..., None]
    l_mat = jnp.where(strict, jnp.einsum('bhncd,bhnjd->bhncj', kb, k) * decay, 0.0)
    rhs = jnp.concatenate([v * beta[..., None], kb * jnp.exp(gc)[..., None]], axis=-1)
    sol = lax.linalg.triangular_solve(jnp.eye(CHUNK, dtype=F32) + l_mat, rhs,
                                      left_side=True, lower=True, unit_diagonal=True)
    u_val, w_dec = sol[..., :HEAD_DIM], sol[..., HEAD_DIM:]
    intra = jnp.einsum('bhncd,bhnjd->bhncj', q, k) * decay
    xs = tuple(jnp.moveaxis(t, 2, 0) for t in (q, k, u_val, w_dec, gc, intra))
    state0 = jnp.zeros((b_, B_HEADS, HEAD_DIM, HEAD_DIM), F32)
    _, o = lax.scan(_delta_step, state0, xs)
    o = jnp.moveaxis(jnp.moveaxis(o, 0, 2), 1, 3).reshape(b_, s_, B_HEADS, HEAD_DIM)
    zf = z.reshape(b_, s_, B_HEADS, HEAD_DIM).astype(F32)
    o = _rmsnorm(o, norm_g) * jax.nn.silu(zf)
    return o.reshape(b_, s_, B_W).astype(z.dtype)

def _sliding_window_sink_gqa(q, k, v, sinks):
    b_, s_, _ = q.shape
    nc = s_ // CHUNK
    grp = C_Q_HEADS // C_KV_HEADS
    n_prev = C_WINDOW_CHUNKS - 1
    pos = jnp.arange(s_)
    q = _rope(q.reshape(b_, s_, C_Q_HEADS, HEAD_DIM), pos)
    k = _rope(k.reshape(b_, s_, C_KV_HEADS, HEAD_DIM), pos)
    q = q.reshape(b_, nc, CHUNK, C_KV_HEADS, grp, HEAD_DIM)
    k = _chunk_band(k.reshape(b_, nc, CHUNK, C_KV_HEADS, HEAD_DIM), n_prev)
    v = _chunk_band(v.reshape(b_, nc, CHUNK, C_KV_HEADS, HEAD_DIM), n_prev)
    s = jnp.einsum('bnqhgd,bnjhd->bnhgqj', q, k).astype(F32) * (HEAD_DIM ** -0.5)
    valid = _band_valid(nc, n_prev)
    s = jnp.where(valid[None, :, None, None, None, :], s, -jnp.inf)
    sink = jnp.broadcast_to(sinks.astype(F32).reshape(C_KV_HEADS, grp)[None, None, :, :, None, None],
                            s.shape[:-1] + (1,))
    p = jax.nn.softmax(jnp.concatenate([s, sink], axis=-1), axis=-1)[..., :-1].astype(v.dtype)
    o = jnp.einsum('bnhgqj,bnjhd->bnqhgd', p, v)
    return o.reshape(b_, s_, C_QW)

def _token_mixing(u, w_in, rel_bias, conv_w, a_log, dt_bias, dn_norm_g, sinks, w_up_a, w_up_b, w_up_c, w_out):
    b_, s_, _ = u.shape
    aq, ak, av, b_qkv, b_z, b_a, b_b, cq, ck, cv, gate_logits = _split_cols(u @ w_in, IN_SIZES)
    y_a = _chunked_relpos_attention(aq, ak, av, rel_bias) @ w_up_a
    y_b = _gated_deltanet(b_qkv, b_z, b_a, b_b, conv_w, a_log, dt_bias, dn_norm_g) @ w_up_b
    y_c = _sliding_window_sink_gqa(cq, ck, cv, sinks) @ w_up_c
    gates = jax.nn.sigmoid(gate_logits.astype(F32)).astype(u.dtype).reshape(b_, s_, N_BRANCH, D_MODEL)
    merged = gates[:, :, 0] * y_a + gates[:, :, 1] * y_b + gates[:, :, 2] * y_c
    return merged @ w_out

def setup_inputs(seed: int = 0) -> dict:
    key = jax.random.key(seed)
    ks = jax.random.split(key, 24)

    def nrm(k, shape, scale):
        return jax.random.normal(k, shape, jnp.float32) * scale

    def gain(k, shape):
        return 1.0 + 0.05 * jax.random.normal(k, shape, jnp.float32)

    dt = jnp.exp(jax.random.uniform(ks[12], (DEPTH, B_HEADS), jnp.float32, math.log(1e-3), math.log(1e-1)))
    return {
        'x': nrm(ks[0], (BATCH, SEQ, D_MODEL), 1.0),
        'c': nrm(ks[1], (BATCH, D_MODEL), 1.0),
        'ada_w': nrm(ks[2], (DEPTH, D_MODEL, N_ADA * D_MODEL), 0.5 * D_MODEL ** -0.5),
        'ada_b': nrm(ks[3], (DEPTH, N_ADA * D_MODEL), 0.1),
        'ffn1_norm_g': gain(ks[4], (DEPTH, D_MODEL)),
        'ffn1_w_in': nrm(ks[5], (DEPTH, D_MODEL, 2 * D_FF), D_MODEL ** -0.5),
        'ffn1_w_out': nrm(ks[6], (DEPTH, D_FF, D_MODEL), D_FF ** -0.5),
        'mix_norm_g': gain(ks[7], (DEPTH, D_MODEL)),
        'mix_w_in': nrm(ks[8], (DEPTH, D_MODEL, IN_TOTAL), D_MODEL ** -0.5),
        'a_rel_bias': nrm(ks[9], (DEPTH, A_HEADS, A_REL_SIZE), 0.5),
        'b_conv_w': nrm(ks[10], (DEPTH, B_CONV, 3 * B_W), B_CONV ** -0.5),
        'b_a_log': jnp.log(jax.random.uniform(ks[11], (DEPTH, B_HEADS), jnp.float32, 1.0, 16.0)),
        'b_dt_bias': dt + jnp.log(-jnp.expm1(-dt)),
        'b_norm_g': gain(ks[13], (DEPTH, HEAD_DIM)),
        'c_sinks': nrm(ks[14], (DEPTH, C_Q_HEADS), 1.0),
        'w_up_a': nrm(ks[15], (DEPTH, A_W, D_MODEL), A_W ** -0.5),
        'w_up_b': nrm(ks[16], (DEPTH, B_W, D_MODEL), B_W ** -0.5),
        'w_up_c': nrm(ks[17], (DEPTH, C_QW, D_MODEL), C_QW ** -0.5),
        'mix_w_out': nrm(ks[18], (DEPTH, D_MODEL, D_MODEL), D_MODEL ** -0.5),
        'ffn2_norm_g': gain(ks[19], (DEPTH, D_MODEL)),
        'ffn2_w_in': nrm(ks[20], (DEPTH, D_MODEL, 2 * D_FF), D_MODEL ** -0.5),
        'ffn2_w_out': nrm(ks[21], (DEPTH, D_FF, D_MODEL), D_FF ** -0.5),
        'final_norm_g': gain(ks[22], (D_MODEL,)),
    }

def reference(x, c, ada_w, ada_b, ffn1_norm_g, ffn1_w_in, ffn1_w_out, mix_norm_g, mix_w_in, a_rel_bias,
              b_conv_w, b_a_log, b_dt_bias, b_norm_g, c_sinks, w_up_a, w_up_b, w_up_c, mix_w_out,
              ffn2_norm_g, ffn2_w_in, ffn2_w_out, final_norm_g):
    cond = jax.nn.silu(c)
    for l in range(DEPTH):
        mod = cond @ ada_w[l] + ada_b[l]
        sh1, sc1, g1, sh2, sc2, g2, sh3, sc3, g3 = [m[:, None, :] for m in jnp.split(mod, N_ADA, axis=-1)]
        h = _modulate(_rmsnorm(x, ffn1_norm_g[l]), sh1, sc1)
        x = x + 0.5 * g1 * _swiglu(h, ffn1_w_in[l], ffn1_w_out[l])
        h = _modulate(_rmsnorm(x, mix_norm_g[l]), sh2, sc2)
        x = x + g2 * _token_mixing(h, mix_w_in[l], a_rel_bias[l], b_conv_w[l], b_a_log[l], b_dt_bias[l],
                                   b_norm_g[l], c_sinks[l], w_up_a[l], w_up_b[l], w_up_c[l], mix_w_out[l])
        h = _modulate(_rmsnorm(x, ffn2_norm_g[l]), sh3, sc3)
        x = x + 0.5 * g3 * _swiglu(h, ffn2_w_in[l], ffn2_w_out[l])
    return _rmsnorm(x, final_norm_g)


_drawn_inputs = setup_inputs


def setup_inputs(seed=0):
    import zlib

    import numpy as np

    out = dict(_drawn_inputs(seed))
    spreads = {}
    factors = {'ffn1_norm_g': 5.019,
     'mix_norm_g': 3.318,
     'a_rel_bias': 3.478,
     'b_norm_g': 6.765,
     'c_sinks': 46.651,
     'ffn2_norm_g': 5.062}
    for name, (base, spread) in spreads.items():
        noise = np.random.default_rng([zlib.crc32(name.encode()), seed]).standard_normal(out[name].shape)
        drawn = base * np.exp(spread * noise) if base else spread * noise
        out[name] = jnp.asarray(drawn.astype(out[name].dtype))
    for name, factor in factors.items():
        out[name] = (out[name] * factor).astype(out[name].dtype)
    return out
```

```python
from contextlib import ExitStack

import numpy as np

import concourse.bass as bass
from concourse import mybir

F32 = mybir.dt.float32
F32R = mybir.dt.float32r
ALU = mybir.AluOpType
ACT = mybir.ActivationFunctionType
AX = mybir.AxisListType

P = 128
D_MODEL, SEQ, DEPTH = 1024, 512, 2
CHUNK, HEAD = 64, 64
D_FF = 2816
EPS = 1e-6
KD = D_MODEL // P
TT = SEQ // P
NCH = SEQ // CHUNK
F_HALF = (12, 10)
KMAX = max(F_HALF)
RAW = 4
UNITS = 180
SUB = 60
MIX = SUB
U_B, U_GATE, U_C, U_A = MIX, MIX + 8, MIX + 32, MIX + 38
U_UP, U_OUT = MIX + 44, MIX + 52
NEG = -1e30
assert 2 * (sum(F_HALF) * P) == 2 * D_FF and U_OUT + 8 == 2 * SUB

HEAD_OF_SLOT = (0, 2, 1, 3)
LEVELS = 6


class Signal:

    def __init__(self, sem, per_layer, credit=0):
        self.sem, self.per_layer, self.credit = sem, per_layer, credit

    def at(self, layer, n):
        return layer * self.per_layer + (n + self.credit)


def encoder_kernel(nc, a, out):
    ctx = ExitStack()
    with ctx:
        base = [16512]

        def place(name, shape, dt, at=None):
            size = 4 * int(np.prod(shape[1:]))
            size = (size + 31) // 32 * 32
            off = base[0] if at is None else at
            if at is None:
                base[0] += size
            return nc.alloc_sbuf_tensor_at(name, shape, dt, offset=off)

        x = place("x", [P, KD, SEQ], F32)
        UH0 = base[0]
        uh = place("uh", [P, KD, SEQ], F32R)
        ul = place("ul", [P, KD, SEQ], F32R)
        raw = place("raw", [P, RAW, KMAX * P], F32)
        wh = place("wh", [P, 2, KMAX * P], F32R)
        wl = place("wl", [P, 2, KMAX * P], F32R)
        ada_raw = place("ada_raw", [P, 2, KD * P], F32)
        ada_acc = place("ada_acc", [P, 24, P], F32)
        cond = place("cond", [P, KD], F32)
        ada_b = place("ada_b", [P, 6, 24], F32)
        norm_g = place("norm_g", [P, 6, KD], F32)
        final_g = place("final_g", [P, KD], F32)
        mod = place("mod", [P, 24], F32)
        scale_eff = place("scale_eff", [P, KD], F32)
        gate_eff = place("gate_eff", [P, KD], F32)
        ident = place("ident", [P, P], F32)
        ones_mean = place("ones_mean", [P, P], F32)
        eps = place("eps", [P, 2], F32)
        tri = place("tri", [P, P], F32)
        same_chunk = place("same_chunk", [P, P], F32)
        strict = place("strict", [P, P], F32)
        level_mask = place("level_mask", [P, LEVELS, P], F32)
        rot = place("rot", [P, P], F32)
        cos = place("cos", [P, SEQ], F32)
        sin = place("sin", [P, SEQ], F32)
        c_mask = place("c_mask", [P, 2 * P], F32)
        a_mask = place("a_mask", [P, 2 * P], F32)
        a_bias = place("a_bias", [P, 4, 2 * P], F32)
        a_far = place("a_far", [P, 4], F32)
        conv_w = place("conv_w", [P, 6, 4], F32)
        small = place("small", [P, 32], F32)
        ab_raw = place("ab_raw", [P, KD, 8], F32)
        ab_hi = place("ab_hi", [P, KD, 8], F32R)
        ab_lo = place("ab_lo", [P, KD, 8], F32R)
        sc = place("sc", [P, 256], F32)
        mx = place("mx", [P, 64], F32)
        egl = place("egl", [P, TT, 2, 2], F32)
        rstd = place("rstd", [P, SEQ], F32)
        ssq = place("ssq", [P, SEQ], F32)
        sq = place("sq", [P, 2, SEQ], F32)
        A0 = base[0]
        h32 = place("h32", [P, 2, SEQ], F32, A0 + 57344)
        silu_s = place("silu_s", [P, 2, SEQ], F32, A0 + 61440)
        hh = place("hh", [P, KMAX, SEQ], F32R, A0)
        hl = place("hl", [P, KMAX, SEQ], F32R, A0 + KMAX * 2048)
        t_buf = place("t_buf", [P, 2, SEQ], F32, A0 + 49152)
        u32 = place("u32", [P, 2, SEQ], F32, A0 + 49152 + 4096)
        ada0 = place("ada0", [P, 16, KD * P], F32, A0)
        ada0g = place("ada0g", [P, 8, KD * P], F32, UH0)
        oh = place("oh", [P, KD, SEQ], F32R, A0)
        ol = place("ol", [P, KD, SEQ], F32R, A0 + 16384)
        W0 = A0 + 32768
        bp = place("bp", [P, 8, SEQ], F32, W0)
        intra = place("intra", [P, TT, 4, P], F32, W0 + 16384)
        u_val = place("u_val", [P, TT, 4, HEAD], F32, W0 + 24576)
        wT = place("wT", [P, 2, SEQ], F32, A0)
        k_dec = place("k_dec", [P, TT, 4, HEAD], F32, A0 + 8192)
        st = place("st", [P, NCH + 1, 2, HEAD], F32, A0 + 12288)
        v_beta = place("v_beta", [P, 4, HEAD], F32, A0 + 17408)
        k_beta = place("k_beta", [P, 4, HEAD], F32, A0 + 18432)
        lT = place("lT", [P, 4, P], F32, A0 + 24576)
        Tm = place("Tm", [P, 4, P], F32, A0 + 26624)
        Um = place("Um", [P, 4, P], F32, A0 + 28672)
        Ym = place("Ym", [P, 4, P], F32, A0 + 30720)
        cT = place("cT", [P, 4, P], F32, A0 + 20480)
        eg = place("eg", [P, 2, P], F32, A0 + 22528)
        pc = place("pc", [P, 6, SEQ], F32, W0)
        v_tok = place("v_tok", [P, TT, 2 * P], F32, W0 + 12288)
        sco = place("sco", [P, 8, 2 * P], F32, W0 + 16384)
        pT = place("pT", [P, TT, SEQ], F32, W0 + 24576)
        g_in = place("g_in", [P, 2, 3, SEQ], F32, W0)
        up_m = place("up_m", [P, 4, SEQ], F32, W0 + 12288)
        assert A0 + 65536 <= 229368, A0 + 65536

        PS = ctx.enter_context(nc.psum_tensor("PS", [P, 8, SEQ], F32))
        gates_dram = nc.dram_tensor("gates_dram", (24, P, SEQ), F32, kind="Internal").ap()

        def sig(name, per_layer=0, credit=0):
            return Signal(ctx.enter_context(nc.semaphore(name)), per_layer, credit)

        arrived = [sig(f"arrived{j}", 16 * UNITS // RAW) for j in range(RAW)]
        hi_ready = sig("hi_ready", UNITS, RAW)
        lo_ready = sig("lo_ready", UNITS, RAW)
        unit_done = sig("unit_done", UNITS, 2)
        consts_in = sig("consts_in")
        cond_in = sig("cond_in")
        cond_done = sig("cond_done")
        layer_in = sig("layer_in", 16 * 5)
        x_in = sig("x_in")
        ada0_in = [sig(f"ada0_in{j}") for j in range(6)]
        ada_in = [sig(f"ada_in{j}") for j in range(2)]
        ada_step = sig("ada_step")
        ada_ready = sig("ada_ready")
        mods_mm = sig("mods_mm", 3)
        mods_done = sig("mods_done", 3)
        mod_step = sig("mod_step", 3)
        ada0_step = sig("ada0_step")
        bias_masked = sig("bias_masked", 1)
        norm_mm = sig("norm_mm", 3)
        root_done = sig("root_done", 3)
        rstd_done = sig("rstd_done", 3)
        t_done = sig("t_done", 24)
        u32_done = sig("u32_done", 24)
        uh_done = sig("uh_done", 24)
        ul_done = sig("ul_done", 24)
        silu_done = sig("silu_done", 44, 2)
        h_done = sig("h_done", 44, 2)
        hh_done = sig("hh_done", 44)
        hl_done = sig("hl_done", 44)
        x_done = sig("x_done", 40, 2)
        sq_done = sig("sq_done", 24)
        ssq_done = sig("ssq_done", 21)
        in_done = sig("in_done", 44, 4)
        ab_hi_done = sig("ab_hi_done", 1)
        ab_lo_done = sig("ab_lo_done", 1)
        ab_mm = sig("ab_mm", 1)
        gate_out = [sig(f"gate_out{j}", 16 * 12) for j in range(2)]
        gate_back = [sig(f"gate_back{j}", 16 * 4) for j in range(2)]
        conv_done = sig("conv_done", 6)
        conv_silu = sig("conv_silu", 6)
        conv_step = sig("conv_step", 18)
        l2_sq = sig("l2_sq", 4)
        l2_mm = sig("l2_mm", 4)
        l2_root = sig("l2_root", 4)
        l2_inv = sig("l2_inv", 4)
        qk_done = sig("qk_done", 4)
        ab_v = sig("ab_v", 7)
        ab_a = sig("ab_a", 7)
        gc_mm = sig("gc_mm", 1)
        gcb_mm = sig("gcb_mm", 4)
        kk_mm = sig("kk_mm", 4)
        tr_mm = sig("tr_mm", 4)
        diff_done = sig("diff_done", 4)
        decay_done = sig("decay_done", 4)
        eg_done = sig("eg_done", 4)
        mask_step = sig("mask_step", 16)
        lt_done = sig("lt_done", 4)
        tok_done = sig("tok_done", 4)
        qe_done = sig("qe_done", 4)
        ct_done = sig("ct_done", 24)
        u_done = sig("u_done", 24)
        tm_done = sig("tm_done", 20)
        y_mm = sig("y_mm", 24)
        y_done = sig("y_done", 20)
        z_mm = sig("z_mm", 20)
        uw_mm = sig("uw_mm", 4)
        uw_done = sig("uw_done", 4)
        settled = sig("settled")
        st_zero = sig("st_zero", 1)
        ws_mm = sig("ws_mm", 8)
        vnew_done = sig("vnew_done", 8)
        kv_mm = sig("kv_mm", 8)
        st_done = sig("st_done", 8)
        o_mm = sig("o_mm", 4)
        o_done = sig("o_done", 4)
        on_sq = sig("on_sq", 2)
        on_mm = sig("on_mm", 2)
        on_root = sig("on_root", 2)
        on_silu = sig("on_silu", 2)
        on_step = sig("on_step", 6)
        ob_hi = sig("ob_hi", 2)
        ob_lo = sig("ob_lo", 2)
        rot_mm = sig("rot_mm", 5)
        rot_step = sig("rot_step", 10)
        rope_done = sig("rope_done", 5)
        vt_mm = sig("vt_mm", 2)
        vt_done = sig("vt_done", 2)
        s_mm = sig("s_mm", 8)
        s_step = sig("s_step", 28)
        bias_done = sig("bias_done", 8)
        negmax_done = sig("negmax_done", 8)
        exp_done = sig("exp_done", 8)
        prob_done = sig("prob_done", 8)
        pt_mm = sig("pt_mm", 17)
        pt_done = sig("pt_done", 17)
        pv_mm = sig("pv_mm", 8)
        o_hi = sig("o_hi", 8)
        o_lo = sig("o_lo", 8)
        merge_step = sig("merge_step", 16)
        mg_used = sig("mg_used", 8, 2)
        mh_done = sig("mh_done", 8)
        ml_done = sig("ml_done", 8)
        out_ready = sig("out_ready")
        out_done = [sig(f"out_done{j}") for j in range(2)]

        block = ctx.enter_context(nc.Block())

        def out_index(l, sub, half, d):
            return (0, 16, 24)[sub] + (8 * half if sub != 1 else 0) + d

        def ada_lot(e, r, lot, step, done):
            r4 = r.rearrange("p u (k n) -> p u k n", k=KD)
            for u in range(4):
                last = e.tensor_tensor(r4[:, u], r4[:, u], cond[:, :].unsqueeze(2).broadcast_to([P, KD, P]), ALU.mult)
            last.then_inc(step.sem, 1)
            e.wait_ge(step.sem, done + 1)
            e.tensor_tensor(r[:, :, 0:512], r[:, :, 0:512], r[:, :, 512:1024], ALU.add).then_inc(step.sem, 1)
            e.wait_ge(step.sem, done + 2)
            e.tensor_tensor(r[:, :, 0:256], r[:, :, 0:256], r[:, :, 256:512], ALU.add).then_inc(step.sem, 1)
            e.wait_ge(step.sem, done + 3)
            e.tensor_tensor(ada_acc[:, 4 * lot:4 * lot + 4, :], r[:, :, 0:128], r[:, :, 128:256], ALU.add)\
                .then_inc(ada_ready.sem, 4)

        @block.sync
        def _(e):
            e.dma_start(cond[:, :], a["c"]).then_inc(cond_in.sem, 16)
            for t, src in ((ident, "ident"), (ones_mean, "ones_mean"), (eps, "eps"), (tri, "tri"),
                           (same_chunk, "same_chunk"), (strict, "strict"), (rot, "rot"), (cos, "cos"),
                           (sin, "sin"), (c_mask, "c_mask"), (a_mask, "a_mask"),
                           (final_g, "final_g")):
                e.dma_start(t[:, :], a[src]).then_inc(consts_in.sem, 16)
            for t, src in ((level_mask, "level_mask"), (ada_b, "ada_b"), (norm_g, "norm_g")):
                e.dma_start(t[:, :, :], a[src]).then_inc(consts_in.sem, 16)
            e.dma_start(x[:, :, :], a["x"]).then_inc(x_in.sem, 16)

            def load(l, m, j, src, K):
                n = l * UNITS + (4 * m + j + 1)
                e.wait_ge(hi_ready.sem, n)
                e.wait_ge(lo_ready.sem, n)
                e.dma_start(raw[:, j, 0:K * P], src).then_inc(arrived[j].sem, 16)

            with e.Fori(0, DEPTH) as l:
                def ffn(first, name):
                    m0 = first // RAW
                    for half, F in enumerate(F_HALF):
                        with e.Fori(0, F // 2) as i:
                            for j in range(4):
                                load(l, m0 + i, j, a[name + "_in"][l * 44 + F_HALF[0] * 2 * half + 4 * i + j], KD)
                        m0 += F // 2
                        with e.Fori(0, 2) as i:
                            for j in range(4):
                                load(l, m0 + i, j, a[f"{name}_out{half}"][l * 8 + 4 * i + j], F)
                        m0 += 2

                ffn(0, "ffn1")
                e.wait_ge(x_done.sem, x_done.at(l, 0))
                e.dma_start(ab_raw[:, :, :], a["w_ab"][l]).then_inc(layer_in.sem, 16)
                e.dma_start(a_bias[:, :, :], a["a_bias"][l]).then_inc(layer_in.sem, 16)
                e.dma_start(a_far[:, :], a["a_far"][l]).then_inc(layer_in.sem, 16)
                e.dma_start(conv_w[:, :, :], a["conv_w"][l]).then_inc(layer_in.sem, 16)
                e.dma_start(small[:, :], a["small"][l]).then_inc(layer_in.sem, 16)
                with e.Fori(0, 11) as i:
                    for j in range(4):
                        load(l, MIX // RAW + i, j, a["mix_in"][l * 44 + 4 * i + j], KD)
                with e.Fori(0, 2) as i:
                    for j in range(4):
                        load(l, U_UP // RAW + i, j, a["mix_up"][l * 8 + 4 * i + j], KD)
                with e.Fori(0, 2) as i:
                    for j in range(4):
                        load(l, U_OUT // RAW + i, j, a["mix_out"][l * 8 + 4 * i + j], KD)
                ffn(2 * SUB, "ffn2")
            for d in range(KD):
                e.wait_ge(out_ready.sem, d + 1)
                e.dma_start(out[:, d, :], sq[:, d % 2, :]).then_inc(out_done[d % 2].sem, 16)
            for j in range(2):
                e.wait_ge(out_done[j].sem, 16 * KD // 2)

        @block.gpsimd
        def _(e):
            for lot in (4, 0, 1, 5, 2, 3):
                dst = ada0[:, 4 * lot:4 * lot + 4, :] if lot < 4 else ada0g[:, 4 * lot - 16:4 * lot - 12, :]
                e.dma_start(dst, a["ada_w"][4 * lot:4 * lot + 4].rearrange("u p n -> p u n")).then_inc(ada0_in[lot].sem, 16)
            e.wait_ge(cond_done.sem, 1)
            for lot in (4, 5):
                e.wait_ge(ada0_in[lot].sem, 16)
                ada_lot(e, ada0g[:, 4 * lot - 16:4 * lot - 12, :], lot, ada_step, 3 * (lot - 4))

            with e.Fori(0, 3 * DEPTH - 1) as g:
                with e.Fori(0, 12) as i:
                    for j in range(2):
                        e.wait_ge(unit_done.sem, g * SUB + 4 * i + (2 * j + 3))
                        e.wait_ge(ada_ready.sem, g * 24 + 2 * i + (23 + j))
                        e.dma_start(ada_raw[:, j, :], a["ada_w"][g * 24 + 2 * i + (24 + j)]).then_inc(ada_in[j].sem, 16)
                    e.wait_ge(mods_mm.sem, g + 1)
                    for j in range(2):
                        n = g * 24 + 2 * i + j
                        r = ada_raw[:, j, :]
                        r3 = r.rearrange("p (k n) -> p k n", k=KD)
                        e.wait_ge(ada_in[j].sem, g * 192 + 16 * i + 16)
                        e.tensor_tensor(r3, r3, cond[:, :].unsqueeze(2).broadcast_to([P, KD, P]), ALU.mult)\
                            .then_inc(ada_step.sem, 1)
                        e.wait_ge(ada_step.sem, n * 3 + 7)
                        e.tensor_tensor(r[:, 0:512], r[:, 0:512], r[:, 512:1024], ALU.add).then_inc(ada_step.sem, 1)
                        e.wait_ge(ada_step.sem, n * 3 + 8)
                        e.tensor_tensor(r[:, 0:256], r[:, 0:256], r[:, 256:512], ALU.add).then_inc(ada_step.sem, 1)
                        e.wait_ge(ada_step.sem, n * 3 + 9)
                        e.tensor_tensor(ada_acc[:, bass.ds(2 * i + j, 1), :].rearrange("p a n -> p (a n)"),
                                        r[:, 0:128], r[:, 128:256], ALU.add).then_inc(ada_ready.sem, 1)

        @block.tensor
        def _(e):
            e.wait_ge(consts_in.sem, 16 * 15)

            def unit(l, n, j, K, bank, xh, xl, waits=None, ks=None):
                ks = range(K) if ks is None else ks
                if ks[0] == 0:
                    e.wait_ge(lo_ready.sem, n + (1 + RAW))
                for k in ks:
                    if waits is not None:
                        waits(k)
                    for w, v in ((wh, xh), (wh, xl), (wl, xh)):
                        mm = e.matmul(PS[:, bank, :], w[:, j % 2, k * P:(k + 1) * P], v[:, k, :],
                                      start=(k == 0 and w is wh and v is xh), stop=(k == K - 1 and w is wl))
                if ks[-1] == K - 1:
                    mm.then_inc(unit_done.sem, 1)

            def settle():
                e.sem_inc(settled.sem, 1)

            def norm_and_mods(l, s):
                e.wait_ge(ssq_done.sem, ssq_done.at(l, 7 * (s + 1)))
                e.matmul(PS[:, 6, :], ones_mean[:, :], ssq[:, :], start=True, stop=True).then_inc(norm_mm.sem, 1)

            def mods(l, s):
                e.wait_ge(ada_ready.sem, l * 72 + 24 * (s + 1))
                for v in range(24):
                    mm = e.matmul(PS[:, 7, v:v + 1], ada_acc[:, v, :], eps[:, 1:2], start=True, stop=True)
                mm.then_inc(mods_mm.sem, 1)

            def ffn(l, s, first):
                base_f = 22 * (s // 2)
                n0 = first
                for half, F in enumerate(F_HALF):
                    with e.Fori(0, F // 2) as i:
                        for j in range(4):
                            n = l * UNITS + 4 * i + (n0 + j)
                            f = l * 44 + 2 * i + (base_f + F_HALF[0] * half + j // 2)
                            e.wait_ge((h_done if j % 2 else silu_done).sem, f + 1)

                            def u_there(k):
                                e.wait_ge(ul_done.sem, ul_done.at(l, 8 * s + k + 1))
                            unit(l, n, j, KD, (0, 2, 1, 3)[j], uh, ul, u_there if j == 0 else None)
                    n0 += 2 * F
                    fs = base_f + (F_HALF[0] if half == 0 else 22)
                    with e.Fori(0, 2) as i:
                        for j in range(4):
                            n = l * UNITS + 4 * i + (n0 + j)
                            e.wait_ge(x_done.sem, l * 40 + 4 * i + (out_index(l, s, half, j) + 1))

                            def h_there(k):
                                if k >= F - 2:
                                    e.wait_ge(hl_done.sem, hl_done.at(l, fs - (F - 1 - k)))
                            unit(l, n, j, F, 4 + j % 2, hh, hl, h_there if j == 0 else None)
                    n0 += 8

            def mixing(l):
                def proj(j, n_local, i=None):
                    n = l * UNITS + n_local if i is None else l * UNITS + 4 * i + n_local
                    m = n_local - MIX
                    v = l * 44 + (m + 1) if i is None else l * 44 + 4 * i + (m + 1)
                    e.wait_ge(in_done.sem, v)

                    def u_there(k):
                        e.wait_ge(ul_done.sem, ul_done.at(l, 8 + k + 1))
                    unit(l, n, j, KD, j, uh, ul, u_there if n_local == MIX else None)

                with e.Fori(0, 2) as i:
                    for j in range(4):
                        proj(j, U_B + j, i)
                e.wait_ge(ab_lo_done.sem, ab_lo_done.at(l, 1))
                for t in range(TT):
                    for k in range(KD):
                        for v, w in ((uh, ab_hi), (ul, ab_hi), (uh, ab_lo)):
                            mm = e.matmul(PS[:, 6, 8 * t:8 * t + 8], v[:, k, t * P:(t + 1) * P], w[:, k, :],
                                          start=(k == 0 and v is uh and w is ab_hi), stop=(k == KD - 1 and w is ab_lo))
                mm.then_inc(ab_mm.sem, 1)
                for i in range(4):
                    e.wait_ge(l2_sq.sem, l2_sq.at(l, i + 1))
                    if i >= 2:
                        e.wait_ge(l2_root.sem, l2_root.at(l, i - 1))
                    e.matmul(PS[:, 4 + i % 2, :], same_chunk[:, :], sq[:, i % 2, :], start=True, stop=True)\
                        .then_inc(l2_mm.sem, 1)
                e.wait_ge(ab_v.sem, ab_v.at(l, 4))
                e.matmul(PS[:, 6, 32:48], tri[:, :], sc[:, 0:16], start=True, stop=True)
                e.matmul(PS[:, 6, 48:64], same_chunk[:, :], sc[:, 0:16], start=True, stop=True).then_inc(gc_mm.sem, 1)
                e.wait_ge(in_done.sem, in_done.at(l, 8))
                e.wait_ge(qk_done.sem, qk_done.at(l, 4))
                for t in range(TT):
                    c0, c1 = t * P, (t + 1) * P
                    if t >= 1:
                        e.wait_ge(tok_done.sem, tok_done.at(l, t))
                        e.wait_ge(uw_done.sem, uw_done.at(l, t))
                        e.wait_ge(lt_done.sem, lt_done.at(l, t))
                    e.wait_ge(ab_a.sem, ab_a.at(l, 5))
                    e.wait_ge(ab_v.sem, ab_v.at(l, 5))
                    for s in range(4):
                        e.matmul(PS[:, 5, s * P:(s + 1) * P],
                                 sc[:, 4 * t + s:4 * t + s + 1].broadcast_to([P, P]), tri[:, :], start=True, stop=True)
                    for s in range(4):
                        mm = e.matmul(PS[:, 6, s * P:(s + 1) * P],
                                      sc[:, 16 + 4 * t + s:17 + 4 * t + s].broadcast_to([P, P]), ident[:, :],
                                      start=True, stop=True)
                    mm.then_inc(gcb_mm.sem, 1)
                    for par in range(2):
                        r = slice(64 * par, 64 * par + 64)
                        for x2 in range(2):
                            for pair in range(2):
                                rhs = bp[r, (2 if x2 == 0 else 0) + pair, c0:c1]
                                mm = e.matmul(PS[:, 2 + par, (2 * x2 + pair) * P:(2 * x2 + pair + 1) * P],
                                              bp[r, 2 + pair, c0:c1], rhs, start=True, stop=True)
                    mm.then_inc(kk_mm.sem, 1)
                    for y in range(4):
                        if y == 2:
                            e.wait_ge(conv_silu.sem, conv_silu.at(l, 6))
                        mm = e.transpose(PS[:, 4, y * P:(y + 1) * P], bp[:, 2 + y, c0:c1], ident[:, :])
                    mm.then_inc(tr_mm.sem, 1)
                    for lv in range(LEVELS):
                        g = 6 * t + lv
                        gl = 5 * t + lv - 1
                        e.wait_ge(ct_done.sem, ct_done.at(l, g + 1))
                        if lv == 1:
                            e.wait_ge(eg_done.sem, eg_done.at(l, t + 1))
                        if lv == 0:
                            for s in range(4):
                                mm = e.transpose(PS[:, 7, s * P:(s + 1) * P], cT[:, s, :], ident[:, :])
                            mm.then_inc(y_mm.sem, 1)
                        else:
                            e.wait_ge(tm_done.sem, tm_done.at(l, gl + 1))
                            for s in range(4):
                                mm = e.matmul(PS[:, 5, s * P:(s + 1) * P], cT[:, s, :], Tm[:, s, :], start=True, stop=True)
                            mm.then_inc(y_mm.sem, 1)
                        e.wait_ge(in_done.sem, in_done.at(l, 8 + max(g - 1, 0)))
                        gn = l * UNITS + (U_GATE + g)
                        unit(l, gn, g, KD, g % 2, uh, ul, ks=range(0, 4))
                        if lv > 0:
                            e.wait_ge(y_done.sem, y_done.at(l, gl + 1))
                            e.wait_ge(u_done.sem, u_done.at(l, g))
                            for s in range(4):
                                mm = e.matmul(PS[:, 6, s * P:(s + 1) * P], Ym[:, s, :], Um[:, s, :], start=True, stop=True)
                            if lv < LEVELS - 1:
                                for s in range(4):
                                    mm = e.matmul(PS[:, 7, s * P:(s + 1) * P], Um[:, s, :], Ym[:, s, :], start=True, stop=True)
                            mm.then_inc(z_mm.sem, 1)
                        unit(l, gn, g, KD, g % 2, uh, ul, ks=range(4, 8))
                    e.wait_ge(u_done.sem, u_done.at(l, 6 * (t + 1)))
                    e.wait_ge(tok_done.sem, tok_done.at(l, t + 1))
                    for s in range(4):
                        e.matmul(PS[:, 5, s * HEAD:(s + 1) * HEAD], Um[:, s, :], v_beta[:, s, :], start=True, stop=True)
                    for s in range(4):
                        par, pair = s // 2, s % 2
                        mm = e.matmul(PS[64 * par:64 * par + 64, 5, 256 + pair * P:256 + (pair + 1) * P],
                                      k_beta[:, s, :], Um[:, s, :], start=True, stop=True)
                    mm.then_inc(uw_mm.sem, 1)
                e.wait_ge(st_zero.sem, st_zero.at(l, 1))
                e.wait_ge(uw_done.sem, uw_done.at(l, TT))
                for n in range(NCH):
                    t, pb = n // 2, 64 * (n % 2)
                    if n >= 1:
                        e.wait_ge(st_done.sem, st_done.at(l, n))
                    settle()
                    for s in range(4):
                        par, pair = s // 2, s % 2
                        r = slice(64 * par, 64 * par + 64)
                        mm = e.matmul(PS[pb:pb + 64, 2 + par, pair * HEAD:(pair + 1) * HEAD],
                                      wT[r, pair, n * CHUNK:(n + 1) * CHUNK], st[r, n, pair, :], start=True, stop=True)
                    mm.then_inc(ws_mm.sem, 1)
                    e.wait_ge(vnew_done.sem, vnew_done.at(l, n + 1))
                    settle()
                    for s in range(4):
                        par, pair = s // 2, s % 2
                        mm = e.matmul(PS[64 * par:64 * par + 64, 4 + n % 2, pair * HEAD:(pair + 1) * HEAD],
                                      k_dec[pb:pb + 64, t, s, :], u_val[pb:pb + 64, t, s, :], start=True, stop=True)
                    mm.then_inc(kv_mm.sem, 1)
                e.wait_ge(qe_done.sem, qe_done.at(l, TT))
                for t in range(TT):
                    if t >= 1:
                        e.wait_ge(o_done.sem, o_done.at(l, t))
                    for s in range(4):
                        par, pair = s // 2, s % 2
                        r = slice(64 * par, 64 * par + 64)
                        e.matmul(PS[r, 6 + pair, 0:P], u_val[:, t, s, :], intra[:, t, s, :], start=True, stop=True)
                    for s in range(4):
                        par, pair = s // 2, s % 2
                        r = slice(64 * par, 64 * par + 64)
                        for ch in range(2):
                            n = 2 * t + ch
                            mm = e.matmul(PS[r, 6 + pair, ch * CHUNK:(ch + 1) * CHUNK], st[r, n, pair, :],
                                          bp[r, pair, n * CHUNK:(n + 1) * CHUNK], start=False, stop=True,
                                          skip_group_check=True)
                    mm.then_inc(o_mm.sem, 1)
                e.wait_ge(st_done.sem, st_done.at(l, NCH))
                for i in range(2):
                    e.wait_ge(on_sq.sem, on_sq.at(l, i + 1))
                    e.matmul(PS[:, 4 + i, :], same_chunk[:, :], sq[:, i, :], start=True, stop=True)\
                        .then_inc(on_mm.sem, 1)

                e.wait_ge(in_done.sem, in_done.at(l, 32))
                for m in range(6):
                    proj(m % 4, U_C + m)
                for i in range(5):
                    e.wait_ge(in_done.sem, in_done.at(l, 32 + i + 1))
                    if i >= 2:
                        e.wait_ge(rope_done.sem, rope_done.at(l, i - 1))
                    elif i == 0:
                        e.wait_ge(on_root.sem, on_root.at(l, 2))
                    e.matmul(PS[:, 4 + i % 2, :], rot[:, :], pc[:, i, :], start=True, stop=True).then_inc(rot_mm.sem, 1)
                e.wait_ge(in_done.sem, in_done.at(l, 38))
                for t in range(TT):
                    mm = e.transpose(PS[:, 6, t * P:(t + 1) * P], pc[:, 5, t * P:(t + 1) * P], ident[:, :])
                mm.then_inc(vt_mm.sem, 1)
                e.wait_ge(rope_done.sem, rope_done.at(l, 5))
                e.wait_ge(vt_done.sem, vt_done.at(l, 1))
                for t in range(TT):
                    lo = 0 if t else P
                    if t >= 1:
                        e.wait_ge(bias_done.sem, bias_done.at(l, t))
                    for h in range(8):
                        r = slice(64 * (h // 4), 64 * (h // 4) + 64)
                        k0 = (t - 1) * P + lo
                        mm = e.matmul(PS[:, h // 2, (h % 2) * 256 + lo:(h % 2) * 256 + 256],
                                      pc[r, h % 4, t * P:(t + 1) * P], pc[r, 4, k0:(t + 1) * P], start=True, stop=True)
                    mm.then_inc(s_mm.sem, 1)
                    e.wait_ge(prob_done.sem, prob_done.at(l, t + 1))
                    n_pt = 2 * t - 1 if t else 0
                    kts = (0, 1) if t else (1,)
                    for z, kt in enumerate(kts):
                        if n_pt + z >= 1:
                            e.wait_ge(pt_done.sem, pt_done.at(l, n_pt + z))
                        for h in range(8):
                            mm = e.transpose(PS[:, 4 + h // 4, (h % 4) * P:(h % 4 + 1) * P],
                                             sco[:, h, kt * P:(kt + 1) * P], ident[:, :])
                        mm.then_inc(pt_mm.sem, 1)
                    e.wait_ge(pt_done.sem, pt_done.at(l, n_pt + len(kts)))
                    if t >= 1:
                        e.wait_ge(o_lo.sem, o_lo.at(l, t))
                    for kv in range(2):
                        for z, kt in enumerate(kts):
                            mm = e.matmul(PS[64 * kv:64 * kv + 64, 6, :], v_tok[:, t - 1 + kt, 64 * kv:64 * kv + 64],
                                          pT[:, 2 * kt + kv, :], start=(z == 0), stop=(z == len(kts) - 1))
                    mm.then_inc(pv_mm.sem, 1)

                e.wait_ge(o_lo.sem, o_lo.at(l, 4))
                for m in range(6):
                    proj((m + 2) % 4, U_A + m)
                e.wait_ge(in_done.sem, in_done.at(l, 44))
                for y in range(2):
                    for t in range(TT):
                        mm = e.transpose(PS[:, 6 + y, t * P:(t + 1) * P], pc[:, 4 + y, t * P:(t + 1) * P], ident[:, :])
                mm.then_inc(vt_mm.sem, 1)
                e.wait_ge(vt_done.sem, vt_done.at(l, 2))
                for t in range(TT):
                    if t >= 1:
                        e.wait_ge(bias_done.sem, bias_done.at(l, 4 + t))
                    for h in range(4):
                        r = slice(64 * (h % 2), 64 * (h % 2) + 64)
                        mm = e.matmul(PS[:, h, 0:(t + 1) * P], pc[r, h // 2, t * P:(t + 1) * P],
                                      pc[r, 2 + h // 2, 0:(t + 1) * P], start=True, stop=True)
                    mm.then_inc(s_mm.sem, 1)
                    e.wait_ge(prob_done.sem, prob_done.at(l, 4 + t + 1))
                    n_pt = 7 + t * (t + 1) // 2
                    for kt in range(t + 1):
                        if kt >= 2:
                            e.wait_ge(pt_done.sem, pt_done.at(l, n_pt + kt - 1))
                        elif t:
                            e.wait_ge(pt_done.sem, pt_done.at(l, n_pt))
                        for h in range(4):
                            sh = sco[:, 2 * h:2 * h + 2, :].rearrange("p a n -> p (a n)")
                            mm = e.transpose(PS[:, 4 + kt % 2, h * P:(h + 1) * P], sh[:, kt * P:(kt + 1) * P], ident[:, :])
                        mm.then_inc(pt_mm.sem, 1)
                    e.wait_ge(pt_done.sem, pt_done.at(l, n_pt + t + 1))
                    if t >= 1:
                        e.wait_ge(o_lo.sem, o_lo.at(l, 4 + t))
                    for h in range(4):
                        r = slice(64 * (h % 2), 64 * (h % 2) + 64)
                        for kt in range(t + 1):
                            mm = e.matmul(PS[r, 6, (h // 2) * P:(h // 2 + 1) * P], v_tok[:, kt, h * HEAD:(h + 1) * HEAD],
                                          pT[:, kt, h * P:(h + 1) * P], start=(kt == 0), stop=(kt == t))
                    mm.then_inc(pv_mm.sem, 1)

                e.wait_ge(o_lo.sem, o_lo.at(l, 8))
                for d in range(KD):
                    n = l * UNITS + (U_UP + d)
                    e.wait_ge(mg_used.sem, l * 8 + (d + 1))
                    e.wait_ge(lo_ready.sem, n + (1 + RAW))
                    for b, ks in enumerate((range(0, 2), range(2, 4), range(4, 8))):
                        for k in ks:
                            for w, v in ((wh, oh), (wh, ol), (wl, oh)):
                                mm = e.matmul(PS[:, 3 * (d % 2) + b, :], w[:, d % 2, k * P:(k + 1) * P], v[:, k, :],
                                              start=(k == ks[0] and w is wh and v is oh),
                                              stop=(k == ks[-1] and w is wl))
                    mm.then_inc(unit_done.sem, 1)
                with e.Fori(0, 2) as i:
                    for j in range(4):
                        n = l * UNITS + 4 * i + (U_OUT + j)
                        e.wait_ge(x_done.sem, l * 40 + 4 * i + (out_index(l, 1, 0, j) + 1))

                        def m_there(k):
                            e.wait_ge(ml_done.sem, ml_done.at(l, k + 1))
                        unit(l, n, j, KD, 6 + j % 2, uh, ul, m_there if j == 0 else None)

            with e.Fori(0, DEPTH) as l:
                norm_and_mods(l, 0)
                mods(l, 0)
                ffn(l, 0, 0)
                norm_and_mods(l, 1)
                mods(l, 1)
                mixing(l)
                norm_and_mods(l, 2)
                mods(l, 2)
                ffn(l, 2, 2 * SUB)
            e.wait_ge(ssq_done.sem, 7 * (3 * DEPTH + 1))
            e.matmul(PS[:, 6, :], ones_mean[:, :], ssq[:, :], start=True, stop=True).then_inc(norm_mm.sem, 1)

        def steps(e, l, first, count, K, nxt, split, use):
            bodies, m0 = count // 4, first // 4

            def body(i, last):
                for j in range(4):
                    if j < 3:
                        split(l, m0, i, j + 1, K)
                    elif not last:
                        split(l, m0 + 1, i, 0, K)
                    elif nxt is not None:
                        split(l, m0 + 1, i, 0, nxt)
                    use(i, j)
            if bodies > 1:
                with e.Fori(0, bodies - 1) as i:
                    body(i, False)
            body(bodies - 1, True)

        @block.scalar
        def _(e):
            def split(l, m0, i, j, K):
                e.wait_ge(arrived[j].sem, l * (16 * UNITS // RAW) + 16 * i + 16 * (m0 + 1))
                e.wait_ge(unit_done.sem, l * UNITS + 4 * i + (4 * m0 + j + 1))
                e.activation(wh[:, j % 2, 0:K * P], raw[:, j, 0:K * P], ACT.Copy).then_inc(hi_ready.sem, 1)

            def multiplied(l, n, i=0):
                e.wait_ge(unit_done.sem, l * UNITS + 4 * i + (n + 3))

            def square(l, s, d):
                if d >= 3:
                    e.wait_ge(ssq_done.sem, ssq_done.at(l, 7 * (s + 1) + d - 2))
                e.activation(ssq[:, :] if d == 0 else sq[:, d % 2, :], x[:, d, :], ACT.Square).then_inc(sq_done.sem, 1)

            def norm(l, s):
                e.wait_ge(norm_mm.sem, norm_mm.at(l, s + 1))
                e.activation(rstd[:, :], PS[:, 6, :], ACT.Sqrt, bias=eps[:, 0:1]).then_inc(root_done.sem, 1)
                e.wait_ge(mods_done.sem, mods_done.at(l, s + 1))
                for k in range(KD):
                    c = 8 * s + k
                    e.wait_ge(t_done.sem, t_done.at(l, c + 1))
                    if k >= 2:
                        e.wait_ge(ul_done.sem, ul_done.at(l, c - 1))
                    e.activation(u32[:, k % 2, :], t_buf[:, k % 2, :], ACT.Identity, scale=scale_eff[:, k:k + 1],
                                 bias=mod[:, k:k + 1]).then_inc(u32_done.sem, 1)
                    e.wait_ge(u32_done.sem, u32_done.at(l, c + 1))
                    e.activation(uh[:, k, :], u32[:, k % 2, :], ACT.Copy).then_inc(uh_done.sem, 1)

            def ffn(l, s, first, last):
                base_f = 22 * (s // 2)
                for half, F in enumerate(F_HALF):
                    f0 = base_f + F_HALF[0] * half

                    def use_in(i, j):
                        multiplied(l, first + j, i)
                        f = l * 44 + 2 * i + (f0 + j // 2)
                        if j % 2 == 0:
                            e.wait_ge(h_done.sem, f + 1)
                            e.activation(silu_s[:, j // 2, :], PS[:, j // 2, :], ACT.Silu).then_inc(silu_done.sem, 1)
                        else:
                            e.wait_ge(h_done.sem, f + 3)
                            dst = hh[:, bass.ds(2 * i + j // 2, 1), :].rearrange("p a n -> p (a n)")
                            e.activation(dst, h32[:, j // 2, :], ACT.Copy).then_inc(hh_done.sem, 1)

                    steps(e, l, first, 2 * F, KD, F, split, use_in)
                    first += 2 * F

                    def use_out(i, j):
                        if half == 1:
                            d = 4 * i + j
                            e.wait_ge(x_done.sem, x_done.at(l, out_index(l, s, half, d) + 1))
                            square(l, s, d)
                    for i in range(2):
                        for j in range(4):
                            nxt = F if 4 * i + j < 7 else (KD if half == 0 or not last else None)
                            if nxt is not None:
                                split(l, first // 4 + (j + 1) // 4, i, (j + 1) % 4, nxt)
                            use_out(i, j)
                    first += 8

            def mixing(l):
                e.wait_ge(layer_in.sem, layer_in.at(l, 80))
                e.activation(ab_hi[:, :, :], ab_raw[:, :, :], ACT.Copy).then_inc(ab_hi_done.sem, 1)
                m_b = U_B // 4
                for m in range(8):
                    split(l, m_b, (m + 1) // 4, (m + 1) % 4, KD)
                    multiplied(l, U_B + m)
                    e.activation(bp[:, m, :], PS[:, m % 4, :], ACT.Copy).then_inc(in_done.sem, 1)
                    if 1 <= m <= 6:
                        e.wait_ge(conv_done.sem, conv_done.at(l, m))
                        e.activation(bp[:, m - 1, :], t_buf[:, (m - 1) % 2, :], ACT.Silu).then_inc(conv_silu.sem, 1)
                for i in range(4):
                    e.wait_ge(conv_silu.sem, conv_silu.at(l, i + 1))
                    if i >= 2:
                        e.wait_ge(l2_mm.sem, l2_mm.at(l, i - 1))
                    e.activation(sq[:, i % 2, :], bp[:, i, :], ACT.Square).then_inc(l2_sq.sem, 1)
                    if i >= 2:
                        e.wait_ge(qk_done.sem, qk_done.at(l, i - 1))
                    e.wait_ge(l2_mm.sem, l2_mm.at(l, i + 1))
                    e.activation(h32[:, i % 2, :], PS[:, 4 + i % 2, :], ACT.Sqrt, bias=eps[:, 0:1])\
                        .then_inc(l2_root.sem, 1)
                e.wait_ge(ab_v.sem, ab_v.at(l, 2))
                e.activation(sc[:, 80:96], sc[:, 64:80], ACT.Abs).then_inc(ab_a.sem, 1)
                e.wait_ge(ab_a.sem, ab_a.at(l, 1))
                e.activation(sc[:, 96:112], sc[:, 80:96], ACT.Exp, scale=-1.0).then_inc(ab_a.sem, 1)
                e.activation(sc[:, 224:228], small[:, 4:8], ACT.Exp).then_inc(ab_a.sem, 1)
                e.wait_ge(ab_a.sem, ab_a.at(l, 2))
                e.activation(sc[:, 112:128], sc[:, 96:112], ACT.Ln, bias=eps[:, 1:2]).then_inc(ab_a.sem, 1)
                e.activation(sc[:, 16:32].rearrange("p (t s) -> p t s", t=TT),
                             sc[:, 32:64].rearrange("p (t s) -> p t s", t=TT)[:, :, 4:8], ACT.Sigmoid)\
                    .then_inc(ab_a.sem, 1)
                e.wait_ge(ab_v.sem, ab_v.at(l, 6))
                e.activation(sc[:, 176:192], sc[:, 128:144], ACT.Exp).then_inc(ab_a.sem, 1)
                e.activation(sc[:, 160:176], sc[:, 208:224], ACT.Exp).then_inc(ab_a.sem, 1)

                def gate_use(g):
                    multiplied(l, U_GATE + g)
                    if g >= 2:
                        e.wait_ge(gate_out[g % 2].sem, gate_out[g % 2].at(l, 16 * (g // 2)))
                    e.activation(silu_s[:, g % 2, :], PS[:, g % 2, :], ACT.Sigmoid).then_inc(in_done.sem, 1)
                    e.wait_ge(in_done.sem, in_done.at(l, 8 + g + 1))
                    e.dma_start(gates_dram[g], silu_s[:, g % 2, :]).then_inc(gate_out[g % 2].sem, 16)

                for t in range(TT):
                    e.wait_ge(diff_done.sem, diff_done.at(l, t + 1))
                    if t >= 1:
                        e.wait_ge(z_mm.sem, z_mm.at(l, 5 * t))
                    e.activation(Ym[:, :, :], lT[:, :, :], ACT.Exp).then_inc(decay_done.sem, 1)
                    if t >= 1:
                        e.wait_ge(qe_done.sem, qe_done.at(l, t))
                    for par in range(2):
                        r = slice(64 * par, 64 * par + 64)
                        last = e.activation(eg[r, :, :], PS[r, 5, par * 256:par * 256 + 256]
                                            .rearrange("p (a n) -> p a n", a=2), ACT.Exp)
                    last.then_inc(eg_done.sem, 1)
                    for lv in range(LEVELS):
                        g = 6 * t + lv
                        if lv >= 1:
                            e.wait_ge(y_mm.sem, y_mm.at(l, g + 1))
                            e.activation(Ym[:, :, :], PS[:, 5, :].rearrange("p (s n) -> p s n", s=4), ACT.Copy)\
                                .then_inc(y_done.sem, 1)
                        split(l, (U_GATE + g + 1) // 4, 0, (g + 1) % 4, KD)
                        if g >= 1:
                            gate_use(g - 1)
                    e.wait_ge(uw_mm.sem, uw_mm.at(l, t + 1))
                    e.activation(u_val[:, t, :, :], PS[:, 5, 0:256].rearrange("p (s n) -> p s n", s=4), ACT.Copy)
                    e.activation(wT[:, :, t * P:(t + 1) * P], PS[:, 5, 256:512].rearrange("p (a n) -> p a n", a=2),
                                 ACT.Copy).then_inc(uw_done.sem, 1)
                gate_use(23)
                for t in range(TT):
                    e.wait_ge(o_mm.sem, o_mm.at(l, t + 1))
                    e.activation(bp[:, 4:6, t * P:(t + 1) * P], PS[:, 6:8, 0:P], ACT.Copy).then_inc(o_done.sem, 1)
                for i in range(2):
                    e.wait_ge(o_done.sem, o_done.at(l, TT))
                    e.activation(sq[:, i, :], bp[:, 4 + i, :], ACT.Square).then_inc(on_sq.sem, 1)
                for i in range(2):
                    e.activation(bp[:, 6 + i, :], bp[:, 6 + i, :], ACT.Silu).then_inc(on_silu.sem, 1)
                for i in range(2):
                    e.wait_ge(on_mm.sem, on_mm.at(l, i + 1))
                    e.activation(h32[:, i, :], PS[:, 4 + i, :], ACT.Sqrt, scale=1.0 / HEAD, bias=eps[:, 0:1])\
                        .then_inc(on_root.sem, 1)
                for i in range(2):
                    e.wait_ge(on_step.sem, on_step.at(l, 3 * (i + 1)))
                    e.activation(oh[:, 2 + i, :], bp[:, 4 + i, :], ACT.Copy).then_inc(ob_hi.sem, 1)

                def project(m, first, count, dst):
                    n = first + m
                    split(l, (n + 1) // 4, 0, (n + 1) % 4, KD)
                    multiplied(l, n)
                    e.activation(dst[:, m, :], PS[:, n % 4, :], ACT.Copy).then_inc(in_done.sem, 1)

                def probs_T(n, prob_tile, banks, dst):
                    e.wait_ge(pt_mm.sem, pt_mm.at(l, n + 1))
                    e.activation(dst, banks, ACT.Copy).then_inc(pt_done.sem, 1)

                e.wait_ge(ob_lo.sem, ob_lo.at(l, 2))
                for q in range(2):
                    e.wait_ge(gate_out[q].sem, gate_out[q].at(l, 16 * 12))
                for m in range(6):
                    project(m, U_C, 6, pc)
                e.wait_ge(vt_mm.sem, vt_mm.at(l, 1))
                e.activation(v_tok[:, :, 0:P], PS[:, 6, :].rearrange("p (t n) -> p t n", t=TT), ACT.Copy)\
                    .then_inc(vt_done.sem, 1)
                n = 0
                for t in range(TT):
                    lo = 0 if t else P
                    e.wait_ge(negmax_done.sem, negmax_done.at(l, t + 1))
                    for h in range(8):
                        e.activation(sco[:, h, lo:256], sco[:, h, lo:256], ACT.Exp, bias=mx[:, 16 + h:17 + h],
                                     accum_out=mx[:, 32 + h:33 + h])
                    e.wait_ge(s_step.sem, s_step.at(l, 5 * t + 3))
                    e.activation(mx[:, 40:48], mx[:, 24:32], ACT.Exp).then_inc(exp_done.sem, 1)
                    if t >= 1:
                        e.wait_ge(pv_mm.sem, pv_mm.at(l, t))
                    for kt in ((0, 1) if t else (1,)):
                        probs_T(n, t, PS[:, 4:6, :], pT[:, 2 * kt:2 * kt + 2, :])
                        n += 1
                    e.wait_ge(pv_mm.sem, pv_mm.at(l, t + 1))
                    e.activation(oh[:, 4:8, t * P:(t + 1) * P], PS[:, 6, :].rearrange("p (a n) -> p a n", a=4),
                                 ACT.Copy).then_inc(o_hi.sem, 1)
                for m in range(6):
                    project(m, U_A, 6, pc)
                e.wait_ge(vt_mm.sem, vt_mm.at(l, 2))
                e.activation(v_tok[:, :, :].rearrange("p t (y n) -> p y t n", y=2),
                             PS[:, 6:8, :].rearrange("p y (t n) -> p y t n", t=TT), ACT.Copy).then_inc(vt_done.sem, 1)
                for t in range(TT):
                    w = (t + 1) * P
                    e.wait_ge(negmax_done.sem, negmax_done.at(l, 4 + t + 1))
                    for h in range(4):
                        sh = sco[:, 2 * h:2 * h + 2, :].rearrange("p a n -> p (a n)")
                        last = e.activation(sh[:, 0:w], sh[:, 0:w], ACT.Exp, bias=mx[:, 16 + h:17 + h],
                                            accum_out=mx[:, 32 + h:33 + h])
                    last.then_inc(exp_done.sem, 1)
                    if t >= 1:
                        e.wait_ge(pv_mm.sem, pv_mm.at(l, 4 + t))
                    for kt in range(t + 1):
                        probs_T(n, t, PS[:, 4 + kt % 2, :], pT[:, kt, :])
                        n += 1
                    e.wait_ge(pv_mm.sem, pv_mm.at(l, 4 + t + 1))
                    e.activation(oh[:, 0:2, t * P:(t + 1) * P], PS[:, 6, 0:256].rearrange("p (a n) -> p a n", a=2),
                                 ACT.Copy).then_inc(o_hi.sem, 1)
                def gates_in(d):
                    e.dma_start(g_in[:, d % 2, :, :],
                                gates_dram.rearrange("(b d) p n -> d p b n", b=3)[d]).then_inc(gate_back[d % 2].sem, 16)
                e.wait_ge(o_lo.sem, o_lo.at(l, 8))
                for q in range(2):
                    e.wait_ge(gate_out[q].sem, gate_out[q].at(l, 16 * 12))
                gates_in(0)
                gates_in(1)
                for d in range(KD):
                    n = U_UP + d
                    split(l, (n + 1) // 4, 0, (n + 1) % 4, KD)
                    e.wait_ge(merge_step.sem, merge_step.at(l, 2 * (d + 1)))
                    e.activation(uh[:, d, :], up_m[:, 3, :], ACT.Copy).then_inc(mh_done.sem, 1)
                    if d + 2 < KD:
                        e.wait_ge(mg_used.sem, mg_used.at(l, d + 1))
                        gates_in(d + 2)
                for d in range(KD):
                    n = U_OUT + d
                    split(l, (n + 1) // 4, 0, (n + 1) % 4, KD)
                    e.wait_ge(x_done.sem, x_done.at(l, out_index(l, 1, 0, d) + 1))
                    square(l, 1, d)

            e.wait_ge(cond_in.sem, 16)
            e.activation(cond[:, :], cond[:, :], ACT.Silu).then_inc(cond_done.sem, 1)
            e.sem_inc(hi_ready.sem, RAW)
            e.wait_ge(x_in.sem, 16)
            e.wait_ge(consts_in.sem, 16 * 15)
            for d in range(KD):
                square(0, -1, d)
            with e.Fori(0, DEPTH) as l:
                split(l, 0, 0, 0, KD)
                norm(l, 0)
                ffn(l, 0, 0, False)
                norm(l, 1)
                mixing(l)
                norm(l, 2)
                ffn(l, 2, 2 * SUB, True)
            e.wait_ge(norm_mm.sem, 3 * DEPTH + 1)
            e.activation(rstd[:, :], PS[:, 6, :], ACT.Sqrt, bias=eps[:, 0:1]).then_inc(root_done.sem, 1)

        @block.vector
        def _(e):
            TTo, TS, STT = e.tensor_tensor, e.tensor_scalar, e.scalar_tensor_tensor

            def split(l, m0, i, j, K):
                e.wait_ge(hi_ready.sem, l * UNITS + 4 * i + (4 * m0 + j + 1 + RAW))
                TTo(wl[:, j % 2, 0:K * P], raw[:, j, 0:K * P], wh[:, j % 2, 0:K * P], ALU.subtract)\
                    .then_inc(lo_ready.sem, 1)

            def multiplied(l, n, i=0):
                e.wait_ge(unit_done.sem, l * UNITS + 4 * i + (n + 3))

            def add_square(l, s, d):
                if d == 0:
                    return
                e.wait_ge(sq_done.sem, sq_done.at(l, 8 * (s + 1) + d + 1))
                if d >= 2:
                    e.wait_ge(ssq_done.sem, ssq_done.at(l, 7 * (s + 1) + d - 1))
                TTo(ssq[:, :], ssq[:, :], sq[:, d % 2, :], ALU.add).then_inc(ssq_done.sem, 1)

            def norm(l, s):
                e.wait_ge(root_done.sem, root_done.at(l, s + 1))
                e.reciprocal(rstd[:, :], rstd[:, :]).then_inc(rstd_done.sem, 1)
                e.wait_ge(mods_mm.sem, mods_mm.at(l, s + 1))
                q = bass.ds(l * 3 + s, 1)
                TTo(mod[:, :], PS[:, 7, 0:24], ada_b[:, q, :].rearrange("p a n -> p (a n)"), ALU.add)\
                    .then_inc(mod_step.sem, 1)
                e.wait_ge(mod_step.sem, mod_step.at(l, s + 1))
                STT(out=scale_eff[:, :], in0=mod[:, 8:16], scalar=1.0,
                    in1=norm_g[:, q, :].rearrange("p a n -> p (a n)"), op0=ALU.add, op1=ALU.mult)
                TS(gate_eff[:, :], mod[:, 16:24], 1.0 if s == 1 else 0.5, None, ALU.mult).then_inc(mods_done.sem, 1)
                e.wait_ge(rstd_done.sem, rstd_done.at(l, s + 1))

                def scaled(k):
                    if k >= 2:
                        e.wait_ge(u32_done.sem, u32_done.at(l, 8 * s + k - 1))
                    TTo(t_buf[:, k % 2, :], x[:, k, :], rstd[:, :], ALU.mult).then_inc(t_done.sem, 1)
                scaled(0)
                scaled(1)
                for k in range(KD):
                    e.wait_ge(uh_done.sem, uh_done.at(l, 8 * s + k + 1))
                    TTo(ul[:, k, :], u32[:, k % 2, :], uh[:, k, :], ALU.subtract).then_inc(ul_done.sem, 1)
                    if k + 2 < KD:
                        scaled(k + 2)

            def residual(l, s, half, d, bank):
                STT(out=x[:, d, :], in0=PS[:, bank, :], scalar=gate_eff[:, d:d + 1], in1=x[:, d, :],
                    op0=ALU.mult, op1=ALU.add).then_inc(x_done.sem, 1)

            def ffn(l, s, first, last):
                base_f = 22 * (s // 2)
                for half, F in enumerate(F_HALF):
                    f0 = base_f + F_HALF[0] * half

                    def use_in(i, j):
                        if j % 2 == 0:
                            return
                        f = l * 44 + 2 * i + (f0 + j // 2)
                        multiplied(l, first + j, i)
                        e.wait_ge(silu_done.sem, f + 3)
                        TTo(h32[:, j // 2, :], silu_s[:, j // 2, :], PS[:, 2 + j // 2, :], ALU.mult)\
                            .then_inc(h_done.sem, 1)
                        e.wait_ge(hh_done.sem, f + 1)
                        slot = bass.ds(2 * i + j // 2, 1)
                        TTo(hl[:, slot, :].rearrange("p a n -> p (a n)"), h32[:, j // 2, :],
                            hh[:, slot, :].rearrange("p a n -> p (a n)"), ALU.subtract).then_inc(hl_done.sem, 1)

                    steps(e, l, first, 2 * F, KD, F, split, use_in)
                    first += 2 * F
                    for i in range(2):
                        for j in range(4):
                            nxt = F if 4 * i + j < 7 else (KD if half == 0 or not last else None)
                            if nxt is not None:
                                split(l, first // 4 + (j + 1) // 4, i, (j + 1) % 4, nxt)
                            multiplied(l, first + j, i)
                            residual(l, s, half, 4 * i + j, 4 + j % 2)
                            if half == 1:
                                add_square(l, s, 4 * i + j)
                    first += 8

            def mixing(l):
                e.wait_ge(ab_hi_done.sem, ab_hi_done.at(l, 1))
                TTo(ab_lo[:, :, :], ab_raw[:, :, :], ab_hi[:, :, :], ALU.subtract).then_inc(ab_lo_done.sem, 1)
                TTo(a_bias[:, :, :], a_bias[:, :, :], a_mask[:, :].unsqueeze(1).broadcast_to([P, 4, 2 * P]), ALU.add)\
                    .then_inc(bias_masked.sem, 1)
                for m in range(8):
                    split(l, U_B // 4, (m + 1) // 4, (m + 1) % 4, KD)
                    if m >= 6:
                        continue
                    e.wait_ge(in_done.sem, in_done.at(l, m + 1))
                    if m >= 2:
                        e.wait_ge(conv_silu.sem, conv_silu.at(l, m - 1))
                    y, v = t_buf[:, m % 2, :], bp[:, m, :]
                    TS(y, v, conv_w[:, m, 3:4], None, ALU.mult).then_inc(conv_step.sem, 1)
                    for back in (1, 2, 3):
                        e.wait_ge(conv_step.sem, conv_step.at(l, 3 * m + back))
                        STT(out=y[:, back:], in0=v[:, :SEQ - back], scalar=conv_w[:, m, 3 - back:4 - back],
                            in1=y[:, back:], op0=ALU.mult, op1=ALU.add)\
                            .then_inc((conv_step if back < 3 else conv_done).sem, 1)
                e.wait_ge(ab_mm.sem, ab_mm.at(l, 1))
                e.tensor_copy(sc[:, 32:64], PS[:, 6, 0:32]).then_inc(ab_v.sem, 1)
                e.wait_ge(ab_v.sem, ab_v.at(l, 1))
                by_t = lambda c: sc[:, c:c + 16].rearrange("p (t s) -> p t s", t=TT)
                TTo(by_t(64), sc[:, 32:64].rearrange("p (t s) -> p t s", t=TT)[:, :, 0:4],
                    small[:, 0:4].unsqueeze(1).broadcast_to([P, TT, 4]), ALU.add).then_inc(ab_v.sem, 1)
                for i in range(4):
                    e.wait_ge(l2_root.sem, l2_root.at(l, i + 1))
                    e.reciprocal(h32[:, i % 2, :], h32[:, i % 2, :]).then_inc(l2_inv.sem, 1)
                    e.wait_ge(l2_inv.sem, l2_inv.at(l, i + 1))
                    STT(out=bp[:, i, :], in0=bp[:, i, :], scalar=HEAD ** -0.5 if i < 2 else 1.0, in1=h32[:, i % 2, :],
                        op0=ALU.mult, op1=ALU.mult).then_inc(qk_done.sem, 1)
                e.wait_ge(ab_a.sem, ab_a.at(l, 4))
                STT(out=sc[:, 192:208], in0=sc[:, 64:80], scalar=0.0, in1=sc[:, 112:128], op0=ALU.max, op1=ALU.add)\
                    .then_inc(ab_v.sem, 1)
                e.wait_ge(ab_v.sem, ab_v.at(l, 3))
                STT(out=by_t(0), in0=by_t(192), scalar=-1.0, in1=sc[:, 224:228].unsqueeze(1).broadcast_to([P, TT, 4]),
                    op0=ALU.mult, op1=ALU.mult).then_inc(ab_v.sem, 1)
                e.wait_ge(gc_mm.sem, gc_mm.at(l, 1))
                e.tensor_copy(sc[:, 128:160], PS[:, 6, 32:64]).then_inc(ab_v.sem, 1)
                e.wait_ge(ab_v.sem, ab_v.at(l, 5))
                TTo(sc[:, 208:224], sc[:, 144:160], sc[:, 128:144], ALU.subtract).then_inc(ab_v.sem, 1)
                e.wait_ge(ab_a.sem, ab_a.at(l, 7))
                TTo(sc[:, 192:208], sc[:, 16:32], sc[:, 176:192], ALU.mult).then_inc(ab_v.sem, 1)

                by_s = lambda m: m.unsqueeze(1).broadcast_to([P, 4, P])
                heads = lambda v: v.rearrange("p (a b n) -> p b a n", a=2, b=2)
                slots = lambda v: v.rearrange("p (b a) n -> p b a n", a=2)
                ps4 = lambda b: PS[:, b, :].rearrange("p (s n) -> p s n", s=4)

                def per_head(c):
                    return sc[:, c:c + 4].rearrange("p (b a) -> p b a", a=2).unsqueeze(3).broadcast_to([P, 2, 2, HEAD])

                for t in range(TT):
                    c0, c1 = t * P, (t + 1) * P
                    e.wait_ge(gcb_mm.sem, gcb_mm.at(l, t + 1))
                    if t >= 1:
                        e.wait_ge(ct_done.sem, ct_done.at(l, 6 * t))
                    for s in range(4):
                        last = TS(lT[:, s, :], PS[:, 5, s * P:(s + 1) * P], sc[:, 128 + 4 * t + s:129 + 4 * t + s], 0.0,
                                  ALU.subtract, ALU.min)
                    last.then_inc(diff_done.sem, 1)
                    e.wait_ge(decay_done.sem, decay_done.at(l, t + 1))
                    TTo(Ym[:, :, :], Ym[:, :, :], by_s(tri[:, :]), ALU.mult).then_inc(mask_step.sem, 1)
                    e.wait_ge(kk_mm.sem, kk_mm.at(l, t + 1))
                    e.wait_ge(mask_step.sem, mask_step.at(l, 4 * t + 1))
                    for par in range(2):
                        last = TTo(intra[:, t, 2 * par:2 * par + 2, :],
                            PS[:, 2 + par, 256:512].rearrange("p (a n) -> p a n", a=2), Ym[:, 2 * par:2 * par + 2, :],
                            ALU.mult)
                    last.then_inc(mask_step.sem, 1)
                    e.wait_ge(mask_step.sem, mask_step.at(l, 4 * t + 2))
                    TTo(Ym[:, :, :], Ym[:, :, :], by_s(strict[:, :]), ALU.mult).then_inc(mask_step.sem, 1)
                    e.wait_ge(mask_step.sem, mask_step.at(l, 4 * t + 3))
                    for par in range(2):
                        last = TTo(lT[:, 2 * par:2 * par + 2, :],
                                   PS[:, 2 + par, 0:256].rearrange("p (a n) -> p a n", a=2),
                                   Ym[:, 2 * par:2 * par + 2, :], ALU.mult)
                    last.then_inc(mask_step.sem, 1)
                    e.wait_ge(mask_step.sem, mask_step.at(l, 4 * t + 4))
                    TTo(lT[:, :, :], lT[:, :, :], ps4(6), ALU.mult).then_inc(lt_done.sem, 1)
                    e.wait_ge(lt_done.sem, lt_done.at(l, t + 1))

                    def blocks(lv):
                        g = 6 * t + lv
                        if g >= 1:
                            e.wait_ge(y_mm.sem, y_mm.at(l, g))
                        if lv == 1:
                            e.wait_ge(u_done.sem, u_done.at(l, 6 * t + 1))
                        TTo(cT[:, :, :], lT[:, :, :], by_s(level_mask[:, lv, :]), ALU.mult).then_inc(ct_done.sem, 1)

                    blocks(0)
                    e.wait_ge(ct_done.sem, ct_done.at(l, 6 * t + 1))
                    if t >= 1:
                        e.wait_ge(uw_mm.sem, uw_mm.at(l, t))
                    TTo(Um[:, :, :], by_s(ident[:, :]), cT[:, :, :], ALU.subtract).then_inc(u_done.sem, 1)
                    for lv in range(LEVELS):
                        g = 6 * t + lv
                        if lv == 0:
                            e.wait_ge(y_mm.sem, y_mm.at(l, g + 1))
                            TTo(Tm[:, :, :], by_s(ident[:, :]), ps4(7), ALU.subtract).then_inc(tm_done.sem, 1)
                        if lv < LEVELS - 1:
                            blocks(lv + 1)
                        split(l, (U_GATE + g + 1) // 4, 0, (g + 1) % 4, KD)
                        if lv == 1:
                            e.wait_ge(tr_mm.sem, tr_mm.at(l, t + 1))
                            e.wait_ge(ab_v.sem, ab_v.at(l, 7))
                            TTo(slots(v_beta[:, :, :]), heads(PS[:, 4, 256:512]), per_head(16 + 4 * t), ALU.mult)
                            TTo(slots(k_beta[:, :, :]), heads(PS[:, 4, 0:256]), per_head(192 + 4 * t), ALU.mult)
                            TTo(slots(k_dec[:, t, :, :]), heads(PS[:, 4, 0:256]), per_head(160 + 4 * t), ALU.mult)\
                                .then_inc(tok_done.sem, 1)
                        if lv == 0:
                            e.wait_ge(eg_done.sem, eg_done.at(l, t + 1))
                            e.tensor_copy(egl[:, t, :, :], eg[:, :, CHUNK - 1::CHUNK])
                            TTo(bp[:, 0:2, c0:c1], bp[:, 0:2, c0:c1], eg[:, :, :], ALU.mult).then_inc(qe_done.sem, 1)
                        if lv >= 1:
                            e.wait_ge(z_mm.sem, z_mm.at(l, 5 * t + lv))
                            if lv < LEVELS - 1:
                                TTo(Tm[:, :, :], Tm[:, :, :], ps4(7), ALU.subtract).then_inc(tm_done.sem, 1)
                            e.wait_ge(u_done.sem, u_done.at(l, g))
                            TTo(Um[:, :, :], Um[:, :, :], ps4(6), ALU.subtract).then_inc(u_done.sem, 1)
                e.memset(st[:, 0, :, :], 0.0).then_inc(st_zero.sem, 1)
                e.wait_ge(uw_done.sem, uw_done.at(l, TT))
                e.wait_ge(qe_done.sem, qe_done.at(l, TT))
                e.wait_ge(st_zero.sem, st_zero.at(l, 1))
                for n in range(NCH):
                    t, pb = n // 2, 64 * (n % 2)
                    e.wait_ge(ws_mm.sem, ws_mm.at(l, n + 1))
                    for par in range(2):
                        v = u_val[pb:pb + 64, t, 2 * par:2 * par + 2, :]
                        last = TTo(v, v, PS[pb:pb + 64, 2 + par, 0:2 * HEAD].rearrange("p (a n) -> p a n", a=2),
                                   ALU.subtract)
                    last.then_inc(vnew_done.sem, 1)
                    e.wait_ge(kv_mm.sem, kv_mm.at(l, n + 1))
                    if n >= 1:
                        e.wait_ge(st_done.sem, st_done.at(l, n))
                    for pair in range(2):
                        last = STT(out=st[:, n + 1, pair, :], in0=st[:, n, pair, :], scalar=egl[:, t, pair, n % 2:n % 2 + 1],
                                   in1=PS[:, 4 + n % 2, pair * HEAD:(pair + 1) * HEAD], op0=ALU.mult, op1=ALU.add)
                    last.then_inc(st_done.sem, 1)
                for i in range(2):
                    e.wait_ge(on_root.sem, on_root.at(l, i + 1))
                    e.reciprocal(h32[:, i, :], h32[:, i, :]).then_inc(on_step.sem, 1)
                    e.wait_ge(on_step.sem, on_step.at(l, 3 * i + 1))
                    STT(out=bp[:, 4 + i, :], in0=bp[:, 4 + i, :], scalar=small[:, 8:9], in1=h32[:, i, :],
                        op0=ALU.mult, op1=ALU.mult).then_inc(on_step.sem, 1)
                    e.wait_ge(on_step.sem, on_step.at(l, 3 * i + 2))
                    e.wait_ge(on_silu.sem, on_silu.at(l, i + 1))
                    TTo(bp[:, 4 + i, :], bp[:, 4 + i, :], bp[:, 6 + i, :], ALU.mult).then_inc(on_step.sem, 1)
                for i in range(2):
                    e.wait_ge(ob_hi.sem, ob_hi.at(l, i + 1))
                    TTo(ol[:, 2 + i, :], bp[:, 4 + i, :], oh[:, 2 + i, :], ALU.subtract).then_inc(ob_lo.sem, 1)

                for m in range(6):
                    n = U_C + m
                    split(l, (n + 1) // 4, 0, (n + 1) % 4, KD)
                for i in range(5):
                    e.wait_ge(rot_mm.sem, rot_mm.at(l, i + 1))
                    TTo(h32[:, i % 2, :], PS[:, 4 + i % 2, :], sin[:, :], ALU.mult).then_inc(rot_step.sem, 1)
                    TTo(pc[:, i, :], pc[:, i, :], cos[:, :], ALU.mult).then_inc(rot_step.sem, 1)
                    e.wait_ge(rot_step.sem, rot_step.at(l, 2 * i + 2))
                    TTo(pc[:, i, :], pc[:, i, :], h32[:, i % 2, :], ALU.add).then_inc(rope_done.sem, 1)
                n_pt = 0
                for t in range(TT):
                    lo = 0 if t else P
                    e.wait_ge(s_mm.sem, s_mm.at(l, t + 1))
                    if t >= 1:
                        e.wait_ge(pt_mm.sem, pt_mm.at(l, n_pt))
                    n_pt += 2 if t else 1
                    STT(out=sco[:, :, lo:256], in0=PS[:, 0:4, :].rearrange("p b (c n) -> p (b c) n", c=2)[:, :, lo:256],
                        scalar=HEAD ** -0.5, in1=c_mask[:, :].unsqueeze(1).broadcast_to([P, 8, 2 * P])[:, :, lo:256],
                        op0=ALU.mult, op1=ALU.add).then_inc(bias_done.sem, 1)
                    e.wait_ge(bias_done.sem, bias_done.at(l, t + 1))
                    e.tensor_reduce(mx[:, 0:8], sco[:, :, lo:256], AX.X, ALU.max).then_inc(s_step.sem, 1)
                    e.wait_ge(s_step.sem, s_step.at(l, 5 * t + 1))
                    TTo(mx[:, 8:16], mx[:, 0:8], small[:, 16:24], ALU.max).then_inc(s_step.sem, 1)
                    e.wait_ge(s_step.sem, s_step.at(l, 5 * t + 2))
                    TS(mx[:, 16:24], mx[:, 8:16], -1.0, None, ALU.mult).then_inc(negmax_done.sem, 1)
                    TTo(mx[:, 24:32], small[:, 16:24], mx[:, 8:16], ALU.subtract).then_inc(s_step.sem, 1)
                    e.wait_ge(exp_done.sem, exp_done.at(l, t + 1))
                    TTo(mx[:, 48:56], mx[:, 32:40], mx[:, 40:48], ALU.add).then_inc(s_step.sem, 1)
                    e.wait_ge(s_step.sem, s_step.at(l, 5 * t + 4))
                    e.reciprocal(mx[:, 56:64], mx[:, 48:56]).then_inc(s_step.sem, 1)
                    e.wait_ge(s_step.sem, s_step.at(l, 5 * t + 5))
                    TTo(sco[:, :, lo:256], sco[:, :, lo:256],
                        mx[:, 56:64].unsqueeze(2).broadcast_to([P, 8, 2 * P])[:, :, lo:256], ALU.mult)\
                        .then_inc(prob_done.sem, 1)
                    e.wait_ge(o_hi.sem, o_hi.at(l, t + 1))
                    TTo(ol[:, 4:8, t * P:(t + 1) * P], PS[:, 6, :].rearrange("p (a n) -> p a n", a=4),
                        oh[:, 4:8, t * P:(t + 1) * P], ALU.subtract).then_inc(o_lo.sem, 1)

                for m in range(6):
                    n = U_A + m
                    split(l, (n + 1) // 4, 0, (n + 1) % 4, KD)
                e.wait_ge(bias_masked.sem, bias_masked.at(l, 1))
                sA = sco[:, :, :].rearrange("p (h a) n -> p h (a n)", a=2)
                for t in range(TT):
                    w, near = (t + 1) * P, max(t - 1, 0) * P
                    e.wait_ge(s_mm.sem, s_mm.at(l, 4 + t + 1))
                    e.wait_ge(pt_mm.sem, pt_mm.at(l, n_pt))
                    n_pt += t + 1
                    if near:
                        for h in range(4):
                            TS(sA[:, h, 0:near], PS[:, h, 0:near], HEAD ** -0.5, a_far[:, h:h + 1], ALU.mult, ALU.add)
                    STT(out=sA[:, :, near:w], in0=PS[:, 0:4, near:w], scalar=HEAD ** -0.5,
                        in1=a_bias[:, :, 256 - (w - near):256], op0=ALU.mult, op1=ALU.add).then_inc(bias_done.sem, 1)
                    e.wait_ge(bias_done.sem, bias_done.at(l, 4 + t + 1))
                    e.tensor_reduce(mx[:, 0:4], sA[:, :, 0:w], AX.X, ALU.max).then_inc(s_step.sem, 1)
                    e.wait_ge(s_step.sem, s_step.at(l, 20 + 2 * t + 1))
                    TS(mx[:, 16:20], mx[:, 0:4], -1.0, None, ALU.mult).then_inc(negmax_done.sem, 1)
                    e.wait_ge(exp_done.sem, exp_done.at(l, 4 + t + 1))
                    e.reciprocal(mx[:, 56:60], mx[:, 32:36]).then_inc(s_step.sem, 1)
                    e.wait_ge(s_step.sem, s_step.at(l, 20 + 2 * t + 2))
                    TTo(sA[:, :, 0:w], sA[:, :, 0:w], mx[:, 56:60].unsqueeze(2).broadcast_to([P, 4, w]), ALU.mult)\
                        .then_inc(prob_done.sem, 1)
                    e.wait_ge(o_hi.sem, o_hi.at(l, 4 + t + 1))
                    TTo(ol[:, 0:2, t * P:(t + 1) * P], PS[:, 6, 0:256].rearrange("p (a n) -> p a n", a=2),
                        oh[:, 0:2, t * P:(t + 1) * P], ALU.subtract).then_inc(o_lo.sem, 1)

                for d in range(KD):
                    n = U_UP + d
                    split(l, (n + 1) // 4, 0, (n + 1) % 4, KD)
                    multiplied(l, n)
                    e.wait_ge(gate_back[d % 2].sem, gate_back[d % 2].at(l, 16 * (d // 2 + 1)))
                    for b in range(3):
                        last = TTo(up_m[:, b, :], g_in[:, d % 2, b, :], PS[:, 3 * (d % 2) + b, :], ALU.mult)
                    last.then_inc(mg_used.sem, 1)
                    e.wait_ge(mg_used.sem, mg_used.at(l, d + 1))
                    TTo(up_m[:, 0, :], up_m[:, 0, :], up_m[:, 1, :], ALU.add).then_inc(merge_step.sem, 1)
                    e.wait_ge(merge_step.sem, merge_step.at(l, 2 * d + 1))
                    TTo(up_m[:, 3, :], up_m[:, 0, :], up_m[:, 2, :], ALU.add).then_inc(merge_step.sem, 1)
                    e.wait_ge(mh_done.sem, mh_done.at(l, d + 1))
                    TTo(ul[:, d, :], up_m[:, 3, :], uh[:, d, :], ALU.subtract).then_inc(ml_done.sem, 1)
                for d in range(KD):
                    n = U_OUT + d
                    split(l, (n + 1) // 4, 0, (n + 1) % 4, KD)
                    multiplied(l, n)
                    residual(l, 1, 0, d, 6 + d % 2)
                    add_square(l, 1, d)

            for s in (lo_ready, unit_done, silu_done, h_done, x_done, in_done, mg_used):
                e.sem_inc(s.sem, s.credit)
            e.wait_ge(cond_done.sem, 1)
            for lot in range(4):
                e.wait_ge(ada0_in[lot].sem, 16)
                ada_lot(e, ada0[:, 4 * lot:4 * lot + 4, :], lot, ada0_step, 3 * lot)
            e.wait_ge(x_in.sem, 16)
            e.wait_ge(consts_in.sem, 16 * 15)
            for d in range(KD):
                add_square(0, -1, d)
            with e.Fori(0, DEPTH) as l:
                split(l, 0, 0, 0, KD)
                norm(l, 0)
                ffn(l, 0, 0, False)
                norm(l, 1)
                mixing(l)
                norm(l, 2)
                ffn(l, 2, 2 * SUB, True)
            e.wait_ge(root_done.sem, 3 * DEPTH + 1)
            e.reciprocal(rstd[:, :], rstd[:, :]).then_inc(rstd_done.sem, 1)
            e.wait_ge(rstd_done.sem, 3 * DEPTH + 1)
            for d in range(KD):
                if d >= 2:
                    e.wait_ge(out_done[d % 2].sem, 16 * (d // 2))
                STT(out=sq[:, d % 2, :], in0=x[:, d, :], scalar=final_g[:, d:d + 1], in1=rstd[:, :],
                    op0=ALU.mult, op1=ALU.mult).then_inc(out_ready.sem, 1)


def _units(w, cols):
    L, K, _ = w.shape
    w = w[:, :, cols].reshape(L, K // P, P, len(cols) // P, P)
    return np.ascontiguousarray(w.transpose(0, 3, 2, 1, 4)).reshape(-1, P, K // P * P)


def _cols(v):
    v = v.reshape(v.shape[:-1] + (v.shape[-1] // P, P))
    return np.ascontiguousarray(np.moveaxis(v, -1, 0))


def _layout(i):
    f32 = np.float32
    L = DEPTH
    i = {k: np.asarray(v) for k, v in i.items()}
    o = {}
    o["x"] = _cols(i["x"].reshape(SEQ, D_MODEL)).transpose(0, 2, 1)
    o["c"] = _cols(i["c"].reshape(D_MODEL))
    o["ada_w"] = _units(i["ada_w"], np.arange(9 * D_MODEL))
    o["ada_b"] = _cols(i["ada_b"].reshape(6, 3 * D_MODEL))
    o["norm_g"] = _cols(np.stack([i["ffn1_norm_g"], i["mix_norm_g"], i["ffn2_norm_g"]], 1).reshape(6, D_MODEL))
    o["final_g"] = _cols(i["final_norm_g"])
    F = D_FF // P
    pairs = np.stack([np.arange(D_FF).reshape(F, P), D_FF + np.arange(D_FF).reshape(F, P)], 1).reshape(-1)
    for n in ("ffn1", "ffn2"):
        o[n + "_in"] = _units(i[n + "_w_in"], pairs)
        cut = F_HALF[0] * P
        o[n + "_out0"] = _units(i[n + "_w_out"][:, :cut], np.arange(D_MODEL))
        o[n + "_out1"] = _units(i[n + "_w_out"][:, cut:], np.arange(D_MODEL))
    AQ, AK, AV, BQ, BZ, BA, BB, CQ, CK, CV, G = np.cumsum([0, 256, 256, 256, 768, 256, 4, 4, 512, 128, 128])
    r = np.arange
    cq = np.concatenate([CQ + 64 * h + r(64) for j in range(4) for h in (j, j + 4)])
    cols = np.concatenate([BQ + r(768), BZ + r(256), G + r(3072), cq, CK + r(128), CV + r(128),
                           AQ + r(256), AK + r(256), AV + r(256)])
    o["mix_in"] = _units(i["mix_w_in"], cols)
    slot = np.array(HEAD_OF_SLOT)
    ab = i["mix_w_in"][:, :, np.concatenate([BA + slot, BB + slot])]
    o["w_ab"] = np.ascontiguousarray(ab.reshape(L, KD, P, 8).transpose(0, 2, 1, 3))
    up_c = i["w_up_c"][:, np.concatenate([64 * h + r(64) for j in range(4) for h in (j, j + 4)])]
    o["mix_up"] = _units(np.concatenate([i["w_up_a"], i["w_up_b"], up_c], 1), r(D_MODEL))
    o["mix_out"] = _units(i["mix_w_out"], r(D_MODEL))
    p, j = r(P)[:, None], r(2 * P)[None, :]
    rel = np.clip(P + p - j, -(CHUNK - 1), 128) + CHUNK - 1
    o["a_bias"] = np.ascontiguousarray(i["a_rel_bias"][:, :, rel].transpose(0, 2, 1, 3))
    o["a_far"] = np.ascontiguousarray(np.broadcast_to(i["a_rel_bias"][:, None, :, -1], (L, P, 4)))
    o["conv_w"] = np.ascontiguousarray(i["b_conv_w"].reshape(L, 4, 6, P).transpose(0, 3, 2, 1))
    small = np.zeros((L, P, 32), f32)
    small[:, :, 0:4] = i["b_dt_bias"][:, None, slot]
    small[:, :, 4:8] = i["b_a_log"][:, None, slot]
    small[:, 0:64, 8] = i["b_norm_g"]
    small[:, 64:128, 8] = i["b_norm_g"]
    small[:, :, 16:24] = i["c_sinks"][:, None, :]
    o["small"] = small
    q, c = r(P)[:, None], r(P)[None, :]
    same = q // CHUNK == c // CHUNK
    o["ident"] = np.eye(P, dtype=f32)
    o["ones_mean"] = np.full((P, P), 1.0 / D_MODEL, f32)
    o["eps"] = np.stack([np.full(P, EPS, f32), np.ones(P, f32)], 1)
    o["tri"] = (same & (q <= c)).astype(f32)
    o["same_chunk"] = same.astype(f32)
    o["strict"] = (q < c).astype(f32)
    o["level_mask"] = np.stack([(c // 2 ** v == q // 2 ** v + 1) & (q // 2 ** v % 2 == 0) for v in range(LEVELS)], 1).astype(f32)
    rot = np.zeros((P, P), f32)
    for h in range(2):
        for d in range(32):
            rot[64 * h + 32 + d, 64 * h + d] = -1.0
            rot[64 * h + d, 64 * h + 32 + d] = 1.0
    o["rot"] = rot
    inv = np.float32(10000.0) ** (-np.arange(32, dtype=f32) / np.float32(32))
    ang = np.arange(SEQ, dtype=f32)[None, :] * inv[:, None].astype(f32)
    o["cos"] = np.tile(np.cos(ang).astype(f32), (4, 1))
    o["sin"] = np.tile(np.sin(ang).astype(f32), (4, 1))
    kc, qc = j // CHUNK - 2, p // CHUNK
    o["c_mask"] = np.where((kc == qc) | (kc == qc - 1), 0.0, NEG).astype(f32)
    o["a_mask"] = np.where(kc <= qc, 0.0, NEG).astype(f32)
    return {k: np.ascontiguousarray(v) for k, v in o.items()}


def kernel(**inputs):
    import concourse.bacc as _bacc
    from concourse.bass_utils import run_bass_kernel_spmd as _run

    nc = _bacc.Bacc("TRN2", target_bir_lowering=False, num_devices=1)
    arrays, aps = {}, {}
    for name, v in _layout(inputs).items():
        arrays[f"in_{name}_dram"] = v
        aps[name] = nc.dram_tensor(f"in_{name}_dram", v.shape, mybir.dt.from_np(v.dtype), kind="ExternalInput").ap()
    out = nc.dram_tensor("out_dram", (P, KD, SEQ), F32, kind="ExternalOutput").ap()
    encoder_kernel(nc, aps, out)
    r = _run(nc, [arrays], core_ids=[0])
    got = r.results[0]["out_dram"]
    return np.ascontiguousarray(got.transpose(2, 1, 0)).reshape(1, SEQ, D_MODEL)
```

```python
from contextlib import ExitStack

import numpy as np

import concourse.bass as bass
from concourse import mybir

F32 = mybir.dt.float32
F32R = mybir.dt.float32r
ALU = mybir.AluOpType
ACT = mybir.ActivationFunctionType
AX = mybir.AxisListType

P = 128
D_MODEL, SEQ, DEPTH = 1024, 512, 2
CHUNK, HEAD = 64, 64
D_FF = 2816
EPS = 1e-6
KD = D_MODEL // P
TT = SEQ // P
NCH = SEQ // CHUNK
F_HALF = (12, 10)
KMAX = max(F_HALF)
RAW = 4
UNITS = 180
SUB = 60
MIX = SUB
M_C, M_A, M_IN = 8, 34, 44
U_UP, U_OUT = MIX + M_IN, MIX + M_IN + 8
NEG = -1e30
assert 2 * (sum(F_HALF) * P) == 2 * D_FF and U_OUT + 8 == 2 * SUB

HEAD_OF_SLOT = (0, 2, 1, 3)
LEVELS = 6


def gate_unit(g):
    return 14 + g if g < 20 else M_A + 6 + g - 20


class Signal:

    def __init__(self, sem, per_layer, credit=0):
        self.sem, self.per_layer, self.credit = sem, per_layer, credit

    def at(self, layer, n):
        return layer * self.per_layer + (n + self.credit)


def encoder_kernel(nc, a, out):
    ctx = ExitStack()
    with ctx:
        base = [16512]

        def place(name, shape, dt, at=None):
            size = 4 * int(np.prod(shape[1:]))
            size = (size + 31) // 32 * 32
            off = base[0] if at is None else at
            if at is None:
                base[0] += size
            return nc.alloc_sbuf_tensor_at(name, shape, dt, offset=off)

        x = place("x", [P, KD, SEQ], F32)
        uh = place("uh", [P, KD, SEQ], F32R)
        ul = place("ul", [P, KD, SEQ], F32R)
        RAW0 = base[0]
        raw = place("raw", [P, RAW, KMAX * P], F32)
        WH0 = base[0]
        wh = place("wh", [P, 2, KMAX * P], F32R)
        wl = place("wl", [P, 2, KMAX * P], F32R)
        ada_raw = place("ada_raw", [P, 2, KD * P], F32)
        ada_acc = place("ada_acc", [P, 24, P], F32)
        cond = place("cond", [P, KD], F32)
        ada_b = place("ada_b", [P, 6, 24], F32)
        norm_g = place("norm_g", [P, 6, KD], F32)
        final_g = place("final_g", [P, KD], F32)
        mod = place("mod", [P, 24], F32)
        scale_eff = place("scale_eff", [P, KD], F32)
        gate_eff = place("gate_eff", [P, KD], F32)
        ident = place("ident", [P, P], F32)
        ones_mean = place("ones_mean", [P, P], F32)
        eps = place("eps", [P, 2], F32)
        tri = place("tri", [P, P], F32)
        same_chunk = place("same_chunk", [P, P], F32)
        strict = place("strict", [P, P], F32)
        level_mask = place("level_mask", [P, LEVELS, P], F32)
        rot = place("rot", [P, P], F32)
        cos = place("cos", [P, SEQ], F32)
        sin = place("sin", [P, SEQ], F32)
        c_mask = place("c_mask", [P, 2 * P], F32)
        a_mask = place("a_mask", [P, 2 * P], F32)
        a_bias = place("a_bias", [P, 4, 2 * P], F32)
        a_far = place("a_far", [P, 4], F32)
        conv_w = place("conv_w", [P, 6, 4], F32)
        small = place("small", [P, 32], F32)
        ab_raw = place("ab_raw", [P, KD, 8], F32)
        ab_hi = place("ab_hi", [P, KD, 8], F32R)
        ab_lo = place("ab_lo", [P, KD, 8], F32R)
        sc = place("sc", [P, 256], F32)
        mx = place("mx", [P, 64], F32)
        egl = place("egl", [P, TT, 2, 2], F32)
        rstd = place("rstd", [P, SEQ], F32)
        ssq = place("ssq", [P, SEQ], F32)
        sq = place("sq", [P, 2, SEQ], F32)
        A0 = base[0]
        h32 = place("h32", [P, 2, SEQ], F32, A0 + 57344)
        silu_s = place("silu_s", [P, 2, SEQ], F32, A0 + 61440)
        hh = place("hh", [P, KMAX, SEQ], F32R, A0)
        hl = place("hl", [P, KMAX, SEQ], F32R, A0 + KMAX * 2048)
        t_buf = place("t_buf", [P, 2, SEQ], F32, A0 + 49152)
        u32 = place("u32", [P, 2, SEQ], F32, A0 + 49152 + 4096)
        ada0 = place("ada0", [P, 16, KD * P], F32, A0)
        oh = place("oh", [P, KD, SEQ], F32R, A0)
        ol = place("ol", [P, KD, SEQ], F32R, A0 + 16384)
        W0 = A0 + 32768
        bp = place("bp", [P, 8, SEQ], F32, W0)
        intra = place("intra", [P, TT, 4, P], F32, W0 + 16384)
        u_val = place("u_val", [P, TT, 4, HEAD], F32, W0 + 24576)
        wT = place("wT", [P, 2, SEQ], F32, A0)
        k_dec = place("k_dec", [P, TT, 4, HEAD], F32, A0 + 8192)
        st = place("st", [P, NCH + 1, 2, HEAD], F32, A0 + 12288)
        v_beta = place("v_beta", [P, 4, HEAD], F32, A0 + 17408)
        k_beta = place("k_beta", [P, 4, HEAD], F32, A0 + 18432)
        Tm = place("Tm", [P, 4, P], F32, A0 + 26624)
        Um = place("Um", [P, 4, P], F32, A0 + 28672)
        Ym = place("Ym", [P, 4, P], F32, A0 + 30720)
        cT = place("cT", [P, 4, P], F32, A0 + 20480)
        eg = place("eg", [P, 2, P], F32, A0 + 22528)
        pc = place("pc", [P, 6, SEQ], F32, W0)
        tails = [RAW0 + j * KMAX * 512 + 4096 for j in range(4)] + [WH0 + j * KMAX * 512 + 4096 for j in range(4)]
        ct = [place(f"ct{j}", [P, SEQ], F32, tails[j]) for j in range(6)]
        g_in = [[place(f"g_in{q}{b}", [P, SEQ], F32, tails[3 * q + b]) for b in range(3)] for q in range(2)]
        lT = [place("lT0", [P, 4, P], F32, A0 + 24576), place("lT1", [P, 4, P], F32, tails[6])]
        dcy = place("dcy", [P, 4, P], F32, tails[7])
        v_tok = place("v_tok", [P, TT, 2 * P], F32, W0 + 12288)
        sco = place("sco", [P, 8, 2 * P], F32, W0 + 16384)
        pT = place("pT", [P, TT, SEQ], F32, W0 + 24576)
        up_m = place("up_m", [P, 4, SEQ], F32, W0 + 12288)
        assert A0 + 65536 <= 229368, A0 + 65536

        PS = ctx.enter_context(nc.psum_tensor("PS", [P, 8, SEQ], F32))
        gates_dram = nc.dram_tensor("gates_dram", (24, P, SEQ), F32, kind="Internal").ap()

        def sig(name, per_layer=0, credit=0):
            return Signal(ctx.enter_context(nc.semaphore(name)), per_layer, credit)

        arrived = [sig(f"arrived{j}", 16 * UNITS // RAW) for j in range(RAW)]
        hi_ready = sig("hi_ready", UNITS, RAW)
        lo_ready = sig("lo_ready", UNITS, RAW)
        unit_done = sig("unit_done", UNITS, 2)
        consts_in = sig("consts_in")
        cond_in = sig("cond_in")
        cond_done = sig("cond_done")
        layer_in = sig("layer_in", 16 * 5)
        x_in = sig("x_in")
        ada0_in = [sig(f"ada0_in{j}") for j in range(6)]
        ada_in = [sig(f"ada_in{j}") for j in range(2)]
        ada_step = sig("ada_step")
        ada_ready = sig("ada_ready")
        ada_gate_ready = sig("ada_gate_ready")
        mods_mm = sig("mods_mm", 3)
        gate_mods_mm = sig("gate_mods_mm", 3)
        gate_mod_step = sig("gate_mod_step", 3)
        gate_mods_done = sig("gate_mods_done", 3)
        mods_done = sig("mods_done", 3)
        mod_step = sig("mod_step", 3)
        ada0_step = sig("ada0_step")
        bias_masked = sig("bias_masked", 1)
        norm_mm = sig("norm_mm", 3)
        root_done = sig("root_done", 3)
        rstd_done = sig("rstd_done", 3)
        t_done = sig("t_done", 24)
        u32_done = sig("u32_done", 24)
        uh_done = sig("uh_done", 24)
        ul_done = sig("ul_done", 24)
        silu_done = sig("silu_done", 44, 2)
        h_done = sig("h_done", 44, 2)
        hh_done = sig("hh_done", 44)
        hl_done = sig("hl_done", 44)
        x_done = sig("x_done", 40, 2)
        sq_done = sig("sq_done", 24)
        ssq_done = sig("ssq_done", 21)
        in_done = sig("in_done", 44, 4)
        ab_hi_done = sig("ab_hi_done", 1)
        ab_lo_done = sig("ab_lo_done", 1)
        ab_mm = sig("ab_mm", 1)
        gate_out = [sig(f"gate_out{j}", 16 * 12) for j in range(2)]
        gate_back = [sig(f"gate_back{j}", 16 * 3 * 4) for j in range(2)]
        conv_done = sig("conv_done", 6)
        conv_silu = sig("conv_silu", 6)
        conv_step = sig("conv_step", 18)
        l2_sq = sig("l2_sq", 4)
        l2_mm = sig("l2_mm", 4)
        l2_root = sig("l2_root", 4)
        l2_inv = sig("l2_inv", 4)
        qk_done = sig("qk_done", 4)
        ab_v = sig("ab_v", 7)
        ab_a = sig("ab_a", 7)
        gc_mm = sig("gc_mm", 1)
        gcb_mm = sig("gcb_mm", 4)
        bb_mm = sig("bb_mm", 4)
        kk_mm = sig("kk_mm", 4)
        tr_mm = sig("tr_mm", 4)
        diff_done = sig("diff_done", 4)
        decay_done = sig("decay_done", 4)
        eg_done = sig("eg_done", 4)
        mask_step = sig("mask_step", 16)
        lt_done = sig("lt_done", 4)
        tok_done = sig("tok_done", 4)
        qe_done = sig("qe_done", 4)
        ct_done = sig("ct_done", 24)
        u_done = sig("u_done", 24)
        tm_done = sig("tm_done", 20)
        y_mm = sig("y_mm", 24)
        y_done = sig("y_done", 20)
        z_mm = sig("z_mm", 20)
        uw_mm = sig("uw_mm", 4)
        uw_done = sig("uw_done", 4)
        settled = sig("settled")
        st_zero = sig("st_zero", 1)
        ws_mm = sig("ws_mm", 8)
        vnew_done = sig("vnew_done", 8)
        kv_mm = sig("kv_mm", 8)
        st_done = sig("st_done", 8)
        o_mm = sig("o_mm", 1)
        o_done = sig("o_done", 1)
        on_sq = sig("on_sq", 2)
        on_mm = sig("on_mm", 2)
        on_root = sig("on_root", 2)
        on_silu = sig("on_silu", 2)
        on_step = sig("on_step", 6)
        ob_hi = sig("ob_hi", 2)
        ob_lo = sig("ob_lo", 2)
        rot_mm = sig("rot_mm", 5)
        rot_step = sig("rot_step", 10)
        rope_done = sig("rope_done", 5)
        vt_mm = sig("vt_mm", 2)
        vt_done = sig("vt_done", 2)
        s_mm = sig("s_mm", 8)
        s_step = sig("s_step", 28)
        bias_done = sig("bias_done", 8)
        negmax_done = sig("negmax_done", 8)
        exp_done = sig("exp_done", 8)
        prob_done = sig("prob_done", 8)
        pt_mm = sig("pt_mm", 17)
        pt_done = sig("pt_done", 17)
        pv_mm = sig("pv_mm", 8)
        o_hi = sig("o_hi", 8)
        o_lo = sig("o_lo", 8)
        sig_done = sig("sig_done", 8)
        merge_step = sig("merge_step", 16)
        mg_used = sig("mg_used", 8, 2)
        mh_done = sig("mh_done", 8)
        ml_done = sig("ml_done", 8)
        out_ready = sig("out_ready")
        out_done = [sig(f"out_done{j}") for j in range(2)]

        block = ctx.enter_context(nc.Block())

        def out_index(l, sub, half, d):
            return (0, 16, 24)[sub] + (8 * half if sub != 1 else 0) + d

        def ada_lot(e, r, lot, step, done, arrived_lot):
            ready = ada_ready if lot < 4 else ada_gate_ready
            e.wait_ge(arrived_lot.sem, 16)
            r4 = r.rearrange("p u (k n) -> p u k n", k=KD)
            for u in range(4):
                last = e.tensor_tensor(r4[:, u], r4[:, u], cond[:, :].unsqueeze(2).broadcast_to([P, KD, P]), ALU.mult)
            last.then_inc(step.sem, 1)
            e.wait_ge(step.sem, done + 1)
            e.tensor_tensor(r[:, :, 0:512], r[:, :, 0:512], r[:, :, 512:1024], ALU.add).then_inc(step.sem, 1)
            e.wait_ge(step.sem, done + 2)
            e.tensor_tensor(r[:, :, 0:256], r[:, :, 0:256], r[:, :, 256:512], ALU.add).then_inc(step.sem, 1)
            e.wait_ge(step.sem, done + 3)
            e.tensor_tensor(ada_acc[:, 4 * lot:4 * lot + 4, :], r[:, :, 0:128], r[:, :, 128:256], ALU.add)\
                .then_inc(ready.sem, 4)

        @block.sync
        def _(e):
            e.dma_start(cond[:, :], a["c"]).then_inc(cond_in.sem, 16)
            for t, src in ((ident, "ident"), (ones_mean, "ones_mean"), (eps, "eps"), (tri, "tri"),
                           (same_chunk, "same_chunk"), (strict, "strict"), (rot, "rot"), (cos, "cos"),
                           (sin, "sin"), (c_mask, "c_mask"), (a_mask, "a_mask"),
                           (final_g, "final_g")):
                e.dma_start(t[:, :], a[src]).then_inc(consts_in.sem, 16)
            for t, src in ((level_mask, "level_mask"), (ada_b, "ada_b"), (norm_g, "norm_g")):
                e.dma_start(t[:, :, :], a[src]).then_inc(consts_in.sem, 16)
            e.dma_start(x[:, :, :], a["x"]).then_inc(x_in.sem, 16)

            def load(l, m, j, src, K):
                n = l * UNITS + (4 * m + j + 1)
                e.wait_ge(hi_ready.sem, n)
                e.wait_ge(lo_ready.sem, n)
                e.dma_start(raw[:, j, 0:K * P], src).then_inc(arrived[j].sem, 16)

            with e.Fori(0, DEPTH) as l:
                def ffn(first, name):
                    m0 = first // RAW
                    for half, F in enumerate(F_HALF):
                        with e.Fori(0, F // 2) as i:
                            for j in range(4):
                                load(l, m0 + i, j, a[name + "_in"][l * 44 + F_HALF[0] * 2 * half + 4 * i + j], KD)
                        m0 += F // 2
                        with e.Fori(0, 2) as i:
                            for j in range(4):
                                load(l, m0 + i, j, a[f"{name}_out{half}"][l * 8 + 4 * i + j], F)
                        m0 += 2

                ffn(0, "ffn1")
                e.wait_ge(x_done.sem, x_done.at(l, 0))
                e.dma_start(ab_raw[:, :, :], a["w_ab"][l]).then_inc(layer_in.sem, 16)
                e.dma_start(a_bias[:, :, :], a["a_bias"][l]).then_inc(layer_in.sem, 16)
                e.dma_start(a_far[:, :], a["a_far"][l]).then_inc(layer_in.sem, 16)
                e.dma_start(conv_w[:, :, :], a["conv_w"][l]).then_inc(layer_in.sem, 16)
                e.dma_start(small[:, :], a["small"][l]).then_inc(layer_in.sem, 16)
                with e.Fori(0, 11) as i:
                    for j in range(4):
                        load(l, MIX // RAW + i, j, a["mix_in"][l * 44 + 4 * i + j], KD)
                with e.Fori(0, 2) as i:
                    for j in range(4):
                        load(l, U_UP // RAW + i, j, a["mix_up"][l * 8 + 4 * i + j], KD)
                with e.Fori(0, 2) as i:
                    for j in range(4):
                        load(l, U_OUT // RAW + i, j, a["mix_out"][l * 8 + 4 * i + j], KD)
                ffn(2 * SUB, "ffn2")
            for d in range(KD):
                e.wait_ge(out_ready.sem, d + 1)
                e.dma_start(out[:, d, :], sq[:, d % 2, :]).then_inc(out_done[d % 2].sem, 16)
            for j in range(2):
                e.wait_ge(out_done[j].sem, 16 * KD // 2)

        @block.gpsimd
        def _(e):
            for lot in (3, 0, 1, 2):
                e.dma_start(ada0[:, 4 * lot:4 * lot + 4, :], a["ada_w"][4 * lot:4 * lot + 4]
                            .rearrange("u p n -> p u n")).then_inc(ada0_in[lot].sem, 16)

            def load_unit(n, u, j):
                if not isinstance(n, int) or n >= 2:
                    e.wait_ge(ada_step.sem, n * 4 - 1)
                e.dma_start(ada_raw[:, j, :], a["ada_w"][u]).then_inc(ada_in[j].sem, 16)

            def sum_unit(n, n_in, v, j, ready, count):
                r = ada_raw[:, j, :]
                r3 = r.rearrange("p (k n) -> p k n", k=KD)
                e.wait_ge(ada_in[j].sem, n_in)
                e.tensor_tensor(r3, r3, cond[:, :].unsqueeze(2).broadcast_to([P, KD, P]), ALU.mult)\
                    .then_inc(ada_step.sem, 1)
                e.wait_ge(ada_step.sem, n * 4 + 4)
                e.tensor_tensor(r[:, 0:512], r[:, 0:512], r[:, 512:1024], ALU.add).then_inc(ada_step.sem, 1)
                e.wait_ge(ada_step.sem, n * 4 + 5)
                e.tensor_tensor(r[:, 0:256], r[:, 0:256], r[:, 256:512], ALU.add).then_inc(ada_step.sem, 1)
                e.wait_ge(ada_step.sem, n * 4 + 6)
                e.tensor_tensor(ada_acc[:, bass.ds(v, 1), :].rearrange("p a n -> p (a n)"),
                                r[:, 0:128], r[:, 128:256], ALU.add).then_inc(ready.sem, 1)
                e.wait_ge(ready.sem, count)
                e.sem_inc(ada_step.sem, 1)

            load_unit(0, 16, 0)
            load_unit(1, 17, 1)
            e.wait_ge(cond_done.sem, 1)
            ada_lot(e, ada0[:, 12:16, :], 3, ada_step, 0, ada0_in[3])
            for n in range(8):
                sum_unit(n, 16 * (n // 2 + 1), 16 + n, n % 2, ada_gate_ready, n + 1)
                if n + 2 < 8:
                    load_unit(n + 2, 18 + n, n % 2)

            with e.Fori(0, 3 * DEPTH - 1) as g:
                for first, last, ready, used, per in ((0, 8, ada_ready, mods_mm, 16),
                                                      (8, 12, ada_gate_ready, gate_mods_mm, 8)):
                    with e.Fori(first, last) as i:
                        for j in range(2):
                            e.wait_ge(unit_done.sem, g * SUB + 4 * i + (2 * j + 3))
                            load_unit(g * 24 + 2 * i + (8 + j), g * 24 + 2 * i + (24 + j), j)
                        e.wait_ge(used.sem, g + 1)
                        for j in range(2):
                            sum_unit(g * 24 + 2 * i + (8 + j), g * 192 + 16 * i + 80, 2 * i + j, j, ready,
                                     g * per + 2 * i + (per - 2 * first + j + 1))

        @block.tensor
        def _(e):
            e.wait_ge(consts_in.sem, 16 * 15)

            def unit(l, n, j, K, bank, xh, xl, waits=None, ks=None):
                ks = range(K) if ks is None else ks
                if ks[0] == 0:
                    e.wait_ge(lo_ready.sem, n + (1 + RAW))
                for k in ks:
                    if waits is not None:
                        waits(k)
                    for w, v in ((wh, xh), (wh, xl), (wl, xh)):
                        mm = e.matmul(PS[:, bank, :], w[:, j % 2, k * P:(k + 1) * P], v[:, k, :],
                                      start=(k == 0 and w is wh and v is xh), stop=(k == K - 1 and w is wl))
                if ks[-1] == K - 1:
                    mm.then_inc(unit_done.sem, 1)

            def first_pair(l, n, banks, there):
                e.wait_ge(lo_ready.sem, n + (2 + RAW))
                for k in range(KD):
                    there(k)
                    for j in range(2):
                        for w, v in ((wh, uh), (wh, ul), (wl, uh)):
                            mm = e.matmul(PS[:, banks[j], :], w[:, j, k * P:(k + 1) * P], v[:, k, :],
                                          start=(k == 0 and w is wh and v is uh), stop=(k == KD - 1 and w is wl))
                        if k == KD - 1:
                            mm.then_inc(unit_done.sem, 1)

            def settle():
                e.sem_inc(settled.sem, 1)

            def norm_and_mods(l, s):
                e.wait_ge(ssq_done.sem, ssq_done.at(l, 7 * (s + 1)))
                e.matmul(PS[:, 6, :], ones_mean[:, :], ssq[:, :], start=True, stop=True).then_inc(norm_mm.sem, 1)

            def mods(l, s):
                e.wait_ge(ada_ready.sem, l * 48 + 16 * (s + 1))
                for v in range(16):
                    mm = e.matmul(PS[:, 7, v:v + 1], ada_acc[:, v, :], eps[:, 1:2], start=True, stop=True)
                mm.then_inc(mods_mm.sem, 1)

            def gate_mods(l, s):
                e.wait_ge(ada_gate_ready.sem, l * 24 + 8 * (s + 1))
                for v in range(16, 24):
                    mm = e.matmul(PS[:, 7, v:v + 1], ada_acc[:, v, :], eps[:, 1:2], start=True, stop=True)
                mm.then_inc(gate_mods_mm.sem, 1)

            def ffn(l, s, first):
                base_f = 22 * (s // 2)
                n0 = first
                for half, F in enumerate(F_HALF):
                    def in_unit(i, j):
                        n = l * UNITS + 4 * i + (n0 + j)
                        f = l * 44 + 2 * i + (base_f + F_HALF[0] * half + j // 2)
                        e.wait_ge((h_done if j % 2 else silu_done).sem, f + 1)
                        unit(l, n, j, KD, (0, 2, 1, 3)[j], uh, ul)

                    if half == 0:
                        e.wait_ge(h_done.sem, h_done.at(l, base_f - 1))
                        first_pair(l, l * UNITS + n0, (0, 2),
                                   lambda k: e.wait_ge(ul_done.sem, ul_done.at(l, 8 * s + k + 1)))
                        in_unit(0, 2)
                        in_unit(0, 3)
                    with e.Fori(1 - half, F // 2) as i:
                        for j in range(4):
                            in_unit(i, j)
                    if half == 0:
                        gate_mods(l, s)
                    n0 += 2 * F
                    fs = base_f + (F_HALF[0] if half == 0 else 22)
                    with e.Fori(0, 2) as i:
                        for j in range(4):
                            n = l * UNITS + 4 * i + (n0 + j)
                            e.wait_ge(x_done.sem, l * 40 + 4 * i + (out_index(l, s, half, j) + 1))

                            def h_there(k):
                                if k >= F - 2:
                                    e.wait_ge(hl_done.sem, hl_done.at(l, fs - (F - 1 - k)))
                            unit(l, n, j, F, 4 + j % 2, hh, hl, h_there if j == 0 else None)
                    n0 += 8

            def mixing(l):
                def proj(m):
                    e.wait_ge(in_done.sem, l * 44 + (m + 1))
                    unit(l, l * UNITS + (MIX + m), m, KD, m % 4, uh, ul)

                at_quarter = [0]

                def gates(quarters):
                    for _ in range(quarters):
                        g, part = divmod(at_quarter[0], 4)
                        at_quarter[0] += 1
                        m = gate_unit(g)
                        if part == 0:
                            e.wait_ge(in_done.sem, in_done.at(l, m if g >= 16 else max(m - 1, 14)))
                        unit(l, l * UNITS + (MIX + m), m, KD, g % 2 if g < 16 else 7, uh, ul,
                             ks=range(2 * part, 2 * part + 2))

                e.wait_ge(in_done.sem, l * 44 + 2)
                first_pair(l, l * UNITS + MIX, (0, 1), lambda k: e.wait_ge(ul_done.sem, ul_done.at(l, 8 + k + 1)))
                for m in range(2, 9):
                    proj(m)
                e.wait_ge(ab_lo_done.sem, ab_lo_done.at(l, 1))
                for t in range(TT):
                    for k in range(KD):
                        for v, w in ((uh, ab_hi), (ul, ab_hi), (uh, ab_lo)):
                            mm = e.matmul(PS[:, 6, 8 * t:8 * t + 8], v[:, k, t * P:(t + 1) * P], w[:, k, :],
                                          start=(k == 0 and v is uh and w is ab_hi), stop=(k == KD - 1 and w is ab_lo))
                mm.then_inc(ab_mm.sem, 1)
                for i in range(4):
                    proj(9 + i)
                    e.wait_ge(l2_sq.sem, l2_sq.at(l, i + 1))
                    if i >= 2:
                        e.wait_ge(l2_root.sem, l2_root.at(l, i - 1))
                    e.matmul(PS[:, 4 + i % 2, :], same_chunk[:, :], sq[:, i % 2, :], start=True, stop=True)\
                        .then_inc(l2_mm.sem, 1)
                proj(13)
                gate_mods(l, 1)
                e.wait_ge(ab_v.sem, ab_v.at(l, 4))
                e.matmul(PS[:, 6, 32:48], tri[:, :], sc[:, 0:16], start=True, stop=True)
                e.matmul(PS[:, 6, 48:64], same_chunk[:, :], sc[:, 0:16], start=True, stop=True).then_inc(gc_mm.sem, 1)
                e.wait_ge(qk_done.sem, qk_done.at(l, 4))
                e.wait_ge(conv_silu.sem, conv_silu.at(l, 6))
                e.wait_ge(in_done.sem, in_done.at(l, 14))
                e.wait_ge(ab_a.sem, ab_a.at(l, 5))
                e.wait_ge(ab_v.sem, ab_v.at(l, 5))

                def run_decay(t):
                    if t:
                        e.wait_ge(tok_done.sem, tok_done.at(l, t))
                    for s in range(4):
                        mm = e.matmul(PS[:, 4 if t else 5, s * P:(s + 1) * P],
                                      sc[:, 4 * t + s:4 * t + s + 1].broadcast_to([P, P]), tri[:, :], start=True, stop=True)
                    mm.then_inc(gcb_mm.sem, 1)

                def beta_and_products(t):
                    if t:
                        e.wait_ge(diff_done.sem, diff_done.at(l, t + 1))
                        e.wait_ge(eg_done.sem, eg_done.at(l, t + 1))
                        e.wait_ge(rope_done.sem, rope_done.at(l, t))
                    for s in range(4):
                        mm = e.matmul(PS[:, 4 if t else 6, s * P:(s + 1) * P],
                                      sc[:, 16 + 4 * t + s:17 + 4 * t + s].broadcast_to([P, P]), ident[:, :],
                                      start=True, stop=True)
                    mm.then_inc(bb_mm.sem, 1)
                    c0, c1 = t * P, (t + 1) * P
                    for par in range(2):
                        r = slice(64 * par, 64 * par + 64)
                        for x2 in range(2):
                            for pair in range(2):
                                rhs = bp[r, (2 if x2 == 0 else 0) + pair, c0:c1]
                                mm = e.matmul(PS[:, 2 + par, (2 * x2 + pair) * P:(2 * x2 + pair + 1) * P],
                                              bp[r, 2 + pair, c0:c1], rhs, start=True, stop=True)
                    mm.then_inc(kk_mm.sem, 1)

                def by_token(t):
                    if t:
                        e.wait_ge(lt_done.sem, lt_done.at(l, t + 1))
                    for y in range(4):
                        mm = e.transpose(PS[:, 4, y * P:(y + 1) * P], bp[:, 2 + y, t * P:(t + 1) * P], ident[:, :])
                    mm.then_inc(tr_mm.sem, 1)

                def rotate(i):
                    e.matmul(PS[:, 2 + i // 4, :], rot[:, :], ct[i][:, :], start=True, stop=True).then_inc(rot_mm.sem, 1)

                run_decay(0)
                beta_and_products(0)
                by_token(0)
                for t in range(TT):
                    for lv in range(LEVELS):
                        g = 6 * t + lv
                        e.wait_ge(ct_done.sem, ct_done.at(l, g + 1))
                        if lv == 0:
                            if t:
                                e.wait_ge(tm_done.sem, tm_done.at(l, 5 * t))
                            for s in range(4):
                                mm = e.transpose(PS[:, 7, s * P:(s + 1) * P], cT[:, s, :], ident[:, :])
                            mm.then_inc(y_mm.sem, 1)
                        else:
                            if lv == 1:
                                if t:
                                    e.wait_ge(uw_done.sem, uw_done.at(l, t))
                                else:
                                    e.wait_ge(eg_done.sem, eg_done.at(l, 1))
                            e.wait_ge(tm_done.sem, tm_done.at(l, 5 * t + lv))
                            for s in range(4):
                                mm = e.matmul(PS[:, 5, s * P:(s + 1) * P], cT[:, s, :], Tm[:, s, :], start=True, stop=True)
                            mm.then_inc(y_mm.sem, 1)
                        if lv == 1:
                            rotate(t)
                            if t + 1 < TT:
                                run_decay(t + 1)
                        gates(1)
                        if lv > 0:
                            e.wait_ge(y_done.sem, y_done.at(l, 5 * t + lv))
                            e.wait_ge(u_done.sem, u_done.at(l, g))
                            for s in range(4):
                                mm = e.matmul(PS[:, 6, s * P:(s + 1) * P], Ym[:, s, :], Um[:, s, :], start=True, stop=True)
                            if lv < LEVELS - 1:
                                for s in range(4):
                                    mm = e.matmul(PS[:, 7, s * P:(s + 1) * P], Um[:, s, :], Ym[:, s, :], start=True, stop=True)
                            mm.then_inc(z_mm.sem, 1)
                        if lv == 3 and t + 1 < TT:
                            beta_and_products(t + 1)
                        if lv == 3 and t + 1 == TT:
                            rotate(4)
                        if lv == 5 and t + 1 < TT:
                            by_token(t + 1)
                        gates(1)
                    e.wait_ge(u_done.sem, u_done.at(l, 6 * (t + 1)))
                    e.wait_ge(tok_done.sem, tok_done.at(l, t + 1))
                    for s in range(4):
                        e.matmul(PS[:, 5, s * HEAD:(s + 1) * HEAD], Um[:, s, :], v_beta[:, s, :], start=True, stop=True)
                    for s in range(4):
                        par, pair = s // 2, s % 2
                        mm = e.matmul(PS[64 * par:64 * par + 64, 5, 256 + pair * P:256 + (pair + 1) * P],
                                      k_beta[:, s, :], Um[:, s, :], start=True, stop=True)
                    mm.then_inc(uw_mm.sem, 1)
                e.wait_ge(st_zero.sem, st_zero.at(l, 1))
                e.wait_ge(rope_done.sem, rope_done.at(l, 5))
                e.wait_ge(uw_done.sem, uw_done.at(l, TT))
                for n in range(NCH):
                    t, pb = n // 2, 64 * (n % 2)
                    if n >= 1:
                        e.wait_ge(st_done.sem, st_done.at(l, n))
                    settle()
                    for s in range(4):
                        par, pair = s // 2, s % 2
                        r = slice(64 * par, 64 * par + 64)
                        mm = e.matmul(PS[pb:pb + 64, 2 + par, pair * HEAD:(pair + 1) * HEAD],
                                      wT[r, pair, n * CHUNK:(n + 1) * CHUNK], st[r, n, pair, :], start=True, stop=True)
                    mm.then_inc(ws_mm.sem, 1)
                    gates(1)
                    e.wait_ge(vnew_done.sem, vnew_done.at(l, n + 1))
                    settle()
                    for s in range(4):
                        par, pair = s // 2, s % 2
                        mm = e.matmul(PS[64 * par:64 * par + 64, 4 + n % 2, pair * HEAD:(pair + 1) * HEAD],
                                      k_dec[pb:pb + 64, t, s, :], u_val[pb:pb + 64, t, s, :], start=True, stop=True)
                    mm.then_inc(kv_mm.sem, 1)
                    gates(1)
                e.wait_ge(qe_done.sem, qe_done.at(l, TT))
                for t in range(TT):
                    for s in range(4):
                        par, pair = s // 2, s % 2
                        r = slice(64 * par, 64 * par + 64)
                        e.matmul(PS[r, 6 + pair, t * P:(t + 1) * P], u_val[:, t, s, :], intra[:, t, s, :],
                                 start=True, stop=True)
                        for ch in range(2):
                            n = 2 * t + ch
                            mm = e.matmul(PS[r, 6 + pair, n * CHUNK:(n + 1) * CHUNK], st[r, n, pair, :],
                                          bp[r, pair, n * CHUNK:(n + 1) * CHUNK], start=False, stop=True,
                                          skip_group_check=True)
                mm.then_inc(o_mm.sem, 1)

                def scores_c(t):
                    lo = 0 if t else P
                    for h in range(8):
                        r = slice(64 * (h // 4), 64 * (h // 4) + 64)
                        k0 = (t - 1) * P + lo
                        mm = e.matmul(PS[:, h // 2, (h % 2) * 256 + lo:(h % 2) * 256 + 256],
                                      ct[h % 4][r, t * P:(t + 1) * P], ct[4][r, k0:(t + 1) * P], start=True, stop=True)
                    mm.then_inc(s_mm.sem, 1)

                e.wait_ge(in_done.sem, in_done.at(l, gate_unit(16)))
                scores_c(0)
                e.wait_ge(st_done.sem, st_done.at(l, NCH))
                for i in range(2):
                    e.wait_ge(on_sq.sem, on_sq.at(l, i + 1))
                    e.matmul(PS[:, 4 + i, :], same_chunk[:, :], sq[:, i, :], start=True, stop=True)\
                        .then_inc(on_mm.sem, 1)
                for t in range(TT):
                    mm = e.transpose(PS[:, 6, t * P:(t + 1) * P], ct[5][:, t * P:(t + 1) * P], ident[:, :])
                mm.then_inc(vt_mm.sem, 1)
                for t in range(TT):
                    gates(4)
                    if t + 1 < TT:
                        e.wait_ge(bias_done.sem, bias_done.at(l, t + 1))
                        scores_c(t + 1)
                    if t == 0:
                        e.wait_ge(on_root.sem, on_root.at(l, 2))
                    e.wait_ge(prob_done.sem, prob_done.at(l, t + 1))
                    n_pt = 2 * t - 1 if t else 0
                    kts = (0, 1) if t else (1,)
                    for z, kt in enumerate(kts):
                        if n_pt + z >= 1:
                            e.wait_ge(pt_done.sem, pt_done.at(l, n_pt + z))
                        for h in range(8):
                            mm = e.transpose(PS[:, 4 + h // 4, (h % 4) * P:(h % 4 + 1) * P],
                                             sco[:, h, kt * P:(kt + 1) * P], ident[:, :])
                        mm.then_inc(pt_mm.sem, 1)
                    e.wait_ge(vt_done.sem, vt_done.at(l, 1))
                    e.wait_ge(pt_done.sem, pt_done.at(l, n_pt + len(kts)))
                    if t >= 1:
                        e.wait_ge(o_lo.sem, o_lo.at(l, t))
                    for kv in range(2):
                        for z, kt in enumerate(kts):
                            mm = e.matmul(PS[64 * kv:64 * kv + 64, 6, :], v_tok[:, t - 1 + kt, 64 * kv:64 * kv + 64],
                                          pT[:, 2 * kt + kv, :], start=(z == 0), stop=(z == len(kts) - 1))
                    mm.then_inc(pv_mm.sem, 1)

                def scores_a(t):
                    for h in range(4):
                        r = slice(64 * (h % 2), 64 * (h % 2) + 64)
                        mm = e.matmul(PS[:, h, 0:(t + 1) * P], pc[r, h // 2, t * P:(t + 1) * P],
                                      pc[r, 2 + h // 2, 0:(t + 1) * P], start=True, stop=True)
                    mm.then_inc(s_mm.sem, 1)

                e.wait_ge(bias_done.sem, bias_done.at(l, TT))
                for m in range(M_A, M_A + 6):
                    proj(m)
                e.wait_ge(in_done.sem, in_done.at(l, M_A + 6))
                scores_a(0)
                e.wait_ge(o_lo.sem, o_lo.at(l, 4))
                for y in range(2):
                    for t in range(TT):
                        mm = e.transpose(PS[:, 6 + y, t * P:(t + 1) * P], pc[:, 4 + y, t * P:(t + 1) * P], ident[:, :])
                mm.then_inc(vt_mm.sem, 1)
                e.wait_ge(vt_done.sem, vt_done.at(l, 2))
                for t in range(TT):
                    gates(4)
                    if t + 1 < TT:
                        e.wait_ge(bias_done.sem, bias_done.at(l, 4 + t + 1))
                        scores_a(t + 1)
                    e.wait_ge(prob_done.sem, prob_done.at(l, 4 + t + 1))
                    n_pt = 7 + t * (t + 1) // 2
                    for kt in range(t + 1):
                        e.wait_ge(pt_done.sem, pt_done.at(l, n_pt + max(kt - 1, 0)))
                        for h in range(4):
                            sh = sco[:, 2 * h:2 * h + 2, :].rearrange("p a n -> p (a n)")
                            mm = e.transpose(PS[:, 4 + kt % 2, h * P:(h + 1) * P], sh[:, kt * P:(kt + 1) * P], ident[:, :])
                        mm.then_inc(pt_mm.sem, 1)
                    e.wait_ge(pt_done.sem, pt_done.at(l, n_pt + t + 1))
                    if t >= 1:
                        e.wait_ge(o_lo.sem, o_lo.at(l, 4 + t))
                    for h in range(4):
                        r = slice(64 * (h % 2), 64 * (h % 2) + 64)
                        for kt in range(t + 1):
                            mm = e.matmul(PS[r, 6, (h // 2) * P:(h // 2 + 1) * P], v_tok[:, kt, h * HEAD:(h + 1) * HEAD],
                                          pT[:, kt, h * P:(h + 1) * P], start=(kt == 0), stop=(kt == t))
                    mm.then_inc(pv_mm.sem, 1)
                assert at_quarter[0] == 4 * 24

                e.wait_ge(o_lo.sem, o_lo.at(l, 8))
                e.wait_ge(in_done.sem, in_done.at(l, M_IN))
                for d in range(KD):
                    n = l * UNITS + (U_UP + d)
                    e.wait_ge(mg_used.sem, l * 8 + (d + 1))
                    e.wait_ge(lo_ready.sem, n + (1 + RAW))
                    for b, ks in enumerate((range(0, 2), range(2, 4), range(4, 8))):
                        for k in ks:
                            for w, v in ((wh, oh), (wh, ol), (wl, oh)):
                                mm = e.matmul(PS[:, 3 * (d % 2) + b, :], w[:, d % 2, k * P:(k + 1) * P], v[:, k, :],
                                              start=(k == ks[0] and w is wh and v is oh),
                                              stop=(k == ks[-1] and w is wl))
                    mm.then_inc(unit_done.sem, 1)
                with e.Fori(0, 2) as i:
                    for j in range(4):
                        n = l * UNITS + 4 * i + (U_OUT + j)
                        e.wait_ge(x_done.sem, l * 40 + 4 * i + (out_index(l, 1, 0, j) + 1))

                        def m_there(k):
                            e.wait_ge(ml_done.sem, ml_done.at(l, k + 1))
                        unit(l, n, j, KD, 6 + j % 2, uh, ul, m_there if j == 0 else None)

            with e.Fori(0, DEPTH) as l:
                norm_and_mods(l, 0)
                mods(l, 0)
                ffn(l, 0, 0)
                norm_and_mods(l, 1)
                mods(l, 1)
                mixing(l)
                norm_and_mods(l, 2)
                mods(l, 2)
                ffn(l, 2, 2 * SUB)
            e.wait_ge(ssq_done.sem, 7 * (3 * DEPTH + 1))
            e.matmul(PS[:, 6, :], ones_mean[:, :], ssq[:, :], start=True, stop=True).then_inc(norm_mm.sem, 1)

        def steps(e, l, first, count, K, nxt, split, use):
            bodies, m0 = count // 4, first // 4

            def body(i, last):
                for j in range(4):
                    if j < 2:
                        split(l, m0, i, j + 2, K)
                    elif not last:
                        split(l, m0 + 1, i, j - 2, K)
                    elif nxt is not None:
                        split(l, m0 + 1, i, j - 2, nxt)
                    use(i, j)
            if bodies > 2:
                with e.Fori(0, bodies - 1) as i:
                    body(i, False)
            else:
                body(0, False)
            body(bodies - 1, True)

        @block.scalar
        def _(e):
            def split(l, m0, i, j, K):
                e.wait_ge(arrived[j].sem, l * (16 * UNITS // RAW) + 16 * i + 16 * (m0 + 1))
                e.wait_ge(unit_done.sem, l * UNITS + 4 * i + (4 * m0 + j + 1))
                e.activation(wh[:, j % 2, 0:K * P], raw[:, j, 0:K * P], ACT.Copy).then_inc(hi_ready.sem, 1)

            def multiplied(l, n, i=0):
                e.wait_ge(unit_done.sem, l * UNITS + 4 * i + (n + 3))

            def square(l, s, d):
                if d >= 3:
                    e.wait_ge(ssq_done.sem, ssq_done.at(l, 7 * (s + 1) + d - 2))
                e.activation(ssq[:, :] if d == 0 else sq[:, d % 2, :], x[:, d, :], ACT.Square).then_inc(sq_done.sem, 1)

            def norm(l, s):
                e.wait_ge(norm_mm.sem, norm_mm.at(l, s + 1))
                e.activation(rstd[:, :], PS[:, 6, :], ACT.Sqrt, bias=eps[:, 0:1]).then_inc(root_done.sem, 1)
                e.wait_ge(mods_done.sem, mods_done.at(l, s + 1))
                for k in range(KD):
                    c = 8 * s + k
                    e.wait_ge(t_done.sem, t_done.at(l, c + 1))
                    if k >= 2:
                        e.wait_ge(ul_done.sem, ul_done.at(l, c - 1))
                    e.activation(u32[:, k % 2, :], t_buf[:, k % 2, :], ACT.Identity, scale=scale_eff[:, k:k + 1],
                                 bias=mod[:, k:k + 1]).then_inc(u32_done.sem, 1)
                    e.wait_ge(u32_done.sem, u32_done.at(l, c + 1))
                    e.activation(uh[:, k, :], u32[:, k % 2, :], ACT.Copy).then_inc(uh_done.sem, 1)

            def ffn(l, s, first, last):
                base_f = 22 * (s // 2)
                for half, F in enumerate(F_HALF):
                    f0 = base_f + F_HALF[0] * half

                    def use_in(i, j):
                        multiplied(l, first + j, i)
                        f = l * 44 + 2 * i + (f0 + j // 2)
                        if j % 2 == 0:
                            e.wait_ge(h_done.sem, f + 1)
                            e.activation(silu_s[:, j // 2, :], PS[:, j // 2, :], ACT.Silu).then_inc(silu_done.sem, 1)
                        else:
                            e.wait_ge(h_done.sem, f + 3)
                            dst = hh[:, bass.ds(2 * i + j // 2, 1), :].rearrange("p a n -> p (a n)")
                            e.activation(dst, h32[:, j // 2, :], ACT.Copy).then_inc(hh_done.sem, 1)

                    steps(e, l, first, 2 * F, KD, F, split, use_in)
                    first += 2 * F

                    def use_out(i, j):
                        if half == 1:
                            d = 4 * i + j
                            e.wait_ge(x_done.sem, x_done.at(l, out_index(l, s, half, d) + 1))
                            square(l, s, d)
                    steps(e, l, first, 8, F, KD if half == 0 or not last else None, split, use_out)
                    first += 8

            def mixing(l):
                e.wait_ge(layer_in.sem, layer_in.at(l, 80))
                e.activation(ab_hi[:, :, :], ab_raw[:, :, :], ACT.Copy).then_inc(ab_hi_done.sem, 1)

                def ahead(n):
                    split(l, (n + 2) // 4, 0, (n + 2) % 4, KD)

                def project(m, dst):
                    ahead(MIX + m)
                    multiplied(l, MIX + m)
                    e.activation(dst, PS[:, m % 4, :], ACT.Copy).then_inc(in_done.sem, 1)

                def gate_step(g):
                    m = gate_unit(g)
                    ahead(MIX + m)
                    multiplied(l, MIX + m)
                    if g >= 2:
                        e.wait_ge(gate_out[g % 2].sem, gate_out[g % 2].at(l, 16 * (g // 2)))
                    hold = (rstd, ssq)[g % 2]
                    e.activation(hold[:, :], PS[:, g % 2 if g < 16 else 7, :], ACT.Copy).then_inc(in_done.sem, 1)
                    e.wait_ge(in_done.sem, in_done.at(l, m + 1))
                    e.dma_start(gates_dram[g], hold[:, :]).then_inc(gate_out[g % 2].sem, 16)

                for m in range(14):
                    project(m, bp[:, m, :] if m < M_C else ct[m - M_C][:, :])
                    if 1 <= m <= 6:
                        e.wait_ge(conv_done.sem, conv_done.at(l, m))
                        e.activation(bp[:, m - 1, :], t_buf[:, (m - 1) % 2, :], ACT.Silu).then_inc(conv_silu.sem, 1)
                    if 8 <= m <= 11:
                        i = m - 8
                        e.wait_ge(conv_silu.sem, conv_silu.at(l, i + 1))
                        if i >= 2:
                            e.wait_ge(l2_mm.sem, l2_mm.at(l, i - 1))
                        e.activation(sq[:, i % 2, :], bp[:, i, :], ACT.Square).then_inc(l2_sq.sem, 1)
                    if 9 <= m <= 12:
                        i = m - 9
                        if i >= 2:
                            e.wait_ge(qk_done.sem, qk_done.at(l, i - 1))
                        e.wait_ge(l2_mm.sem, l2_mm.at(l, i + 1))
                        e.activation(h32[:, i % 2, :], PS[:, 4 + i % 2, :], ACT.Sqrt, bias=eps[:, 0:1])\
                            .then_inc(l2_root.sem, 1)
                e.wait_ge(ab_v.sem, ab_v.at(l, 2))
                e.activation(sc[:, 80:96], sc[:, 64:80], ACT.Abs).then_inc(ab_a.sem, 1)
                e.wait_ge(ab_a.sem, ab_a.at(l, 1))
                e.activation(sc[:, 96:112], sc[:, 80:96], ACT.Exp, scale=-1.0).then_inc(ab_a.sem, 1)
                e.activation(sc[:, 224:228], small[:, 4:8], ACT.Exp).then_inc(ab_a.sem, 1)
                e.wait_ge(ab_a.sem, ab_a.at(l, 2))
                e.activation(sc[:, 112:128], sc[:, 96:112], ACT.Ln, bias=eps[:, 1:2]).then_inc(ab_a.sem, 1)
                e.activation(sc[:, 16:32].rearrange("p (t s) -> p t s", t=TT),
                             sc[:, 32:64].rearrange("p (t s) -> p t s", t=TT)[:, :, 4:8], ACT.Sigmoid)\
                    .then_inc(ab_a.sem, 1)
                e.wait_ge(ab_v.sem, ab_v.at(l, 6))
                e.activation(sc[:, 176:192], sc[:, 128:144], ACT.Exp).then_inc(ab_a.sem, 1)
                e.activation(sc[:, 160:176], sc[:, 208:224], ACT.Exp).then_inc(ab_a.sem, 1)

                def decays(t):
                    e.wait_ge(diff_done.sem, diff_done.at(l, t + 1))
                    if t >= 1:
                        e.wait_ge(lt_done.sem, lt_done.at(l, t))
                        e.wait_ge(qe_done.sem, qe_done.at(l, t))
                    e.activation(dcy[:, :, :], lT[t % 2][:, :, :], ACT.Exp).then_inc(decay_done.sem, 1)
                    for par in range(2):
                        r = slice(64 * par, 64 * par + 64)
                        last = e.activation(eg[r, :, :], PS[r, 4 if t else 5, par * 256:par * 256 + 256]
                                            .rearrange("p (a n) -> p a n", a=2), ACT.Exp)
                    last.then_inc(eg_done.sem, 1)

                decays(0)
                for t in range(TT):
                    for lv in range(LEVELS):
                        g = 6 * t + lv
                        if lv >= 1:
                            e.wait_ge(y_mm.sem, y_mm.at(l, g + 1))
                            e.activation(Ym[:, :, :], PS[:, 5, :].rearrange("p (s n) -> p s n", s=4), ACT.Copy)\
                                .then_inc(y_done.sem, 1)
                        if g % 2 == 0 and g >= 2:
                            gate_step(g // 2 - 1)
                        if lv == 3 and t + 1 < TT:
                            decays(t + 1)
                    e.wait_ge(uw_mm.sem, uw_mm.at(l, t + 1))
                    e.activation(u_val[:, t, :, :], PS[:, 5, 0:256].rearrange("p (s n) -> p s n", s=4), ACT.Copy)
                    e.activation(wT[:, :, t * P:(t + 1) * P], PS[:, 5, 256:512].rearrange("p (a n) -> p a n", a=2),
                                 ACT.Copy).then_inc(uw_done.sem, 1)
                for g in range(11, 16):
                    gate_step(g)
                e.wait_ge(o_mm.sem, o_mm.at(l, 1))
                e.activation(bp[:, 4:6, :], PS[:, 6:8, :], ACT.Copy).then_inc(o_done.sem, 1)
                e.wait_ge(o_done.sem, o_done.at(l, 1))
                for i in range(2):
                    e.activation(sq[:, i, :], bp[:, 4 + i, :], ACT.Square).then_inc(on_sq.sem, 1)
                for i in range(2):
                    e.wait_ge(on_mm.sem, on_mm.at(l, i + 1))
                    e.activation(h32[:, i, :], PS[:, 4 + i, :], ACT.Sqrt, scale=1.0 / HEAD, bias=eps[:, 0:1])\
                        .then_inc(on_root.sem, 1)
                for i in range(2):
                    e.activation(bp[:, 6 + i, :], bp[:, 6 + i, :], ACT.Silu).then_inc(on_silu.sem, 1)
                for i in range(2):
                    e.wait_ge(on_step.sem, on_step.at(l, 3 * (i + 1)))
                    e.activation(oh[:, 2 + i, :], bp[:, 4 + i, :], ACT.Copy).then_inc(ob_hi.sem, 1)

                def probs_T(n, banks, dst):
                    e.wait_ge(pt_mm.sem, pt_mm.at(l, n + 1))
                    e.activation(dst, banks, ACT.Copy).then_inc(pt_done.sem, 1)

                e.wait_ge(vt_mm.sem, vt_mm.at(l, 1))
                e.activation(v_tok[:, :, 0:P], PS[:, 6, :].rearrange("p (t n) -> p t n", t=TT), ACT.Copy)\
                    .then_inc(vt_done.sem, 1)
                n = 0
                for t in range(TT):
                    lo = 0 if t else P
                    e.wait_ge(negmax_done.sem, negmax_done.at(l, t + 1))
                    for h in range(8):
                        e.activation(sco[:, h, lo:256], sco[:, h, lo:256], ACT.Exp, bias=mx[:, 16 + h:17 + h],
                                     accum_out=mx[:, 32 + h:33 + h])
                    e.wait_ge(s_step.sem, s_step.at(l, 5 * t + 3))
                    e.activation(mx[:, 40:48], mx[:, 24:32], ACT.Exp).then_inc(exp_done.sem, 1)
                    gate_step(16 + t)
                    if t >= 1:
                        e.wait_ge(pv_mm.sem, pv_mm.at(l, t))
                    for kt in ((0, 1) if t else (1,)):
                        probs_T(n, PS[:, 4:6, :], pT[:, 2 * kt:2 * kt + 2, :])
                        n += 1
                    e.wait_ge(pv_mm.sem, pv_mm.at(l, t + 1))
                    e.activation(oh[:, 4:8, t * P:(t + 1) * P], PS[:, 6, :].rearrange("p (a n) -> p a n", a=4),
                                 ACT.Copy).then_inc(o_hi.sem, 1)

                def gates_in(d):
                    for b in range(3):
                        e.dma_start(g_in[d % 2][b][:, :], gates_dram[8 * b + d]).then_inc(gate_back[d % 2].sem, 16)

                for q in range(2):
                    e.wait_ge(gate_out[q].sem, gate_out[q].at(l, 16 * 9))
                    gates_in(q)
                for m in range(M_A, M_A + 6):
                    project(m, pc[:, m - M_A, :])
                e.wait_ge(vt_mm.sem, vt_mm.at(l, 2))
                e.activation(v_tok[:, :, :].rearrange("p t (y n) -> p y t n", y=2),
                             PS[:, 6:8, :].rearrange("p y (t n) -> p y t n", t=TT), ACT.Copy).then_inc(vt_done.sem, 1)
                for t in range(TT):
                    w = (t + 1) * P
                    e.wait_ge(negmax_done.sem, negmax_done.at(l, 4 + t + 1))
                    for h in range(4):
                        sh = sco[:, 2 * h:2 * h + 2, :].rearrange("p a n -> p (a n)")
                        last = e.activation(sh[:, 0:w], sh[:, 0:w], ACT.Exp, bias=mx[:, 16 + h:17 + h],
                                            accum_out=mx[:, 32 + h:33 + h])
                    last.then_inc(exp_done.sem, 1)
                    gate_step(20 + t)
                    if t >= 1:
                        e.wait_ge(pv_mm.sem, pv_mm.at(l, 4 + t))
                    for kt in range(t + 1):
                        probs_T(n, PS[:, 4 + kt % 2, :], pT[:, kt, :])
                        n += 1
                    e.wait_ge(pv_mm.sem, pv_mm.at(l, 4 + t + 1))
                    e.activation(oh[:, 0:2, t * P:(t + 1) * P], PS[:, 6, 0:256].rearrange("p (a n) -> p a n", a=2),
                                 ACT.Copy).then_inc(o_hi.sem, 1)
                def sigmoids(d):
                    e.wait_ge(gate_back[d % 2].sem, gate_back[d % 2].at(l, 48 * (d // 2 + 1)))
                    for b in range(3):
                        last = e.activation(g_in[d % 2][b][:, :], g_in[d % 2][b][:, :], ACT.Sigmoid)
                    last.then_inc(sig_done.sem, 1)

                sigmoids(0)
                for q in range(2):
                    e.wait_ge(gate_out[q].sem, gate_out[q].at(l, 16 * 12))
                for d in range(KD):
                    ahead(U_UP + d)
                    if d + 1 < KD:
                        sigmoids(d + 1)
                    e.wait_ge(merge_step.sem, merge_step.at(l, 2 * (d + 1)))
                    e.activation(uh[:, d, :], up_m[:, 3, :], ACT.Copy).then_inc(mh_done.sem, 1)
                    if d + 2 < KD:
                        e.wait_ge(mg_used.sem, mg_used.at(l, d + 1))
                        gates_in(d + 2)
                for d in range(KD):
                    ahead(U_OUT + d)
                    e.wait_ge(x_done.sem, x_done.at(l, out_index(l, 1, 0, d) + 1))
                    square(l, 1, d)

            e.wait_ge(cond_in.sem, 16)
            e.activation(cond[:, :], cond[:, :], ACT.Silu).then_inc(cond_done.sem, 1)
            e.sem_inc(hi_ready.sem, RAW)
            e.wait_ge(x_in.sem, 16)
            e.wait_ge(consts_in.sem, 16 * 15)
            for d in range(KD):
                square(0, -1, d)
            with e.Fori(0, DEPTH) as l:
                split(l, 0, 0, 0, KD)
                split(l, 0, 0, 1, KD)
                norm(l, 0)
                ffn(l, 0, 0, False)
                norm(l, 1)
                mixing(l)
                norm(l, 2)
                ffn(l, 2, 2 * SUB, True)
            e.wait_ge(norm_mm.sem, 3 * DEPTH + 1)
            e.activation(rstd[:, :], PS[:, 6, :], ACT.Sqrt, bias=eps[:, 0:1]).then_inc(root_done.sem, 1)

        @block.vector
        def _(e):
            TTo, TS, STT = e.tensor_tensor, e.tensor_scalar, e.scalar_tensor_tensor

            def split(l, m0, i, j, K):
                e.wait_ge(hi_ready.sem, l * UNITS + 4 * i + (4 * m0 + j + 1 + RAW))
                TTo(wl[:, j % 2, 0:K * P], raw[:, j, 0:K * P], wh[:, j % 2, 0:K * P], ALU.subtract)\
                    .then_inc(lo_ready.sem, 1)

            def multiplied(l, n, i=0):
                e.wait_ge(unit_done.sem, l * UNITS + 4 * i + (n + 3))

            def add_square(l, s, d):
                if d == 0:
                    return
                e.wait_ge(sq_done.sem, sq_done.at(l, 8 * (s + 1) + d + 1))
                if d >= 2:
                    e.wait_ge(ssq_done.sem, ssq_done.at(l, 7 * (s + 1) + d - 1))
                TTo(ssq[:, :], ssq[:, :], sq[:, d % 2, :], ALU.add).then_inc(ssq_done.sem, 1)

            def norm(l, s):
                e.wait_ge(root_done.sem, root_done.at(l, s + 1))
                e.reciprocal(rstd[:, :], rstd[:, :]).then_inc(rstd_done.sem, 1)
                e.wait_ge(mods_mm.sem, mods_mm.at(l, s + 1))
                q = bass.ds(l * 3 + s, 1)
                TTo(mod[:, 0:16], PS[:, 7, 0:16], ada_b[:, q, 0:16].rearrange("p a n -> p (a n)"), ALU.add)\
                    .then_inc(mod_step.sem, 1)
                e.wait_ge(mod_step.sem, mod_step.at(l, s + 1))
                STT(out=scale_eff[:, :], in0=mod[:, 8:16], scalar=1.0,
                    in1=norm_g[:, q, :].rearrange("p a n -> p (a n)"), op0=ALU.add, op1=ALU.mult)\
                    .then_inc(mods_done.sem, 1)
                e.wait_ge(rstd_done.sem, rstd_done.at(l, s + 1))

                def scaled(k):
                    if k >= 2:
                        e.wait_ge(u32_done.sem, u32_done.at(l, 8 * s + k - 1))
                    TTo(t_buf[:, k % 2, :], x[:, k, :], rstd[:, :], ALU.mult).then_inc(t_done.sem, 1)
                scaled(0)
                scaled(1)
                for k in range(KD):
                    e.wait_ge(uh_done.sem, uh_done.at(l, 8 * s + k + 1))
                    TTo(ul[:, k, :], u32[:, k % 2, :], uh[:, k, :], ALU.subtract).then_inc(ul_done.sem, 1)
                    if k + 2 < KD:
                        scaled(k + 2)

            def gate_mods(l, s):
                q = bass.ds(l * 3 + s, 1)
                e.wait_ge(gate_mods_mm.sem, gate_mods_mm.at(l, s + 1))
                TTo(mod[:, 16:24], PS[:, 7, 16:24], ada_b[:, q, 16:24].rearrange("p a n -> p (a n)"), ALU.add)\
                    .then_inc(gate_mod_step.sem, 1)
                e.wait_ge(gate_mod_step.sem, gate_mod_step.at(l, s + 1))
                TS(gate_eff[:, :], mod[:, 16:24], 1.0 if s == 1 else 0.5, None, ALU.mult)\
                    .then_inc(gate_mods_done.sem, 1)
                e.wait_ge(gate_mods_done.sem, gate_mods_done.at(l, s + 1))

            def residual(l, s, half, d, bank):
                STT(out=x[:, d, :], in0=PS[:, bank, :], scalar=gate_eff[:, d:d + 1], in1=x[:, d, :],
                    op0=ALU.mult, op1=ALU.add).then_inc(x_done.sem, 1)

            def ffn(l, s, first, last):
                base_f = 22 * (s // 2)
                for half, F in enumerate(F_HALF):
                    f0 = base_f + F_HALF[0] * half

                    def use_in(i, j):
                        if j % 2 == 0:
                            return
                        f = l * 44 + 2 * i + (f0 + j // 2)
                        multiplied(l, first + j, i)
                        e.wait_ge(silu_done.sem, f + 3)
                        TTo(h32[:, j // 2, :], silu_s[:, j // 2, :], PS[:, 2 + j // 2, :], ALU.mult)\
                            .then_inc(h_done.sem, 1)
                        e.wait_ge(hh_done.sem, f + 1)
                        slot = bass.ds(2 * i + j // 2, 1)
                        TTo(hl[:, slot, :].rearrange("p a n -> p (a n)"), h32[:, j // 2, :],
                            hh[:, slot, :].rearrange("p a n -> p (a n)"), ALU.subtract).then_inc(hl_done.sem, 1)

                    steps(e, l, first, 2 * F, KD, F, split, use_in)
                    first += 2 * F
                    if half == 0:
                        gate_mods(l, s)

                    def use_out(i, j):
                        multiplied(l, first + j, i)
                        residual(l, s, half, 4 * i + j, 4 + j % 2)
                        if half == 1:
                            add_square(l, s, 4 * i + j)
                    steps(e, l, first, 8, F, KD if half == 0 or not last else None, split, use_out)
                    first += 8

            def mixing(l):
                def ahead(n):
                    split(l, (n + 2) // 4, 0, (n + 2) % 4, KD)

                e.wait_ge(ab_hi_done.sem, ab_hi_done.at(l, 1))
                TTo(ab_lo[:, :, :], ab_raw[:, :, :], ab_hi[:, :, :], ALU.subtract).then_inc(ab_lo_done.sem, 1)
                by_t = lambda c: sc[:, c:c + 16].rearrange("p (t s) -> p t s", t=TT)
                for m in range(14):
                    ahead(MIX + m)
                    if m < 6:
                        e.wait_ge(in_done.sem, in_done.at(l, m + 1))
                        if m >= 2:
                            e.wait_ge(conv_silu.sem, conv_silu.at(l, m - 1))
                        y, v = t_buf[:, m % 2, :], bp[:, m, :]
                        TS(y, v, conv_w[:, m, 3:4], None, ALU.mult).then_inc(conv_step.sem, 1)
                        for back in (1, 2, 3):
                            e.wait_ge(conv_step.sem, conv_step.at(l, 3 * m + back))
                            STT(out=y[:, back:], in0=v[:, :SEQ - back], scalar=conv_w[:, m, 3 - back:4 - back],
                                in1=y[:, back:], op0=ALU.mult, op1=ALU.add)\
                                .then_inc((conv_step if back < 3 else conv_done).sem, 1)
                    if m == 6:
                        TTo(a_bias[:, :, :], a_bias[:, :, :], a_mask[:, :].unsqueeze(1).broadcast_to([P, 4, 2 * P]),
                            ALU.add).then_inc(bias_masked.sem, 1)
                    if m == 9:
                        e.wait_ge(ab_mm.sem, ab_mm.at(l, 1))
                        e.tensor_copy(sc[:, 32:64], PS[:, 6, 0:32]).then_inc(ab_v.sem, 1)
                        e.wait_ge(ab_v.sem, ab_v.at(l, 1))
                        TTo(by_t(64), sc[:, 32:64].rearrange("p (t s) -> p t s", t=TT)[:, :, 0:4],
                            small[:, 0:4].unsqueeze(1).broadcast_to([P, TT, 4]), ALU.add).then_inc(ab_v.sem, 1)
                    if m >= 10:
                        i = m - 10
                        e.wait_ge(l2_root.sem, l2_root.at(l, i + 1))
                        e.reciprocal(h32[:, i % 2, :], h32[:, i % 2, :]).then_inc(l2_inv.sem, 1)
                        e.wait_ge(l2_inv.sem, l2_inv.at(l, i + 1))
                        STT(out=bp[:, i, :], in0=bp[:, i, :], scalar=HEAD ** -0.5 if i < 2 else 1.0,
                            in1=h32[:, i % 2, :], op0=ALU.mult, op1=ALU.mult).then_inc(qk_done.sem, 1)
                gate_mods(l, 1)
                e.wait_ge(ab_a.sem, ab_a.at(l, 4))
                STT(out=sc[:, 192:208], in0=sc[:, 64:80], scalar=0.0, in1=sc[:, 112:128], op0=ALU.max, op1=ALU.add)\
                    .then_inc(ab_v.sem, 1)
                e.wait_ge(ab_v.sem, ab_v.at(l, 3))
                STT(out=by_t(0), in0=by_t(192), scalar=-1.0, in1=sc[:, 224:228].unsqueeze(1).broadcast_to([P, TT, 4]),
                    op0=ALU.mult, op1=ALU.mult).then_inc(ab_v.sem, 1)
                e.wait_ge(gc_mm.sem, gc_mm.at(l, 1))
                e.tensor_copy(sc[:, 128:160], PS[:, 6, 32:64]).then_inc(ab_v.sem, 1)
                e.wait_ge(ab_v.sem, ab_v.at(l, 5))
                TTo(sc[:, 208:224], sc[:, 144:160], sc[:, 128:144], ALU.subtract).then_inc(ab_v.sem, 1)
                e.wait_ge(ab_a.sem, ab_a.at(l, 7))
                TTo(sc[:, 192:208], sc[:, 16:32], sc[:, 176:192], ALU.mult).then_inc(ab_v.sem, 1)

                by_s = lambda m: m.unsqueeze(1).broadcast_to([P, 4, P])
                heads = lambda v: v.rearrange("p (a b n) -> p b a n", a=2, b=2)
                slots = lambda v: v.rearrange("p (b a) n -> p b a n", a=2)
                ps4 = lambda b: PS[:, b, :].rearrange("p (s n) -> p s n", s=4)

                def per_head(c):
                    return sc[:, c:c + 4].rearrange("p (b a) -> p b a", a=2).unsqueeze(3).broadcast_to([P, 2, 2, HEAD])


                def differences(t):
                    e.wait_ge(gcb_mm.sem, gcb_mm.at(l, t + 1))
                    if t >= 2:
                        e.wait_ge(ct_done.sem, ct_done.at(l, 6 * (t - 1)))
                    for s in range(4):
                        last = TS(lT[t % 2][:, s, :], PS[:, 4 if t else 5, s * P:(s + 1) * P],
                                  sc[:, 128 + 4 * t + s:129 + 4 * t + s], 0.0, ALU.subtract, ALU.min)
                    last.then_inc(diff_done.sem, 1)

                def within(t):
                    e.wait_ge(decay_done.sem, decay_done.at(l, t + 1))
                    TTo(dcy[:, :, :], dcy[:, :, :], by_s(tri[:, :]), ALU.mult).then_inc(mask_step.sem, 1)
                    e.wait_ge(kk_mm.sem, kk_mm.at(l, t + 1))
                    e.wait_ge(mask_step.sem, mask_step.at(l, 4 * t + 1))
                    for par in range(2):
                        last = TTo(intra[:, t, 2 * par:2 * par + 2, :],
                                   PS[:, 2 + par, 256:512].rearrange("p (a n) -> p a n", a=2),
                                   dcy[:, 2 * par:2 * par + 2, :], ALU.mult)
                    last.then_inc(mask_step.sem, 1)

                def lower(t):
                    e.wait_ge(mask_step.sem, mask_step.at(l, 4 * t + 2))
                    TTo(dcy[:, :, :], dcy[:, :, :], by_s(strict[:, :]), ALU.mult).then_inc(mask_step.sem, 1)
                    e.wait_ge(mask_step.sem, mask_step.at(l, 4 * t + 3))
                    for par in range(2):
                        last = TTo(lT[t % 2][:, 2 * par:2 * par + 2, :],
                                   PS[:, 2 + par, 0:256].rearrange("p (a n) -> p a n", a=2),
                                   dcy[:, 2 * par:2 * par + 2, :], ALU.mult)
                    last.then_inc(mask_step.sem, 1)
                    e.wait_ge(bb_mm.sem, bb_mm.at(l, t + 1))
                    e.wait_ge(mask_step.sem, mask_step.at(l, 4 * t + 4))
                    TTo(lT[t % 2][:, :, :], lT[t % 2][:, :, :], ps4(4 if t else 6), ALU.mult).then_inc(lt_done.sem, 1)

                def decayed_q(t):
                    e.wait_ge(kk_mm.sem, kk_mm.at(l, t + 1))
                    e.wait_ge(eg_done.sem, eg_done.at(l, t + 1))
                    e.tensor_copy(egl[:, t, :, :], eg[:, :, CHUNK - 1::CHUNK])
                    TTo(bp[:, 0:2, t * P:(t + 1) * P], bp[:, 0:2, t * P:(t + 1) * P], eg[:, :, :], ALU.mult)\
                        .then_inc(qe_done.sem, 1)

                def rope(i):
                    e.wait_ge(rot_mm.sem, rot_mm.at(l, i + 1))
                    TTo(sq[:, i % 2, :], PS[:, 2 + i // 4, :], sin[:, :], ALU.mult).then_inc(rot_step.sem, 1)
                    TTo(ct[i][:, :], ct[i][:, :], cos[:, :], ALU.mult).then_inc(rot_step.sem, 1)
                    e.wait_ge(rot_step.sem, rot_step.at(l, 2 * i + 2))
                    TTo(ct[i][:, :], ct[i][:, :], sq[:, i % 2, :], ALU.add).then_inc(rope_done.sem, 1)

                differences(0)
                within(0)
                lower(0)
                decayed_q(0)
                for t in range(TT):
                    e.wait_ge(lt_done.sem, lt_done.at(l, t + 1))

                    def blocks(lv):
                        g = 6 * t + lv
                        if g >= 1:
                            e.wait_ge(y_mm.sem, y_mm.at(l, g))
                        if lv == 1:
                            e.wait_ge(u_done.sem, u_done.at(l, 6 * t + 1))
                        TTo(cT[:, :, :], lT[t % 2][:, :, :], by_s(level_mask[:, lv, :]), ALU.mult)\
                            .then_inc(ct_done.sem, 1)

                    blocks(0)
                    e.wait_ge(ct_done.sem, ct_done.at(l, 6 * t + 1))
                    if t >= 1:
                        e.wait_ge(uw_mm.sem, uw_mm.at(l, t))
                    TTo(Um[:, :, :], by_s(ident[:, :]), cT[:, :, :], ALU.subtract).then_inc(u_done.sem, 1)
                    for lv in range(LEVELS):
                        g = 6 * t + lv
                        if lv == 0:
                            e.wait_ge(y_mm.sem, y_mm.at(l, g + 1))
                            TTo(Tm[:, :, :], by_s(ident[:, :]), ps4(7), ALU.subtract).then_inc(tm_done.sem, 1)
                        if lv < LEVELS - 1:
                            blocks(lv + 1)
                        if g % 2 == 0 and g >= 2:
                            ahead(MIX + gate_unit(g // 2 - 1))
                        if lv >= 1:
                            e.wait_ge(z_mm.sem, z_mm.at(l, 5 * t + lv))
                            if lv < LEVELS - 1:
                                TTo(Tm[:, :, :], Tm[:, :, :], ps4(7), ALU.subtract).then_inc(tm_done.sem, 1)
                            e.wait_ge(u_done.sem, u_done.at(l, g))
                            TTo(Um[:, :, :], Um[:, :, :], ps4(6), ALU.subtract).then_inc(u_done.sem, 1)
                        if lv == 0:
                            e.wait_ge(tr_mm.sem, tr_mm.at(l, t + 1))
                            e.wait_ge(ab_v.sem, ab_v.at(l, 7))
                            TTo(slots(v_beta[:, :, :]), heads(PS[:, 4, 256:512]), per_head(16 + 4 * t), ALU.mult)
                            TTo(slots(k_beta[:, :, :]), heads(PS[:, 4, 0:256]), per_head(192 + 4 * t), ALU.mult)
                            TTo(slots(k_dec[:, t, :, :]), heads(PS[:, 4, 0:256]), per_head(160 + 4 * t), ALU.mult)\
                                .then_inc(tok_done.sem, 1)
                        if lv == 1:
                            rope(t)
                        if t + 1 < TT:
                            if lv == 2:
                                differences(t + 1)
                            if lv == 4:
                                within(t + 1)
                            if lv == 5:
                                lower(t + 1)
                                decayed_q(t + 1)
                        elif lv == 4:
                            rope(4)
                e.memset(st[:, 0, :, :], 0.0).then_inc(st_zero.sem, 1)
                e.wait_ge(uw_done.sem, uw_done.at(l, TT))
                e.wait_ge(qe_done.sem, qe_done.at(l, TT))
                e.wait_ge(st_zero.sem, st_zero.at(l, 1))
                for n in range(NCH):
                    t, pb = n // 2, 64 * (n % 2)
                    e.wait_ge(ws_mm.sem, ws_mm.at(l, n + 1))
                    for par in range(2):
                        v = u_val[pb:pb + 64, t, 2 * par:2 * par + 2, :]
                        last = TTo(v, v, PS[pb:pb + 64, 2 + par, 0:2 * HEAD].rearrange("p (a n) -> p a n", a=2),
                                   ALU.subtract)
                    last.then_inc(vnew_done.sem, 1)
                    e.wait_ge(kv_mm.sem, kv_mm.at(l, n + 1))
                    if n >= 1:
                        e.wait_ge(st_done.sem, st_done.at(l, n))
                    for pair in range(2):
                        last = STT(out=st[:, n + 1, pair, :], in0=st[:, n, pair, :], scalar=egl[:, t, pair, n % 2:n % 2 + 1],
                                   in1=PS[:, 4 + n % 2, pair * HEAD:(pair + 1) * HEAD], op0=ALU.mult, op1=ALU.add)
                    last.then_inc(st_done.sem, 1)
                    if n % 2 == 0:
                        ahead(MIX + gate_unit(11 + n // 2))
                ahead(MIX + gate_unit(15))
                for i in range(2):
                    e.wait_ge(on_root.sem, on_root.at(l, i + 1))
                    e.reciprocal(h32[:, i, :], h32[:, i, :]).then_inc(on_step.sem, 1)
                    e.wait_ge(on_step.sem, on_step.at(l, 3 * i + 1))
                    STT(out=bp[:, 4 + i, :], in0=bp[:, 4 + i, :], scalar=small[:, 8:9], in1=h32[:, i, :],
                        op0=ALU.mult, op1=ALU.mult).then_inc(on_step.sem, 1)
                    e.wait_ge(on_step.sem, on_step.at(l, 3 * i + 2))
                    e.wait_ge(on_silu.sem, on_silu.at(l, i + 1))
                    TTo(bp[:, 4 + i, :], bp[:, 4 + i, :], bp[:, 6 + i, :], ALU.mult).then_inc(on_step.sem, 1)
                for i in range(2):
                    e.wait_ge(ob_hi.sem, ob_hi.at(l, i + 1))
                    TTo(ol[:, 2 + i, :], bp[:, 4 + i, :], oh[:, 2 + i, :], ALU.subtract).then_inc(ob_lo.sem, 1)

                n_pt = 0
                for t in range(TT):
                    lo = 0 if t else P
                    e.wait_ge(s_mm.sem, s_mm.at(l, t + 1))
                    if t >= 1:
                        e.wait_ge(pt_mm.sem, pt_mm.at(l, n_pt))
                    n_pt += 2 if t else 1
                    STT(out=sco[:, :, lo:256], in0=PS[:, 0:4, :].rearrange("p b (c n) -> p (b c) n", c=2)[:, :, lo:256],
                        scalar=HEAD ** -0.5, in1=c_mask[:, :].unsqueeze(1).broadcast_to([P, 8, 2 * P])[:, :, lo:256],
                        op0=ALU.mult, op1=ALU.add).then_inc(bias_done.sem, 1)
                    e.wait_ge(bias_done.sem, bias_done.at(l, t + 1))
                    e.tensor_reduce(mx[:, 0:8], sco[:, :, lo:256], AX.X, ALU.max).then_inc(s_step.sem, 1)
                    e.wait_ge(s_step.sem, s_step.at(l, 5 * t + 1))
                    TTo(mx[:, 8:16], mx[:, 0:8], small[:, 16:24], ALU.max).then_inc(s_step.sem, 1)
                    e.wait_ge(s_step.sem, s_step.at(l, 5 * t + 2))
                    TS(mx[:, 16:24], mx[:, 8:16], -1.0, None, ALU.mult).then_inc(negmax_done.sem, 1)
                    TTo(mx[:, 24:32], small[:, 16:24], mx[:, 8:16], ALU.subtract).then_inc(s_step.sem, 1)
                    e.wait_ge(exp_done.sem, exp_done.at(l, t + 1))
                    TTo(mx[:, 48:56], mx[:, 32:40], mx[:, 40:48], ALU.add).then_inc(s_step.sem, 1)
                    e.wait_ge(s_step.sem, s_step.at(l, 5 * t + 4))
                    e.reciprocal(mx[:, 56:64], mx[:, 48:56]).then_inc(s_step.sem, 1)
                    e.wait_ge(s_step.sem, s_step.at(l, 5 * t + 5))
                    TTo(sco[:, :, lo:256], sco[:, :, lo:256],
                        mx[:, 56:64].unsqueeze(2).broadcast_to([P, 8, 2 * P])[:, :, lo:256], ALU.mult)\
                        .then_inc(prob_done.sem, 1)
                    ahead(MIX + gate_unit(16 + t))
                    e.wait_ge(o_hi.sem, o_hi.at(l, t + 1))
                    TTo(ol[:, 4:8, t * P:(t + 1) * P], PS[:, 6, :].rearrange("p (a n) -> p a n", a=4),
                        oh[:, 4:8, t * P:(t + 1) * P], ALU.subtract).then_inc(o_lo.sem, 1)

                for m in range(M_A, M_A + 6):
                    ahead(MIX + m)
                e.wait_ge(bias_masked.sem, bias_masked.at(l, 1))
                sA = sco[:, :, :].rearrange("p (h a) n -> p h (a n)", a=2)
                for t in range(TT):
                    w, near = (t + 1) * P, max(t - 1, 0) * P
                    e.wait_ge(s_mm.sem, s_mm.at(l, 4 + t + 1))
                    e.wait_ge(pt_mm.sem, pt_mm.at(l, n_pt))
                    n_pt += t + 1
                    if near:
                        for h in range(4):
                            TS(sA[:, h, 0:near], PS[:, h, 0:near], HEAD ** -0.5, a_far[:, h:h + 1], ALU.mult, ALU.add)
                    STT(out=sA[:, :, near:w], in0=PS[:, 0:4, near:w], scalar=HEAD ** -0.5,
                        in1=a_bias[:, :, 256 - (w - near):256], op0=ALU.mult, op1=ALU.add).then_inc(bias_done.sem, 1)
                    e.wait_ge(bias_done.sem, bias_done.at(l, 4 + t + 1))
                    e.tensor_reduce(mx[:, 0:4], sA[:, :, 0:w], AX.X, ALU.max).then_inc(s_step.sem, 1)
                    e.wait_ge(s_step.sem, s_step.at(l, 20 + 2 * t + 1))
                    TS(mx[:, 16:20], mx[:, 0:4], -1.0, None, ALU.mult).then_inc(negmax_done.sem, 1)
                    e.wait_ge(exp_done.sem, exp_done.at(l, 4 + t + 1))
                    e.reciprocal(mx[:, 56:60], mx[:, 32:36]).then_inc(s_step.sem, 1)
                    e.wait_ge(s_step.sem, s_step.at(l, 20 + 2 * t + 2))
                    TTo(sA[:, :, 0:w], sA[:, :, 0:w], mx[:, 56:60].unsqueeze(2).broadcast_to([P, 4, w]), ALU.mult)\
                        .then_inc(prob_done.sem, 1)
                    ahead(MIX + gate_unit(20 + t))
                    e.wait_ge(o_hi.sem, o_hi.at(l, 4 + t + 1))
                    TTo(ol[:, 0:2, t * P:(t + 1) * P], PS[:, 6, 0:256].rearrange("p (a n) -> p a n", a=2),
                        oh[:, 0:2, t * P:(t + 1) * P], ALU.subtract).then_inc(o_lo.sem, 1)

                for d in range(KD):
                    n = U_UP + d
                    ahead(n)
                    multiplied(l, n)
                    e.wait_ge(sig_done.sem, sig_done.at(l, d + 1))
                    for b in range(3):
                        last = TTo(up_m[:, b, :], g_in[d % 2][b][:, :], PS[:, 3 * (d % 2) + b, :], ALU.mult)
                    last.then_inc(mg_used.sem, 1)
                    e.wait_ge(mg_used.sem, mg_used.at(l, d + 1))
                    TTo(up_m[:, 0, :], up_m[:, 0, :], up_m[:, 1, :], ALU.add).then_inc(merge_step.sem, 1)
                    e.wait_ge(merge_step.sem, merge_step.at(l, 2 * d + 1))
                    TTo(up_m[:, 3, :], up_m[:, 0, :], up_m[:, 2, :], ALU.add).then_inc(merge_step.sem, 1)
                    e.wait_ge(mh_done.sem, mh_done.at(l, d + 1))
                    TTo(ul[:, d, :], up_m[:, 3, :], uh[:, d, :], ALU.subtract).then_inc(ml_done.sem, 1)
                for d in range(KD):
                    n = U_OUT + d
                    ahead(n)
                    multiplied(l, n)
                    residual(l, 1, 0, d, 6 + d % 2)
                    add_square(l, 1, d)

            for s in (lo_ready, unit_done, silu_done, h_done, x_done, in_done, mg_used):
                e.sem_inc(s.sem, s.credit)
            e.wait_ge(cond_done.sem, 1)
            for lot in range(3):
                ada_lot(e, ada0[:, 4 * lot:4 * lot + 4, :], lot, ada0_step, 3 * lot, ada0_in[lot])
            e.wait_ge(x_in.sem, 16)
            e.wait_ge(consts_in.sem, 16 * 15)
            for d in range(KD):
                add_square(0, -1, d)
            with e.Fori(0, DEPTH) as l:
                split(l, 0, 0, 0, KD)
                split(l, 0, 0, 1, KD)
                norm(l, 0)
                ffn(l, 0, 0, False)
                norm(l, 1)
                mixing(l)
                norm(l, 2)
                ffn(l, 2, 2 * SUB, True)
            e.wait_ge(root_done.sem, 3 * DEPTH + 1)
            e.reciprocal(rstd[:, :], rstd[:, :]).then_inc(rstd_done.sem, 1)
            e.wait_ge(rstd_done.sem, 3 * DEPTH + 1)
            for d in range(KD):
                if d >= 2:
                    e.wait_ge(out_done[d % 2].sem, 16 * (d // 2))
                STT(out=sq[:, d % 2, :], in0=x[:, d, :], scalar=final_g[:, d:d + 1], in1=rstd[:, :],
                    op0=ALU.mult, op1=ALU.mult).then_inc(out_ready.sem, 1)


def _units(w, cols):
    L, K, _ = w.shape
    w = w[:, :, cols].reshape(L, K // P, P, len(cols) // P, P)
    return np.ascontiguousarray(w.transpose(0, 3, 2, 1, 4)).reshape(-1, P, K // P * P)


def _cols(v):
    v = v.reshape(v.shape[:-1] + (v.shape[-1] // P, P))
    return np.ascontiguousarray(np.moveaxis(v, -1, 0))


def _layout(i):
    f32 = np.float32
    L = DEPTH
    i = {k: np.asarray(v) for k, v in i.items()}
    o = {}
    o["x"] = _cols(i["x"].reshape(SEQ, D_MODEL)).transpose(0, 2, 1)
    o["c"] = _cols(i["c"].reshape(D_MODEL))
    o["ada_w"] = _units(i["ada_w"], np.arange(9 * D_MODEL))
    o["ada_b"] = _cols(i["ada_b"].reshape(6, 3 * D_MODEL))
    o["norm_g"] = _cols(np.stack([i["ffn1_norm_g"], i["mix_norm_g"], i["ffn2_norm_g"]], 1).reshape(6, D_MODEL))
    o["final_g"] = _cols(i["final_norm_g"])
    F = D_FF // P
    pairs = np.stack([np.arange(D_FF).reshape(F, P), D_FF + np.arange(D_FF).reshape(F, P)], 1).reshape(-1)
    for n in ("ffn1", "ffn2"):
        o[n + "_in"] = _units(i[n + "_w_in"], pairs)
        cut = F_HALF[0] * P
        o[n + "_out0"] = _units(i[n + "_w_out"][:, :cut], np.arange(D_MODEL))
        o[n + "_out1"] = _units(i[n + "_w_out"][:, cut:], np.arange(D_MODEL))
    AQ, AK, AV, BQ, BZ, BA, BB, CQ, CK, CV, G = np.cumsum([0, 256, 256, 256, 768, 256, 4, 4, 512, 128, 128])
    r = np.arange
    cq = np.concatenate([CQ + 64 * h + r(64) for j in range(4) for h in (j, j + 4)])
    cols = np.concatenate([BQ + r(768), BZ + r(256), cq, CK + r(128), CV + r(128), G + r(2560),
                           AQ + r(256), AK + r(256), AV + r(256), G + 2560 + r(512)])
    o["mix_in"] = _units(i["mix_w_in"], cols)
    slot = np.array(HEAD_OF_SLOT)
    ab = i["mix_w_in"][:, :, np.concatenate([BA + slot, BB + slot])]
    o["w_ab"] = np.ascontiguousarray(ab.reshape(L, KD, P, 8).transpose(0, 2, 1, 3))
    up_c = i["w_up_c"][:, np.concatenate([64 * h + r(64) for j in range(4) for h in (j, j + 4)])]
    o["mix_up"] = _units(np.concatenate([i["w_up_a"], i["w_up_b"], up_c], 1), r(D_MODEL))
    o["mix_out"] = _units(i["mix_w_out"], r(D_MODEL))
    p, j = r(P)[:, None], r(2 * P)[None, :]
    rel = np.clip(P + p - j, -(CHUNK - 1), 128) + CHUNK - 1
    o["a_bias"] = np.ascontiguousarray(i["a_rel_bias"][:, :, rel].transpose(0, 2, 1, 3))
    o["a_far"] = np.ascontiguousarray(np.broadcast_to(i["a_rel_bias"][:, None, :, -1], (L, P, 4)))
    o["conv_w"] = np.ascontiguousarray(i["b_conv_w"].reshape(L, 4, 6, P).transpose(0, 3, 2, 1))
    small = np.zeros((L, P, 32), f32)
    small[:, :, 0:4] = i["b_dt_bias"][:, None, slot]
    small[:, :, 4:8] = i["b_a_log"][:, None, slot]
    small[:, 0:64, 8] = i["b_norm_g"]
    small[:, 64:128, 8] = i["b_norm_g"]
    small[:, :, 16:24] = i["c_sinks"][:, None, :]
    o["small"] = small
    q, c = r(P)[:, None], r(P)[None, :]
    same = q // CHUNK == c // CHUNK
    o["ident"] = np.eye(P, dtype=f32)
    o["ones_mean"] = np.full((P, P), 1.0 / D_MODEL, f32)
    o["eps"] = np.stack([np.full(P, EPS, f32), np.ones(P, f32)], 1)
    o["tri"] = (same & (q <= c)).astype(f32)
    o["same_chunk"] = same.astype(f32)
    o["strict"] = (q < c).astype(f32)
    o["level_mask"] = np.stack([(c // 2 ** v == q // 2 ** v + 1) & (q // 2 ** v % 2 == 0) for v in range(LEVELS)], 1).astype(f32)
    rot = np.zeros((P, P), f32)
    for h in range(2):
        for d in range(32):
            rot[64 * h + 32 + d, 64 * h + d] = -1.0
            rot[64 * h + d, 64 * h + 32 + d] = 1.0
    o["rot"] = rot
    inv = np.float32(10000.0) ** (-np.arange(32, dtype=f32) / np.float32(32))
    ang = np.arange(SEQ, dtype=f32)[None, :] * inv[:, None].astype(f32)
    o["cos"] = np.tile(np.cos(ang).astype(f32), (4, 1))
    o["sin"] = np.tile(np.sin(ang).astype(f32), (4, 1))
    kc, qc = j // CHUNK - 2, p // CHUNK
    o["c_mask"] = np.where((kc == qc) | (kc == qc - 1), 0.0, NEG).astype(f32)
    o["a_mask"] = np.where(kc <= qc, 0.0, NEG).astype(f32)
    return {k: np.ascontiguousarray(v) for k, v in o.items()}


def kernel(**inputs):
    import concourse.bacc as _bacc
    from concourse.bass_utils import run_bass_kernel_spmd as _run

    nc = _bacc.Bacc("TRN2", target_bir_lowering=False, num_devices=1)
    arrays, aps = {}, {}
    for name, v in _layout(inputs).items():
        arrays[f"in_{name}_dram"] = v
        aps[name] = nc.dram_tensor(f"in_{name}_dram", v.shape, mybir.dt.from_np(v.dtype), kind="ExternalInput").ap()
    out = nc.dram_tensor("out_dram", (P, KD, SEQ), F32, kind="ExternalOutput").ap()
    encoder_kernel(nc, aps, out)
    r = _run(nc, [arrays], core_ids=[0])
    got = r.results[0]["out_dram"]
    return np.ascontiguousarray(got.transpose(2, 1, 0)).reshape(1, SEQ, D_MODEL)
```

```python
from contextlib import ExitStack

import numpy as np

import concourse.bass as bass
from concourse import mybir

F32 = mybir.dt.float32
F32R = mybir.dt.float32r
ALU = mybir.AluOpType
ACT = mybir.ActivationFunctionType
AX = mybir.AxisListType

P = 128
D_MODEL, SEQ, DEPTH = 1024, 512, 2
CHUNK, HEAD = 64, 64
D_FF = 2816
EPS = 1e-6
KD = D_MODEL // P
TT = SEQ // P
NCH = SEQ // CHUNK
F_HALF = (12, 10)
KMAX = max(F_HALF)
ADA_STEPS = 12
ADA_LOTS = KD
RAW = 4
UNITS = 180
SUB = 60
MIX = SUB
M_C, M_A, M_IN = 8, 31, 44
U_UP, U_OUT = MIX + M_IN, MIX + M_IN + 8
NEG = -1e30
assert 2 * (sum(F_HALF) * P) == 2 * D_FF and U_OUT + 8 == 2 * SUB

HEAD_OF_SLOT = (0, 2, 1, 3)
LEVELS = 6


def gate_unit(g):
    return 14 + g if g < 17 else M_A + 6 + g - 17


class Signal:

    def __init__(self, sem, per_layer, credit=0):
        self.sem, self.per_layer, self.credit = sem, per_layer, credit

    def at(self, layer, n):
        return layer * self.per_layer + (n + self.credit)


def encoder_kernel(nc, a, out):
    ctx = ExitStack()
    with ctx:
        base = [16512]

        def place(name, shape, dt, at=None):
            size = 4 * int(np.prod(shape[1:]))
            size = (size + 31) // 32 * 32
            off = base[0] if at is None else at
            if at is None:
                base[0] += size
            return nc.alloc_sbuf_tensor_at(name, shape, dt, offset=off)

        x = place("x", [P, KD, SEQ], F32)
        uh = place("uh", [P, KD, SEQ], F32R)
        ul = place("ul", [P, KD, SEQ], F32R)
        RAW0 = base[0]
        raw = place("raw", [P, RAW, KMAX * P], F32)
        WH0 = base[0]
        wh = place("wh", [P, 2, KMAX * P], F32R)
        wl = place("wl", [P, 2, KMAX * P], F32R)
        ada_raw = place("ada_raw", [P, 2, KD * P], F32)
        ada_sum = place("ada_sum", [P, 24], F32)
        cond = place("cond", [P, KD * P], F32)
        ada_b = place("ada_b", [P, 6 * 24], F32)
        norm_g = place("norm_g", [P, 6, KD], F32)
        final_g = place("final_g", [P, KD], F32)
        scale_eff = place("scale_eff", [P, KD], F32)
        gate_eff = place("gate_eff", [P, KD], F32)
        ident = place("ident", [P, P], F32)
        ones_mean = place("ones_mean", [P, P], F32)
        eps = place("eps", [P, 2], F32)
        tri = place("tri", [P, P], F32)
        same_chunk = place("same_chunk", [P, P], F32)
        strict = place("strict", [P, P], F32)
        level_mask = place("level_mask", [P, LEVELS, P], F32)
        rot = place("rot", [P, P], F32)
        cos = place("cos", [P, SEQ], F32)
        sin = place("sin", [P, SEQ], F32)
        c_mask = place("c_mask", [P, 2 * P], F32)
        a_mask = place("a_mask", [P, 2 * P], F32)
        a_bias = place("a_bias", [P, 4, 2 * P], F32)
        a_far = place("a_far", [P, 4], F32)
        conv_w = place("conv_w", [P, 6, 4], F32)
        small = place("small", [P, 32], F32)
        ab_raw = place("ab_raw", [P, KD, 8], F32)
        ab_hi = place("ab_hi", [P, KD, 8], F32R)
        ab_lo = place("ab_lo", [P, KD, 8], F32R)
        sc = place("sc", [P, 256], F32)
        mx = place("mx", [P, 64], F32)
        egl = place("egl", [P, TT, 2, 2], F32)
        root_tok = place("root_tok", [P, TT], F32)
        rstd_tok = place("rstd_tok", [P, TT], F32)
        ab_T = place("ab_T", [8, SEQ], F32)
        warm = place("warm", [P, 2], F32)
        gate_hold = place("gate_hold", [P, SEQ], F32)
        ssq = place("ssq", [P, SEQ], F32)
        sq = place("sq", [P, 2, SEQ], F32)
        A0 = base[0]
        h32 = place("h32", [P, 2, SEQ], F32, A0 + 57344)
        silu_s = place("silu_s", [P, 2, SEQ], F32, A0 + 61440)
        hh = place("hh", [P, KMAX, SEQ], F32R, A0)
        hl = place("hl", [P, KMAX, SEQ], F32R, A0 + KMAX * 2048)
        t_buf = place("t_buf", [P, 4, SEQ], F32, A0 + 49152)
        ada0 = place("ada0", [P, 16, KD * P], F32, A0)
        oh = place("oh", [P, KD, SEQ], F32R, A0)
        ol = place("ol", [P, KD, SEQ], F32R, A0 + 16384)
        W0 = A0 + 32768
        bp = place("bp", [P, 8, SEQ], F32, W0)
        intra = place("intra", [P, TT, 4, P], F32, W0 + 16384)
        u_val = place("u_val", [P, TT, 4, HEAD], F32, W0 + 24576)
        wT = place("wT", [P, 2, SEQ], F32, A0)
        k_dec = place("k_dec", [P, TT, 4, HEAD], F32, A0 + 8192)
        st = place("st", [P, NCH + 1, 2, HEAD], F32, A0 + 12288)
        v_beta = place("v_beta", [P, 4, HEAD], F32, A0 + 17408)
        k_beta = place("k_beta", [P, 4, HEAD], F32, A0 + 18432)
        Tm = place("Tm", [P, 4, P], F32, A0 + 26624)
        Um = place("Um", [P, 4, P], F32, A0 + 28672)
        Ym = place("Ym", [P, 4, P], F32, A0 + 30720)
        cT = place("cT", [P, 4, P], F32, A0 + 20480)
        eg = place("eg", [P, 2, P], F32, A0 + 22528)
        pc = place("pc", [P, 6, SEQ], F32, W0)
        tails = [RAW0 + j * KMAX * 512 + 4096 for j in range(4)] + [WH0 + j * KMAX * 512 + 4096 for j in range(4)]
        ct = [place(f"ct{j}", [P, SEQ], F32, tails[j]) for j in range(6)]
        g_in = [[place(f"g_in{q}{b}", [P, SEQ], F32, tails[3 * q + b]) for b in range(3)] for q in range(2)]
        lT = [place("lT0", [P, 4, P], F32, A0 + 24576), place("lT1", [P, 4, P], F32, tails[6])]
        dcy = place("dcy", [P, 4, P], F32, tails[7])
        v_tok = place("v_tok", [P, TT, 2 * P], F32, W0 + 12288)
        sco = place("sco", [P, 8, 2 * P], F32, W0 + 16384)
        pT = place("pT", [P, TT, SEQ], F32, W0 + 24576)
        up_m = place("up_m", [P, 5, SEQ], F32, W0 + 12288)
        assert A0 + 65536 <= 229368, A0 + 65536

        PS = ctx.enter_context(nc.psum_tensor("PS", [P, 8, SEQ], F32))
        gates_dram = nc.dram_tensor("gates_dram", (24, P, SEQ), F32, kind="Internal").ap()

        def sig(name, per_layer=0, credit=0):
            return Signal(ctx.enter_context(nc.semaphore(name)), per_layer, credit)

        arrived = [sig(f"arrived{j}", 16 * UNITS // RAW) for j in range(RAW)]
        hi_ready = sig("hi_ready", UNITS, RAW)
        lo_ready = sig("lo_ready", UNITS, RAW)
        unit_done = sig("unit_done", UNITS, 2)
        consts_in = sig("consts_in")
        tables_in = sig("tables_in")
        cond_in = sig("cond_in")
        cond_done = sig("cond_done")
        layer_in = sig("layer_in", 16 * 5)
        x_in = sig("x_in")
        ada0_in = [sig(f"ada0_in{j}") for j in range(ADA_LOTS)]
        ada_in = [sig(f"ada_in{j}") for j in range(2)]
        ada_step = sig("ada_step")
        ada0_step = sig("ada0_step")
        ada_ready = sig("ada_ready")
        ada_gate_ready = sig("ada_gate_ready")
        gate_mods_done = sig("gate_mods_done", 3)
        mods_done = sig("mods_done", 3)
        bias_masked = sig("bias_masked", 1)
        norm_mm = sig("norm_mm", 3)
        rstd_mm = sig("rstd_mm", 3)
        root_done = sig("root_done", 3)
        rstd_done = sig("rstd_done", 3)
        t_done = sig("t_done", 24)
        uh_done = sig("uh_done", 24)
        ul_done = sig("ul_done", 24)
        silu_done = sig("silu_done", 44, 2)
        h_done = sig("h_done", 44, 2)
        hh_done = sig("hh_done", 44)
        hl_done = sig("hl_done", 44)
        x_done = sig("x_done", 40, 2)
        sq_done = sig("sq_done", 24)
        ssq_done = sig("ssq_done", 18)
        in_done = sig("in_done", 44, 4)
        ab_hi_done = sig("ab_hi_done", 1)
        ab_lo_done = sig("ab_lo_done", 1)
        ab_mm = sig("ab_mm", 1)
        ab_copied = sig("ab_copied", 1)
        ab_tr = sig("ab_tr", 1)
        gate_out = [sig(f"gate_out{j}", 16 * 12) for j in range(2)]
        gate_back = [sig(f"gate_back{j}", 16 * 3 * 4) for j in range(2)]
        conv_done = sig("conv_done", 6)
        conv_silu = sig("conv_silu", 6)
        conv_step = sig("conv_step", 18)
        l2_sq = sig("l2_sq", 4)
        l2_mm = sig("l2_mm", 4)
        l2_root = sig("l2_root", 4)
        l2_inv = sig("l2_inv", 4)
        qk_done = sig("qk_done", 4)
        ab_v = sig("ab_v", 7)
        ab_a = sig("ab_a", 7)
        gc_mm = sig("gc_mm", 1)
        gcb_mm = sig("gcb_mm", 4)
        bb_mm = sig("bb_mm", 4)
        kk_mm = sig("kk_mm", 4)
        tr_mm = sig("tr_mm", 4)
        diff_done = sig("diff_done", 4)
        decay_done = sig("decay_done", 4)
        eg_done = sig("eg_done", 4)
        mask_step = sig("mask_step", 16)
        lt_done = sig("lt_done", 4)
        tok_done = sig("tok_done", 4)
        qe_done = sig("qe_done", 4)
        ct_done = sig("ct_done", 24)
        u_done = sig("u_done", 24)
        tm_done = sig("tm_done", 20)
        y_mm = sig("y_mm", 24)
        y_done = sig("y_done", 20)
        z_mm = sig("z_mm", 20)
        uw_mm = sig("uw_mm", 4)
        uw_done = sig("uw_done", 4)
        settled = sig("settled")
        st_zero = sig("st_zero", 1)
        ws_mm = sig("ws_mm", 8)
        vnew_done = sig("vnew_done", 8)
        kv_mm = sig("kv_mm", 8)
        st_done = sig("st_done", 8)
        o_mm = sig("o_mm", 1)
        o_done = sig("o_done", 1)
        on_sq = sig("on_sq", 2)
        on_mm = sig("on_mm", 2)
        on_root = sig("on_root", 2)
        on_silu = sig("on_silu", 2)
        on_step = sig("on_step", 6)
        ob_hi = sig("ob_hi", 2)
        ob_lo = sig("ob_lo", 2)
        rot_mm = sig("rot_mm", 5)
        rot_step = sig("rot_step", 10)
        rope_done = sig("rope_done", 5)
        vt_mm = sig("vt_mm", 2)
        vt_done = sig("vt_done", 2)
        s_mm = sig("s_mm", 8)
        s_step = sig("s_step", 28)
        bias_done = sig("bias_done", 8)
        negmax_done = sig("negmax_done", 8)
        exp_done = sig("exp_done", 8)
        prob_done = sig("prob_done", 8)
        pt_mm = sig("pt_mm", 17)
        pt_done = sig("pt_done", 17)
        pv_mm = sig("pv_mm", 8)
        o_hi = sig("o_hi", 8)
        o_lo = sig("o_lo", 8)
        sig_done = sig("sig_done", 8)
        merge_step = sig("merge_step", 16)
        mg_used = sig("mg_used", 8, 2)
        mh_done = sig("mh_done", 8)
        ml_done = sig("ml_done", 8)
        out_ready = sig("out_ready")
        out_done = [sig(f"out_done{j}") for j in range(2)]

        block = ctx.enter_context(nc.Block())

        def out_index(l, sub, half, d):
            return (0, 16, 24)[sub] + (8 * half if sub != 1 else 0) + d

        @block.sync
        def _(e):
            e.dma_start(cond[:, :], a["c"].broadcast_to([P, KD * P])).then_inc(cond_in.sem, 16)

            def ada_lot(lot):
                for v in (lot, KD + lot):
                    e.dma_start(ada0[:, v, :], a["ada_w"][v]).then_inc(ada0_in[lot].sem, 16)
            ada_lot(0)
            ada_lot(1)
            e.dma_start(x[:, :, :], a["x"]).then_inc(x_in.sem, 16)
            for t, src in ((ident, "ident"), (ones_mean, "ones_mean"), (eps, "eps"), (final_g, "final_g"),
                           (ada_b, "ada_b")):
                e.dma_start(t[:, :], a[src]).then_inc(consts_in.sem, 16)
            e.dma_start(norm_g[:, :, :], a["norm_g"]).then_inc(consts_in.sem, 16)
            for lot in range(2, ADA_LOTS):
                ada_lot(lot)

            def load(l, m, j, src, K):
                n = l * UNITS + (4 * m + j + 1)
                e.wait_ge(hi_ready.sem, n)
                e.wait_ge(lo_ready.sem, n)
                e.dma_start(raw[:, j, 0:K * P], src).then_inc(arrived[j].sem, 16)

            with e.Fori(0, DEPTH) as l:
                def ffn(first, name):
                    m0 = first // RAW
                    for half, F in enumerate(F_HALF):
                        with e.Fori(0, F // 2) as i:
                            for j in range(4):
                                load(l, m0 + i, j, a[name + "_in"][l * 44 + F_HALF[0] * 2 * half + 4 * i + j], KD)
                        m0 += F // 2
                        with e.Fori(0, 2) as i:
                            for j in range(4):
                                load(l, m0 + i, j, a[f"{name}_out{half}"][l * 8 + 4 * i + j], F)
                        m0 += 2

                ffn(0, "ffn1")
                e.wait_ge(x_done.sem, x_done.at(l, 0))
                e.dma_start(ab_raw[:, :, :], a["w_ab"][l]).then_inc(layer_in.sem, 16)
                e.dma_start(a_bias[:, :, :], a["a_bias"][l]).then_inc(layer_in.sem, 16)
                e.dma_start(a_far[:, :], a["a_far"][l]).then_inc(layer_in.sem, 16)
                e.dma_start(conv_w[:, :, :], a["conv_w"][l]).then_inc(layer_in.sem, 16)
                e.dma_start(small[:, :], a["small"][l]).then_inc(layer_in.sem, 16)
                with e.Fori(0, 11) as i:
                    for j in range(4):
                        load(l, MIX // RAW + i, j, a["mix_in"][l * 44 + 4 * i + j], KD)
                with e.Fori(0, 2) as i:
                    for j in range(4):
                        load(l, U_UP // RAW + i, j, a["mix_up"][l * 8 + 4 * i + j], KD)
                with e.Fori(0, 2) as i:
                    for j in range(4):
                        load(l, U_OUT // RAW + i, j, a["mix_out"][l * 8 + 4 * i + j], KD)
                ffn(2 * SUB, "ffn2")
            for d in range(KD):
                e.wait_ge(out_ready.sem, d + 1)
                e.dma_start(out[:, d, :], sq[:, d % 2, :]).then_inc(out_done[d % 2].sem, 16)
            for j in range(2):
                e.wait_ge(out_done[j].sem, 16 * KD // 2)

        @block.gpsimd
        def _(e):
            for d in range(1, KD - 1):
                e.wait_ge(sq_done.sem, d + 1)
                if d >= 2:
                    e.wait_ge(ssq_done.sem, d - 1)
                e.tensor_tensor(ssq[:, :], ssq[:, :], sq[:, d % 2, :], ALU.add).then_inc(ssq_done.sem, 1)
            for lot in range(ADA_LOTS):
                e.wait_ge(ada0_in[lot].sem, 32)

            def load_unit(n, u, j):
                if not isinstance(n, int) or n >= 2:
                    e.wait_ge(ada_step.sem, ADA_STEPS * (n - 1))
                e.dma_start(ada_raw[:, j, :], a["ada_w"][u]).then_inc(ada_in[j].sem, 16)

            def sum_unit(n, n_in, v, b, j, ready):
                e.wait_ge(ada_in[j].sem, n_in)
                r = ada_raw[:, j, :]
                e.tensor_tensor(r, r, cond[:, :], ALU.mult).then_inc(ada_step.sem, 1)
                for h in range(1, ADA_STEPS - 1):
                    w = KD * P >> h
                    e.wait_ge(ada_step.sem, n * ADA_STEPS + h)
                    e.tensor_tensor(r[:, 0:w], r[:, 0:w], r[:, w:2 * w], ALU.add).then_inc(ada_step.sem, 1)
                e.wait_ge(ada_step.sem, n * ADA_STEPS + (ADA_STEPS - 1))
                e.tensor_tensor(ada_sum[:, v], r[:, 0:1], ada_b[:, b], ALU.add).then_inc(ada_step.sem, 1)
                e.wait_ge(ada_step.sem, n * ADA_STEPS + ADA_STEPS)
                e.sem_inc(ready.sem, 1)

            load_unit(0, 16, 0)
            load_unit(1, 17, 1)
            for t, src in ((tri, "tri"), (same_chunk, "same_chunk"), (strict, "strict"), (rot, "rot"), (cos, "cos"),
                           (sin, "sin"), (c_mask, "c_mask"), (a_mask, "a_mask")):
                e.dma_start(t[:, :], a[src]).then_inc(tables_in.sem, 16)
            e.dma_start(level_mask[:, :, :], a["level_mask"]).then_inc(tables_in.sem, 16)
            e.wait_ge(cond_done.sem, 1)
            e.wait_ge(consts_in.sem, 16 * 6)
            for n in range(8):
                v = slice(16 + n, 17 + n)
                sum_unit(n, 16 * (n // 2 + 1), v, v, n % 2, ada_gate_ready)
                if n + 2 < 8:
                    load_unit(n + 2, 18 + n, n % 2)

            with e.Fori(0, 3 * DEPTH - 1) as g:
                for first, last, ready, used in ((0, 8, ada_ready, ul_done), (8, 12, ada_gate_ready, gate_mods_done)):
                    with e.Fori(first, last) as i:
                        for j in range(2):
                            e.wait_ge(unit_done.sem, g * SUB + 4 * i + (2 * j + 3))
                            load_unit(g * 24 + 2 * i + (8 + j), g * 24 + 2 * i + (24 + j), j)
                        e.wait_ge(used.sem, g * (8 if used is ul_done else 1) + (8 if used is ul_done else 1))
                        for j in range(2):
                            sum_unit(g * 24 + 2 * i + (8 + j), g * 192 + 16 * i + 80, bass.ds(2 * i + j, 1),
                                     bass.ds(g * 24 + 2 * i + (24 + j), 1), j, ready)

        @block.tensor
        def _(e):
            e.wait_ge(consts_in.sem, 16 * 6)

            def unit(l, n, j, K, bank, xh, xl, waits=None, ks=None):
                ks = range(K) if ks is None else ks
                if ks[0] == 0:
                    e.wait_ge(lo_ready.sem, n + (1 + RAW))
                for k in ks:
                    if waits is not None:
                        waits(k)
                    for w, v in ((wh, xh), (wh, xl), (wl, xh)):
                        mm = e.matmul(PS[:, bank, :], w[:, j % 2, k * P:(k + 1) * P], v[:, k, :],
                                      start=(k == 0 and w is wh and v is xh), stop=(k == K - 1 and w is wl))
                if ks[-1] == K - 1:
                    mm.then_inc(unit_done.sem, 1)

            def first_pair(l, n, banks, there):
                e.wait_ge(lo_ready.sem, n + (2 + RAW))
                for k in range(KD):
                    there(k)
                    for j in range(2):
                        for w, v in ((wh, uh), (wh, ul), (wl, uh)):
                            mm = e.matmul(PS[:, banks[j], :], w[:, j, k * P:(k + 1) * P], v[:, k, :],
                                          start=(k == 0 and w is wh and v is uh), stop=(k == KD - 1 and w is wl))
                        if k == KD - 1:
                            mm.then_inc(unit_done.sem, 1)

            def settle():
                e.sem_inc(settled.sem, 1)

            def norm(l, s):
                e.wait_ge(ssq_done.sem, ssq_done.at(l, 6 * (s + 1)))
                for t in range(TT):
                    e.matmul(PS[:, 6, t:t + 1], ssq[:, t * P:(t + 1) * P], ones_mean[:, 0:1],
                             start=t == 0, stop=False)
                e.wait_ge(sq_done.sem, sq_done.at(l, 8 * (s + 1)))
                for t in range(TT):
                    mm = e.matmul(PS[:, 6, t:t + 1], sq[:, 1, t * P:(t + 1) * P], ones_mean[:, 0:1],
                                  start=False, stop=t == TT - 1)
                mm.then_inc(norm_mm.sem, 1)
                e.wait_ge(rstd_done.sem, rstd_done.at(l, s + 1))
                for t in range(TT):
                    mm = e.matmul(PS[:, 6, t * P:(t + 1) * P], rstd_tok[:, t:t + 1].broadcast_to([P, P]), ident[:, :],
                                  start=True, stop=True)
                mm.then_inc(rstd_mm.sem, 1)

            def ffn(l, s, first):
                base_f = 22 * (s // 2)
                n0 = first
                for half, F in enumerate(F_HALF):
                    def in_unit(i, j):
                        n = l * UNITS + 4 * i + (n0 + j)
                        f = l * 44 + 2 * i + (base_f + F_HALF[0] * half + j // 2)
                        e.wait_ge((h_done if j % 2 else silu_done).sem, f + 1)
                        unit(l, n, j, KD, (0, 2, 1, 3)[j], uh, ul)

                    if half == 0:
                        e.wait_ge(h_done.sem, h_done.at(l, base_f - 1))
                        first_pair(l, l * UNITS + n0, (0, 2),
                                   lambda k: e.wait_ge(ul_done.sem, ul_done.at(l, 8 * s + k + 1)))
                        in_unit(0, 2)
                        in_unit(0, 3)
                    with e.Fori(1 - half, F // 2) as i:
                        for j in range(4):
                            in_unit(i, j)
                    n0 += 2 * F
                    fs = base_f + (F_HALF[0] if half == 0 else 22)
                    with e.Fori(0, 2) as i:
                        for j in range(4):
                            n = l * UNITS + 4 * i + (n0 + j)
                            e.wait_ge(x_done.sem, l * 40 + 4 * i + (out_index(l, s, half, j) + 1))

                            def h_there(k):
                                if k >= F - 2:
                                    e.wait_ge(hl_done.sem, hl_done.at(l, fs - (F - 1 - k)))
                            unit(l, n, j, F, 4 + j % 2, hh, hl, h_there if j == 0 else None)
                    n0 += 8

            def mixing(l):
                def proj(m):
                    e.wait_ge(in_done.sem, l * 44 + (m + 1))
                    unit(l, l * UNITS + (MIX + m), m, KD, m % 4, uh, ul)

                at_quarter = [0]

                def gates(quarters):
                    for _ in range(quarters):
                        g, part = divmod(at_quarter[0], 4)
                        at_quarter[0] += 1
                        m = gate_unit(g)
                        if part == 0:
                            e.wait_ge(in_done.sem, in_done.at(l, m if g >= 17 else m - 1))
                        unit(l, l * UNITS + (MIX + m), m, KD, g % 2 if g < 17 else 7, uh, ul,
                             ks=range(2 * part, 2 * part + 2))

                def proj_a(i):
                    e.wait_ge(in_done.sem, in_done.at(l, M_A + i))
                    unit(l, l * UNITS + (MIX + M_A + i), M_A + i, KD, 7, uh, ul)

                e.wait_ge(in_done.sem, l * 44 + 2)
                first_pair(l, l * UNITS + MIX, (0, 1), lambda k: e.wait_ge(ul_done.sem, ul_done.at(l, 8 + k + 1)))
                for m in range(2, 9):
                    proj(m)
                e.wait_ge(ab_lo_done.sem, ab_lo_done.at(l, 1))
                for k in range(KD):
                    for v, w in ((uh, ab_hi), (ul, ab_hi), (uh, ab_lo)):
                        mm = e.matmul(PS[0:8, 6, :], w[:, k, :], v[:, k, :],
                                      start=(k == 0 and v is uh and w is ab_hi), stop=(k == KD - 1 and w is ab_lo))
                mm.then_inc(ab_mm.sem, 1)
                for i in range(4):
                    proj(9 + i)
                    if i == 0:
                        e.wait_ge(tables_in.sem, 16 * 9)
                        e.wait_ge(ab_copied.sem, ab_copied.at(l, 1))
                        for t in range(TT):
                            mm = e.transpose(PS[:, 6, 8 * t:8 * t + 8], ab_T[:, t * P:(t + 1) * P], ident[0:8, 0:8])
                        mm.then_inc(ab_tr.sem, 1)
                    e.wait_ge(l2_sq.sem, l2_sq.at(l, i + 1))
                    if i >= 2:
                        e.wait_ge(l2_root.sem, l2_root.at(l, i - 1))
                    e.matmul(PS[:, 4 + i % 2, :], same_chunk[:, :], sq[:, i % 2, :], start=True, stop=True)\
                        .then_inc(l2_mm.sem, 1)
                proj(13)
                e.wait_ge(ab_v.sem, ab_v.at(l, 4))
                e.matmul(PS[:, 6, 32:48], tri[:, :], sc[:, 0:16], start=True, stop=True)
                e.matmul(PS[:, 6, 48:64], same_chunk[:, :], sc[:, 0:16], start=True, stop=True).then_inc(gc_mm.sem, 1)
                e.wait_ge(qk_done.sem, qk_done.at(l, 4))
                e.wait_ge(conv_silu.sem, conv_silu.at(l, 6))
                e.wait_ge(in_done.sem, in_done.at(l, 14))
                e.wait_ge(ab_a.sem, ab_a.at(l, 5))
                e.wait_ge(ab_v.sem, ab_v.at(l, 5))

                def run_decay(t):
                    if t:
                        e.wait_ge(tok_done.sem, tok_done.at(l, t))
                    for s in range(4):
                        mm = e.matmul(PS[:, 4 if t else 5, s * P:(s + 1) * P],
                                      sc[:, 4 * t + s:4 * t + s + 1].broadcast_to([P, P]), tri[:, :], start=True, stop=True)
                    mm.then_inc(gcb_mm.sem, 1)

                def beta_and_products(t):
                    if t:
                        e.wait_ge(diff_done.sem, diff_done.at(l, t + 1))
                        e.wait_ge(eg_done.sem, eg_done.at(l, t + 1))
                        e.wait_ge(rope_done.sem, rope_done.at(l, t))
                    for s in range(4):
                        mm = e.matmul(PS[:, 4 if t else 6, s * P:(s + 1) * P],
                                      sc[:, 16 + 4 * t + s:17 + 4 * t + s].broadcast_to([P, P]), ident[:, :],
                                      start=True, stop=True)
                    mm.then_inc(bb_mm.sem, 1)
                    c0, c1 = t * P, (t + 1) * P
                    for par in range(2):
                        r = slice(64 * par, 64 * par + 64)
                        for x2 in range(2):
                            for pair in range(2):
                                rhs = bp[r, (2 if x2 == 0 else 0) + pair, c0:c1]
                                mm = e.matmul(PS[:, 2 + par, (2 * x2 + pair) * P:(2 * x2 + pair + 1) * P],
                                              bp[r, 2 + pair, c0:c1], rhs, start=True, stop=True)
                    mm.then_inc(kk_mm.sem, 1)

                def by_token(t):
                    if t:
                        e.wait_ge(lt_done.sem, lt_done.at(l, t + 1))
                    for y in range(4):
                        mm = e.transpose(PS[:, 4, y * P:(y + 1) * P], bp[:, 2 + y, t * P:(t + 1) * P], ident[:, :])
                    mm.then_inc(tr_mm.sem, 1)

                def rotate(i):
                    e.matmul(PS[:, 2 + i // 4, :], rot[:, :], ct[i][:, :], start=True, stop=True).then_inc(rot_mm.sem, 1)

                run_decay(0)
                beta_and_products(0)
                by_token(0)
                gates(4)
                for t in range(TT):
                    for lv in range(LEVELS):
                        g = 6 * t + lv
                        e.wait_ge(ct_done.sem, ct_done.at(l, g + 1))
                        if lv == 0:
                            if t:
                                e.wait_ge(tm_done.sem, tm_done.at(l, 5 * t))
                            for s in range(4):
                                mm = e.transpose(PS[:, 7, s * P:(s + 1) * P], cT[:, s, :], ident[:, :])
                            mm.then_inc(y_mm.sem, 1)
                        else:
                            if lv == 1:
                                if t:
                                    e.wait_ge(uw_done.sem, uw_done.at(l, t))
                                else:
                                    e.wait_ge(eg_done.sem, eg_done.at(l, 1))
                            e.wait_ge(tm_done.sem, tm_done.at(l, 5 * t + lv))
                            for s in range(4):
                                mm = e.matmul(PS[:, 5, s * P:(s + 1) * P], cT[:, s, :], Tm[:, s, :], start=True, stop=True)
                            mm.then_inc(y_mm.sem, 1)
                        if lv == 1:
                            rotate(t)
                            if t + 1 < TT:
                                run_decay(t + 1)
                        gates(1)
                        if lv > 0:
                            e.wait_ge(y_done.sem, y_done.at(l, 5 * t + lv))
                            e.wait_ge(u_done.sem, u_done.at(l, g))
                            for s in range(4):
                                mm = e.matmul(PS[:, 6, s * P:(s + 1) * P], Ym[:, s, :], Um[:, s, :], start=True, stop=True)
                            if lv < LEVELS - 1:
                                for s in range(4):
                                    mm = e.matmul(PS[:, 7, s * P:(s + 1) * P], Um[:, s, :], Ym[:, s, :], start=True, stop=True)
                            mm.then_inc(z_mm.sem, 1)
                        if lv == 3 and t + 1 < TT:
                            beta_and_products(t + 1)
                        if lv == 3 and t + 1 == TT:
                            rotate(4)
                        if lv == 5 and t + 1 < TT:
                            by_token(t + 1)
                        gates(1)
                    e.wait_ge(u_done.sem, u_done.at(l, 6 * (t + 1)))
                    e.wait_ge(tok_done.sem, tok_done.at(l, t + 1))
                    for s in range(4):
                        e.matmul(PS[:, 5, s * HEAD:(s + 1) * HEAD], Um[:, s, :], v_beta[:, s, :], start=True, stop=True)
                    for s in range(4):
                        par, pair = s // 2, s % 2
                        mm = e.matmul(PS[64 * par:64 * par + 64, 5, 256 + pair * P:256 + (pair + 1) * P],
                                      k_beta[:, s, :], Um[:, s, :], start=True, stop=True)
                    mm.then_inc(uw_mm.sem, 1)
                e.wait_ge(st_zero.sem, st_zero.at(l, 1))
                e.wait_ge(rope_done.sem, rope_done.at(l, 5))
                e.wait_ge(uw_done.sem, uw_done.at(l, TT))
                for n in range(NCH):
                    t, pb = n // 2, 64 * (n % 2)
                    if n >= 1:
                        e.wait_ge(st_done.sem, st_done.at(l, n))
                    settle()
                    for s in range(4):
                        par, pair = s // 2, s % 2
                        r = slice(64 * par, 64 * par + 64)
                        mm = e.matmul(PS[pb:pb + 64, 2 + par, pair * HEAD:(pair + 1) * HEAD],
                                      wT[r, pair, n * CHUNK:(n + 1) * CHUNK], st[r, n, pair, :], start=True, stop=True)
                    mm.then_inc(ws_mm.sem, 1)
                    gates(1)
                    e.wait_ge(vnew_done.sem, vnew_done.at(l, n + 1))
                    settle()
                    for s in range(4):
                        par, pair = s // 2, s % 2
                        mm = e.matmul(PS[64 * par:64 * par + 64, 4 + n % 2, pair * HEAD:(pair + 1) * HEAD],
                                      k_dec[pb:pb + 64, t, s, :], u_val[pb:pb + 64, t, s, :], start=True, stop=True)
                    mm.then_inc(kv_mm.sem, 1)
                    gates(1)
                e.wait_ge(qe_done.sem, qe_done.at(l, TT))
                for t in range(TT):
                    for s in range(4):
                        par, pair = s // 2, s % 2
                        r = slice(64 * par, 64 * par + 64)
                        e.matmul(PS[r, 6 + pair, t * P:(t + 1) * P], u_val[:, t, s, :], intra[:, t, s, :],
                                 start=True, stop=True)
                        for ch in range(2):
                            n = 2 * t + ch
                            mm = e.matmul(PS[r, 6 + pair, n * CHUNK:(n + 1) * CHUNK], st[r, n, pair, :],
                                          bp[r, pair, n * CHUNK:(n + 1) * CHUNK], start=False, stop=True,
                                          skip_group_check=True)
                mm.then_inc(o_mm.sem, 1)

                def scores_c(t):
                    lo = 0 if t else P
                    for h in range(8):
                        r = slice(64 * (h // 4), 64 * (h // 4) + 64)
                        k0 = (t - 1) * P + lo
                        mm = e.matmul(PS[:, h // 2, (h % 2) * 256 + lo:(h % 2) * 256 + 256],
                                      ct[h % 4][r, t * P:(t + 1) * P], ct[4][r, k0:(t + 1) * P], start=True, stop=True)
                    mm.then_inc(s_mm.sem, 1)

                e.wait_ge(in_done.sem, in_done.at(l, M_A))
                scores_c(0)
                e.wait_ge(st_done.sem, st_done.at(l, NCH))
                for i in range(2):
                    e.wait_ge(on_sq.sem, on_sq.at(l, i + 1))
                    e.matmul(PS[:, 4 + i, :], same_chunk[:, :], sq[:, i, :], start=True, stop=True)\
                        .then_inc(on_mm.sem, 1)
                for t in range(TT):
                    mm = e.transpose(PS[:, 6, t * P:(t + 1) * P], ct[5][:, t * P:(t + 1) * P], ident[:, :])
                mm.then_inc(vt_mm.sem, 1)
                proj_a(0)
                for t in range(TT):
                    if t == TT - 1:
                        gates(4)
                    else:
                        proj_a((1, 2, 4)[t])
                        e.wait_ge(bias_done.sem, bias_done.at(l, t + 1))
                        scores_c(t + 1)
                    if t in (1, 2):
                        proj_a((3, 5)[t - 1])
                    elif t == TT - 1:
                        gates(4)
                    if t == 0:
                        e.wait_ge(on_root.sem, on_root.at(l, 2))
                    e.wait_ge(prob_done.sem, prob_done.at(l, t + 1))
                    n_pt = 2 * t - 1 if t else 0
                    kts = (0, 1) if t else (1,)
                    for z, kt in enumerate(kts):
                        if n_pt + z >= 1:
                            e.wait_ge(pt_done.sem, pt_done.at(l, n_pt + z))
                        for h in range(8):
                            mm = e.transpose(PS[:, 4 + h // 4, (h % 4) * P:(h % 4 + 1) * P],
                                             sco[:, h, kt * P:(kt + 1) * P], ident[:, :])
                        mm.then_inc(pt_mm.sem, 1)
                    e.wait_ge(vt_done.sem, vt_done.at(l, 1))
                    e.wait_ge(pt_done.sem, pt_done.at(l, n_pt + len(kts)))
                    if t >= 1:
                        e.wait_ge(o_lo.sem, o_lo.at(l, t))
                    for kv in range(2):
                        for z, kt in enumerate(kts):
                            mm = e.matmul(PS[64 * kv:64 * kv + 64, 6, :], v_tok[:, t - 1 + kt, 64 * kv:64 * kv + 64],
                                          pT[:, 2 * kt + kv, :], start=(z == 0), stop=(z == len(kts) - 1))
                    mm.then_inc(pv_mm.sem, 1)

                def scores_a(t):
                    for h in range(4):
                        r = slice(64 * (h % 2), 64 * (h % 2) + 64)
                        mm = e.matmul(PS[:, h, 0:(t + 1) * P], pc[r, h // 2, t * P:(t + 1) * P],
                                      pc[r, 2 + h // 2, 0:(t + 1) * P], start=True, stop=True)
                    mm.then_inc(s_mm.sem, 1)

                e.wait_ge(bias_done.sem, bias_done.at(l, TT))
                e.wait_ge(in_done.sem, in_done.at(l, gate_unit(19)))
                scores_a(0)
                e.wait_ge(o_lo.sem, o_lo.at(l, 4))
                for y in range(2):
                    for t in range(TT):
                        mm = e.transpose(PS[:, 6 + y, t * P:(t + 1) * P], pc[:, 4 + y, t * P:(t + 1) * P], ident[:, :])
                mm.then_inc(vt_mm.sem, 1)
                e.wait_ge(vt_done.sem, vt_done.at(l, 2))
                for t in range(TT):
                    gates(4)
                    if t + 1 < TT:
                        e.wait_ge(bias_done.sem, bias_done.at(l, 4 + t + 1))
                        scores_a(t + 1)
                    else:
                        gates(4)
                    e.wait_ge(prob_done.sem, prob_done.at(l, 4 + t + 1))
                    n_pt = 7 + t * (t + 1) // 2
                    for kt in range(t + 1):
                        e.wait_ge(pt_done.sem, pt_done.at(l, n_pt + max(kt - 1, 0)))
                        for h in range(4):
                            sh = sco[:, 2 * h:2 * h + 2, :].rearrange("p a n -> p (a n)")
                            mm = e.transpose(PS[:, 4 + kt % 2, h * P:(h + 1) * P], sh[:, kt * P:(kt + 1) * P], ident[:, :])
                        mm.then_inc(pt_mm.sem, 1)
                    e.wait_ge(pt_done.sem, pt_done.at(l, n_pt + t + 1))
                    if t >= 1:
                        e.wait_ge(o_lo.sem, o_lo.at(l, 4 + t))
                    for h in range(4):
                        r = slice(64 * (h % 2), 64 * (h % 2) + 64)
                        for kt in range(t + 1):
                            mm = e.matmul(PS[r, 6, (h // 2) * P:(h // 2 + 1) * P], v_tok[:, kt, h * HEAD:(h + 1) * HEAD],
                                          pT[:, kt, h * P:(h + 1) * P], start=(kt == 0), stop=(kt == t))
                    mm.then_inc(pv_mm.sem, 1)
                assert at_quarter[0] == 4 * 24

                e.wait_ge(o_lo.sem, o_lo.at(l, 8))
                e.wait_ge(in_done.sem, in_done.at(l, M_IN))
                for d in range(KD):
                    n = l * UNITS + (U_UP + d)
                    e.wait_ge(mg_used.sem, l * 8 + (d + 1))
                    e.wait_ge(lo_ready.sem, n + (1 + RAW))
                    for b, ks in enumerate((range(0, 2), range(2, 4), range(4, 8))):
                        for k in ks:
                            for w, v in ((wh, oh), (wh, ol), (wl, oh)):
                                mm = e.matmul(PS[:, 3 * (d % 2) + b, :], w[:, d % 2, k * P:(k + 1) * P], v[:, k, :],
                                              start=(k == ks[0] and w is wh and v is oh),
                                              stop=(k == ks[-1] and w is wl))
                    mm.then_inc(unit_done.sem, 1)
                with e.Fori(0, 2) as i:
                    for j in range(4):
                        n = l * UNITS + 4 * i + (U_OUT + j)
                        e.wait_ge(x_done.sem, l * 40 + 4 * i + (out_index(l, 1, 0, j) + 1))

                        def m_there(k):
                            e.wait_ge(ml_done.sem, ml_done.at(l, k + 1))
                        unit(l, n, j, KD, 6 + j % 2, uh, ul, m_there if j == 0 else None)

            with e.Fori(0, DEPTH) as l:
                norm(l, 0)
                ffn(l, 0, 0)
                norm(l, 1)
                mixing(l)
                norm(l, 2)
                ffn(l, 2, 2 * SUB)
            norm(DEPTH, 0)

        def steps(e, l, first, count, K, nxt, split, use, but_last=False):
            bodies, m0 = count // 4, first // 4

            def body(i, last):
                for j in range(4):
                    if last and but_last and j == 3:
                        pass
                    elif j < 2:
                        split(l, m0, i, j + 2, K)
                    elif not last:
                        split(l, m0 + 1, i, j - 2, K)
                    elif nxt is not None:
                        split(l, m0 + 1, i, j - 2, nxt)
                    use(i, j)
            if bodies > 2:
                with e.Fori(0, bodies - 1) as i:
                    body(i, False)
            else:
                body(0, False)
            body(bodies - 1, True)

        @block.scalar
        def _(e):
            def split(l, m0, i, j, K):
                e.wait_ge(arrived[j].sem, l * (16 * UNITS // RAW) + 16 * i + 16 * (m0 + 1))
                e.wait_ge(unit_done.sem, l * UNITS + 4 * i + (4 * m0 + j + 1))
                e.activation(wh[:, j % 2, 0:K * P], raw[:, j, 0:K * P], ACT.Copy).then_inc(hi_ready.sem, 1)

            def multiplied(l, n, i=0):
                e.wait_ge(unit_done.sem, l * UNITS + 4 * i + (n + 3))

            def square(l, s, d):
                if d >= 3:
                    e.wait_ge(ssq_done.sem, ssq_done.at(l, 6 * (s + 1) + d - 2))
                e.activation(ssq[:, :] if d == 0 else sq[:, d % 2, :], x[:, d, :], ACT.Square).then_inc(sq_done.sem, 1)

            def splits(l, s, n):
                if s == 0:
                    split(l, n // 4, 0, 0, KD)
                split(l, n // 4, 0, 1, KD)

            def root(l, s):
                e.wait_ge(norm_mm.sem, norm_mm.at(l, s + 1))
                e.activation(root_tok[:, :], PS[:, 6, 0:TT], ACT.Sqrt, bias=eps[:, 0:1]).then_inc(root_done.sem, 1)

            def norm(l, s, n):
                root(l, s)
                splits(l, s, n)
                e.wait_ge(mods_done.sem, mods_done.at(l, s + 1))
                for k in range(KD):
                    e.wait_ge(t_done.sem, t_done.at(l, 8 * s + k + 1))
                    e.activation(uh[:, k, :], t_buf[:, k % 4, :], ACT.Identity, bias=ada_sum[:, k:k + 1])\
                        .then_inc(uh_done.sem, 1)

            def ffn(l, s, first, last):
                base_f = 22 * (s // 2)
                for half, F in enumerate(F_HALF):
                    f0 = base_f + F_HALF[0] * half

                    def use_in(i, j):
                        multiplied(l, first + j, i)
                        f = l * 44 + 2 * i + (f0 + j // 2)
                        if j % 2 == 0:
                            e.wait_ge(h_done.sem, f + 1)
                            e.activation(silu_s[:, j // 2, :], PS[:, j // 2, :], ACT.Silu).then_inc(silu_done.sem, 1)
                        else:
                            e.wait_ge(h_done.sem, f + 3)
                            dst = hh[:, bass.ds(2 * i + j // 2, 1), :].rearrange("p a n -> p (a n)")
                            e.activation(dst, h32[:, j // 2, :], ACT.Copy).then_inc(hh_done.sem, 1)

                    steps(e, l, first, 2 * F, KD, F, split, use_in)
                    first += 2 * F

                    def use_out(i, j):
                        if half == 1:
                            d = 4 * i + j
                            if d == 1:
                                e.activation(warm[:, 0:1], eps[:, 0:1], ACT.Sqrt)
                            e.wait_ge(x_done.sem, x_done.at(l, out_index(l, s, half, d) + 1))
                            square(l, s, d)
                    steps(e, l, first, 8, F, KD if half == 0 or not last else None, split, use_out, half == 1)
                    first += 8

            def mixing(l):
                e.wait_ge(layer_in.sem, layer_in.at(l, 80))
                e.activation(ab_hi[:, :, :], ab_raw[:, :, :], ACT.Copy).then_inc(ab_hi_done.sem, 1)

                def ahead(n):
                    split(l, (n + 2) // 4, 0, (n + 2) % 4, KD)

                def project(m, dst, bank):
                    ahead(MIX + m)
                    multiplied(l, MIX + m)
                    e.activation(dst, PS[:, bank, :], ACT.Copy).then_inc(in_done.sem, 1)

                def project_a(i):
                    project(M_A + i, pc[:, i, :], 7)

                def gate_step(g):
                    m = gate_unit(g)
                    ahead(MIX + m)
                    multiplied(l, MIX + m)
                    if g >= 2:
                        e.wait_ge(gate_out[g % 2].sem, gate_out[g % 2].at(l, 16 * (g // 2)))
                    hold = (gate_hold, ssq)[g % 2]
                    e.activation(hold[:, :], PS[:, g % 2 if g < 17 else 7, :], ACT.Copy).then_inc(in_done.sem, 1)
                    e.wait_ge(in_done.sem, in_done.at(l, m + 1))
                    e.dma_start(gates_dram[g], hold[:, :]).then_inc(gate_out[g % 2].sem, 16)

                def ab_nonlinear():
                    e.wait_ge(ab_v.sem, ab_v.at(l, 2))
                    e.activation(sc[:, 80:96], sc[:, 64:80], ACT.Abs).then_inc(ab_a.sem, 1)
                    e.wait_ge(ab_a.sem, ab_a.at(l, 1))
                    e.activation(sc[:, 96:112], sc[:, 80:96], ACT.Exp, scale=-1.0).then_inc(ab_a.sem, 1)
                    e.activation(sc[:, 224:228], small[:, 4:8], ACT.Exp).then_inc(ab_a.sem, 1)
                    e.wait_ge(ab_a.sem, ab_a.at(l, 2))
                    e.activation(sc[:, 112:128], sc[:, 96:112], ACT.Ln, bias=eps[:, 1:2]).then_inc(ab_a.sem, 1)
                    e.activation(sc[:, 16:32].rearrange("p (t s) -> p t s", t=TT),
                                 sc[:, 32:64].rearrange("p (t s) -> p t s", t=TT)[:, :, 4:8], ACT.Sigmoid)\
                        .then_inc(ab_a.sem, 1)

                for m in range(14):
                    if m == 13:
                        ab_nonlinear()
                    project(m, bp[:, m, :] if m < M_C else ct[m - M_C][:, :], m % 4)
                    if 1 <= m <= 6:
                        e.wait_ge(conv_done.sem, conv_done.at(l, m))
                        e.activation(bp[:, m - 1, :], t_buf[:, (m - 1) % 2, :], ACT.Silu).then_inc(conv_silu.sem, 1)
                    if 8 <= m <= 11:
                        i = m - 8
                        e.wait_ge(conv_silu.sem, conv_silu.at(l, i + 1))
                        if i >= 2:
                            e.wait_ge(l2_mm.sem, l2_mm.at(l, i - 1))
                        e.activation(sq[:, i % 2, :], bp[:, i, :], ACT.Square).then_inc(l2_sq.sem, 1)
                    if 9 <= m <= 12:
                        i = m - 9
                        if i >= 2:
                            e.wait_ge(qk_done.sem, qk_done.at(l, i - 1))
                        e.wait_ge(l2_mm.sem, l2_mm.at(l, i + 1))
                        e.activation(h32[:, i % 2, :], PS[:, 4 + i % 2, :], ACT.Sqrt, bias=eps[:, 0:1])\
                            .then_inc(l2_root.sem, 1)
                e.wait_ge(ab_v.sem, ab_v.at(l, 6))
                e.activation(sc[:, 176:192], sc[:, 128:144], ACT.Exp).then_inc(ab_a.sem, 1)
                e.activation(sc[:, 160:176], sc[:, 208:224], ACT.Exp).then_inc(ab_a.sem, 1)

                def decays(t):
                    e.wait_ge(diff_done.sem, diff_done.at(l, t + 1))
                    if t >= 1:
                        e.wait_ge(lt_done.sem, lt_done.at(l, t))
                        e.wait_ge(qe_done.sem, qe_done.at(l, t))
                    e.activation(dcy[:, :, :], lT[t % 2][:, :, :], ACT.Exp).then_inc(decay_done.sem, 1)
                    for par in range(2):
                        r = slice(64 * par, 64 * par + 64)
                        last = e.activation(eg[r, :, :], PS[r, 4 if t else 5, par * 256:par * 256 + 256]
                                            .rearrange("p (a n) -> p a n", a=2), ACT.Exp)
                    last.then_inc(eg_done.sem, 1)

                decays(0)
                gate_step(0)
                for t in range(TT):
                    for lv in range(LEVELS):
                        g = 6 * t + lv
                        if lv >= 1:
                            e.wait_ge(y_mm.sem, y_mm.at(l, g + 1))
                            e.activation(Ym[:, :, :], PS[:, 5, :].rearrange("p (s n) -> p s n", s=4), ACT.Copy)\
                                .then_inc(y_done.sem, 1)
                        if g % 2 == 0 and g >= 2:
                            gate_step(g // 2)
                        if lv == 3 and t + 1 < TT:
                            decays(t + 1)
                    e.wait_ge(uw_mm.sem, uw_mm.at(l, t + 1))
                    e.activation(u_val[:, t, :, :], PS[:, 5, 0:256].rearrange("p (s n) -> p s n", s=4), ACT.Copy)
                    e.activation(wT[:, :, t * P:(t + 1) * P], PS[:, 5, 256:512].rearrange("p (a n) -> p a n", a=2),
                                 ACT.Copy).then_inc(uw_done.sem, 1)
                for g in range(12, 17):
                    gate_step(g)
                e.wait_ge(o_mm.sem, o_mm.at(l, 1))
                e.activation(bp[:, 4:6, :], PS[:, 6:8, :], ACT.Copy).then_inc(o_done.sem, 1)
                e.wait_ge(o_done.sem, o_done.at(l, 1))
                for i in range(2):
                    e.activation(sq[:, i, :], bp[:, 4 + i, :], ACT.Square).then_inc(on_sq.sem, 1)
                for i in range(2):
                    e.wait_ge(on_mm.sem, on_mm.at(l, i + 1))
                    e.activation(h32[:, i, :], PS[:, 4 + i, :], ACT.Sqrt, scale=1.0 / HEAD, bias=eps[:, 0:1])\
                        .then_inc(on_root.sem, 1)
                for i in range(2):
                    e.activation(bp[:, 6 + i, :], bp[:, 6 + i, :], ACT.Silu).then_inc(on_silu.sem, 1)
                for i in range(2):
                    e.wait_ge(on_step.sem, on_step.at(l, 3 * (i + 1)))
                    e.activation(oh[:, 2 + i, :], bp[:, 4 + i, :], ACT.Copy).then_inc(ob_hi.sem, 1)

                def probs_T(n, banks, dst):
                    e.wait_ge(pt_mm.sem, pt_mm.at(l, n + 1))
                    e.activation(dst, banks, ACT.Copy).then_inc(pt_done.sem, 1)

                e.wait_ge(vt_mm.sem, vt_mm.at(l, 1))
                e.activation(v_tok[:, :, 0:P], PS[:, 6, :].rearrange("p (t n) -> p t n", t=TT), ACT.Copy)\
                    .then_inc(vt_done.sem, 1)
                n = 0
                project_a(0)
                for t in range(TT):
                    lo = 0 if t else P
                    if t == 0:
                        project_a(1)
                    e.wait_ge(negmax_done.sem, negmax_done.at(l, t + 1))
                    for h in range(8):
                        e.activation(sco[:, h, lo:256], sco[:, h, lo:256], ACT.Exp, bias=mx[:, 16 + h:17 + h],
                                     accum_out=mx[:, 32 + h:33 + h])
                    e.wait_ge(s_step.sem, s_step.at(l, 5 * t + 3))
                    e.activation(mx[:, 40:48], mx[:, 24:32], ACT.Exp).then_inc(exp_done.sem, 1)
                    if t == 1:
                        e.wait_ge(ob_lo.sem, ob_lo.at(l, 2))
                    for i in (((), (2, 3), (4, 5), ())[t]):
                        project_a(i)
                    if t == TT - 1:
                        gate_step(17)
                        gate_step(18)
                    if t >= 1:
                        e.wait_ge(pv_mm.sem, pv_mm.at(l, t))
                    for kt in ((0, 1) if t else (1,)):
                        probs_T(n, PS[:, 4:6, :], pT[:, 2 * kt:2 * kt + 2, :])
                        n += 1
                    e.wait_ge(pv_mm.sem, pv_mm.at(l, t + 1))
                    e.activation(oh[:, 4:8, t * P:(t + 1) * P], PS[:, 6, :].rearrange("p (a n) -> p a n", a=4),
                                 ACT.Copy).then_inc(o_hi.sem, 1)

                def gates_in(d):
                    for b in range(3):
                        e.dma_start(g_in[d % 2][b][:, :], gates_dram[8 * b + d]).then_inc(gate_back[d % 2].sem, 16)

                for q in range(2):
                    e.wait_ge(gate_out[q].sem, gate_out[q].at(l, 16 * 9))
                    gates_in(q)
                e.wait_ge(vt_mm.sem, vt_mm.at(l, 2))
                e.activation(v_tok[:, :, :].rearrange("p t (y n) -> p y t n", y=2),
                             PS[:, 6:8, :].rearrange("p y (t n) -> p y t n", t=TT), ACT.Copy).then_inc(vt_done.sem, 1)
                for t in range(TT):
                    w = (t + 1) * P
                    e.wait_ge(negmax_done.sem, negmax_done.at(l, 4 + t + 1))
                    for h in range(4):
                        sh = sco[:, 2 * h:2 * h + 2, :].rearrange("p a n -> p (a n)")
                        last = e.activation(sh[:, 0:w], sh[:, 0:w], ACT.Exp, bias=mx[:, 16 + h:17 + h],
                                            accum_out=mx[:, 32 + h:33 + h])
                    last.then_inc(exp_done.sem, 1)
                    gate_step(19 + t)
                    if t == TT - 1:
                        gate_step(23)
                    if t >= 1:
                        e.wait_ge(pv_mm.sem, pv_mm.at(l, 4 + t))
                    for kt in range(t + 1):
                        probs_T(n, PS[:, 4 + kt % 2, :], pT[:, kt, :])
                        n += 1
                    e.wait_ge(pv_mm.sem, pv_mm.at(l, 4 + t + 1))
                    e.activation(oh[:, 0:2, t * P:(t + 1) * P], PS[:, 6, 0:256].rearrange("p (a n) -> p a n", a=2),
                                 ACT.Copy).then_inc(o_hi.sem, 1)
                def sigmoids(d):
                    e.wait_ge(gate_back[d % 2].sem, gate_back[d % 2].at(l, 48 * (d // 2 + 1)))
                    for b in range(3):
                        last = e.activation(g_in[d % 2][b][:, :], g_in[d % 2][b][:, :], ACT.Sigmoid)
                    last.then_inc(sig_done.sem, 1)

                sigmoids(0)
                for q in range(2):
                    e.wait_ge(gate_out[q].sem, gate_out[q].at(l, 16 * 12))
                for d in range(KD):
                    ahead(U_UP + d)
                    if d + 1 < KD:
                        sigmoids(d + 1)
                    e.wait_ge(merge_step.sem, merge_step.at(l, 2 * (d + 1)))
                    e.activation(uh[:, d, :], up_m[:, 3 + d % 2, :], ACT.Copy).then_inc(mh_done.sem, 1)
                    if d + 2 < KD:
                        e.wait_ge(mg_used.sem, mg_used.at(l, d + 1))
                        gates_in(d + 2)
                for d in range(KD):
                    if d < KD - 1:
                        ahead(U_OUT + d)
                    if d == 1:
                        e.activation(warm[:, 0:1], eps[:, 0:1], ACT.Sqrt)
                    e.wait_ge(x_done.sem, x_done.at(l, out_index(l, 1, 0, d) + 1))
                    square(l, 1, d)

            e.wait_ge(cond_in.sem, 16)
            e.activation(cond[:, :], cond[:, :], ACT.Silu).then_inc(cond_done.sem, 1)
            e.sem_inc(hi_ready.sem, RAW)
            e.wait_ge(x_in.sem, 16)
            for d in range(KD):
                square(0, -1, d)
            e.wait_ge(consts_in.sem, 16 * 6)
            with e.Fori(0, DEPTH) as l:
                norm(l, 0, 0)
                ffn(l, 0, 0, False)
                norm(l, 1, SUB)
                mixing(l)
                norm(l, 2, 2 * SUB)
                ffn(l, 2, 2 * SUB, True)
            root(DEPTH, 0)

        @block.vector
        def _(e):
            TTo, TS, STT = e.tensor_tensor, e.tensor_scalar, e.scalar_tensor_tensor

            def split(l, m0, i, j, K):
                e.wait_ge(hi_ready.sem, l * UNITS + 4 * i + (4 * m0 + j + 1 + RAW))
                TTo(wl[:, j % 2, 0:K * P], raw[:, j, 0:K * P], wh[:, j % 2, 0:K * P], ALU.subtract)\
                    .then_inc(lo_ready.sem, 1)

            def multiplied(l, n, i=0):
                e.wait_ge(unit_done.sem, l * UNITS + 4 * i + (n + 3))

            def add_square(l, s, d):
                if d == 0 or d == KD - 1:
                    return
                e.wait_ge(sq_done.sem, sq_done.at(l, 8 * (s + 1) + d + 1))
                if d >= 2:
                    e.wait_ge(ssq_done.sem, ssq_done.at(l, 6 * (s + 1) + d - 1))
                TTo(ssq[:, :], ssq[:, :], sq[:, d % 2, :], ALU.add).then_inc(ssq_done.sem, 1)

            def inverse_root(l, s):
                e.wait_ge(root_done.sem, root_done.at(l, s + 1))
                e.reciprocal(rstd_tok[:, :], root_tok[:, :]).then_inc(rstd_done.sem, 1)

            def norm(l, s, n):
                e.wait_ge(ada_ready.sem, l * 48 + 16 * (s + 1))
                q = bass.ds(l * 3 + s, 1)
                STT(out=scale_eff[:, :], in0=ada_sum[:, 8:16], scalar=1.0,
                    in1=norm_g[:, q, :].rearrange("p a n -> p (a n)"), op0=ALU.add, op1=ALU.mult)\
                    .then_inc(mods_done.sem, 1)
                e.wait_ge(mods_done.sem, mods_done.at(l, s + 1))
                inverse_root(l, s)
                if s == 0:
                    split(l, n // 4, 0, 0, KD)
                split(l, n // 4, 0, 1, KD)
                e.wait_ge(rstd_mm.sem, rstd_mm.at(l, s + 1))

                def scaled(k):
                    if k >= 4:
                        e.wait_ge(ul_done.sem, ul_done.at(l, 8 * s + k - 3))
                    STT(out=t_buf[:, k % 4, :], in0=x[:, k, :], scalar=scale_eff[:, k:k + 1], in1=PS[:, 6, :],
                        op0=ALU.mult, op1=ALU.mult).then_inc(t_done.sem, 1)
                scaled(0)
                scaled(1)
                for k in range(KD):
                    e.wait_ge(uh_done.sem, uh_done.at(l, 8 * s + k + 1))
                    STT(out=ul[:, k, :], in0=t_buf[:, k % 4, :], scalar=ada_sum[:, k:k + 1], in1=uh[:, k, :],
                        op0=ALU.add, op1=ALU.subtract).then_inc(ul_done.sem, 1)
                    if k + 2 < KD:
                        scaled(k + 2)

            def gate_mods(l, s):
                e.wait_ge(ada_gate_ready.sem, l * 24 + 8 * (s + 1))
                TS(gate_eff[:, :], ada_sum[:, 16:24], 1.0 if s == 1 else 0.5, None, ALU.mult)\
                    .then_inc(gate_mods_done.sem, 1)
                e.wait_ge(gate_mods_done.sem, gate_mods_done.at(l, s + 1))

            def residual(l, s, half, d, bank):
                STT(out=x[:, d, :], in0=PS[:, bank, :], scalar=gate_eff[:, d:d + 1], in1=x[:, d, :],
                    op0=ALU.mult, op1=ALU.add).then_inc(x_done.sem, 1)

            def ffn(l, s, first, last):
                base_f = 22 * (s // 2)
                for half, F in enumerate(F_HALF):
                    f0 = base_f + F_HALF[0] * half

                    def use_in(i, j):
                        if j % 2 == 0:
                            return
                        f = l * 44 + 2 * i + (f0 + j // 2)
                        multiplied(l, first + j, i)
                        e.wait_ge(silu_done.sem, f + 3)
                        TTo(h32[:, j // 2, :], silu_s[:, j // 2, :], PS[:, 2 + j // 2, :], ALU.mult)\
                            .then_inc(h_done.sem, 1)
                        e.wait_ge(hh_done.sem, f + 1)
                        slot = bass.ds(2 * i + j // 2, 1)
                        TTo(hl[:, slot, :].rearrange("p a n -> p (a n)"), h32[:, j // 2, :],
                            hh[:, slot, :].rearrange("p a n -> p (a n)"), ALU.subtract).then_inc(hl_done.sem, 1)

                    steps(e, l, first, 2 * F, KD, F, split, use_in)
                    first += 2 * F
                    if half == 0:
                        gate_mods(l, s)

                    def use_out(i, j):
                        multiplied(l, first + j, i)
                        residual(l, s, half, 4 * i + j, 4 + j % 2)
                        if half == 1:
                            add_square(l, s, 4 * i + j)
                    steps(e, l, first, 8, F, KD if half == 0 or not last else None, split, use_out, half == 1)
                    first += 8

            def mixing(l):
                def ahead(n):
                    split(l, (n + 2) // 4, 0, (n + 2) % 4, KD)

                def ab_decay():
                    e.wait_ge(ab_a.sem, ab_a.at(l, 4))
                    STT(out=sc[:, 192:208], in0=sc[:, 64:80], scalar=0.0, in1=sc[:, 112:128], op0=ALU.max, op1=ALU.add)\
                        .then_inc(ab_v.sem, 1)
                    e.wait_ge(ab_v.sem, ab_v.at(l, 3))
                    STT(out=by_t(0), in0=by_t(192), scalar=-1.0,
                        in1=sc[:, 224:228].unsqueeze(1).broadcast_to([P, TT, 4]), op0=ALU.mult, op1=ALU.mult)\
                        .then_inc(ab_v.sem, 1)

                e.wait_ge(ab_hi_done.sem, ab_hi_done.at(l, 1))
                e.wait_ge(tables_in.sem, 16 * 9)
                TTo(ab_lo[:, :, :], ab_raw[:, :, :], ab_hi[:, :, :], ALU.subtract).then_inc(ab_lo_done.sem, 1)
                by_t = lambda c: sc[:, c:c + 16].rearrange("p (t s) -> p t s", t=TT)
                for m in range(14):
                    if m == 13:
                        ab_decay()
                    ahead(MIX + m)
                    if m < 6:
                        e.wait_ge(in_done.sem, in_done.at(l, m + 1))
                        if m >= 2:
                            e.wait_ge(conv_silu.sem, conv_silu.at(l, m - 1))
                        y, v = t_buf[:, m % 2, :], bp[:, m, :]
                        TS(y, v, conv_w[:, m, 3:4], None, ALU.mult).then_inc(conv_step.sem, 1)
                        for back in (1, 2, 3):
                            e.wait_ge(conv_step.sem, conv_step.at(l, 3 * m + back))
                            STT(out=y[:, back:], in0=v[:, :SEQ - back], scalar=conv_w[:, m, 3 - back:4 - back],
                                in1=y[:, back:], op0=ALU.mult, op1=ALU.add)\
                                .then_inc((conv_step if back < 3 else conv_done).sem, 1)
                    if m == 6:
                        TTo(a_bias[:, :, :], a_bias[:, :, :], a_mask[:, :].unsqueeze(1).broadcast_to([P, 4, 2 * P]),
                            ALU.add).then_inc(bias_masked.sem, 1)
                    if m == 8:
                        e.wait_ge(ab_mm.sem, ab_mm.at(l, 1))
                        e.tensor_copy(ab_T[:, :], PS[0:8, 6, :]).then_inc(ab_copied.sem, 1)
                    if m == 9:
                        e.wait_ge(ab_tr.sem, ab_tr.at(l, 1))
                        e.tensor_copy(sc[:, 32:64], PS[:, 6, 0:32]).then_inc(ab_v.sem, 1)
                        e.wait_ge(ab_v.sem, ab_v.at(l, 1))
                        TTo(by_t(64), sc[:, 32:64].rearrange("p (t s) -> p t s", t=TT)[:, :, 0:4],
                            small[:, 0:4].unsqueeze(1).broadcast_to([P, TT, 4]), ALU.add).then_inc(ab_v.sem, 1)
                    if m >= 10:
                        i = m - 10
                        e.wait_ge(l2_root.sem, l2_root.at(l, i + 1))
                        e.reciprocal(h32[:, i % 2, :], h32[:, i % 2, :]).then_inc(l2_inv.sem, 1)
                        e.wait_ge(l2_inv.sem, l2_inv.at(l, i + 1))
                        STT(out=bp[:, i, :], in0=bp[:, i, :], scalar=HEAD ** -0.5 if i < 2 else 1.0,
                            in1=h32[:, i % 2, :], op0=ALU.mult, op1=ALU.mult).then_inc(qk_done.sem, 1)
                gate_mods(l, 1)
                e.wait_ge(gc_mm.sem, gc_mm.at(l, 1))
                e.tensor_copy(sc[:, 128:160], PS[:, 6, 32:64]).then_inc(ab_v.sem, 1)
                e.wait_ge(ab_v.sem, ab_v.at(l, 5))
                TTo(sc[:, 208:224], sc[:, 144:160], sc[:, 128:144], ALU.subtract).then_inc(ab_v.sem, 1)
                e.wait_ge(ab_a.sem, ab_a.at(l, 7))
                TTo(sc[:, 192:208], sc[:, 16:32], sc[:, 176:192], ALU.mult).then_inc(ab_v.sem, 1)

                by_s = lambda m: m.unsqueeze(1).broadcast_to([P, 4, P])
                heads = lambda v: v.rearrange("p (a b n) -> p b a n", a=2, b=2)
                slots = lambda v: v.rearrange("p (b a) n -> p b a n", a=2)
                ps4 = lambda b: PS[:, b, :].rearrange("p (s n) -> p s n", s=4)

                def per_head(c):
                    return sc[:, c:c + 4].rearrange("p (b a) -> p b a", a=2).unsqueeze(3).broadcast_to([P, 2, 2, HEAD])


                def differences(t):
                    e.wait_ge(gcb_mm.sem, gcb_mm.at(l, t + 1))
                    if t >= 2:
                        e.wait_ge(ct_done.sem, ct_done.at(l, 6 * (t - 1)))
                    for s in range(4):
                        last = TS(lT[t % 2][:, s, :], PS[:, 4 if t else 5, s * P:(s + 1) * P],
                                  sc[:, 128 + 4 * t + s:129 + 4 * t + s], 0.0, ALU.subtract, ALU.min)
                    last.then_inc(diff_done.sem, 1)

                def within(t):
                    e.wait_ge(decay_done.sem, decay_done.at(l, t + 1))
                    TTo(dcy[:, :, :], dcy[:, :, :], by_s(tri[:, :]), ALU.mult).then_inc(mask_step.sem, 1)
                    e.wait_ge(kk_mm.sem, kk_mm.at(l, t + 1))
                    e.wait_ge(mask_step.sem, mask_step.at(l, 4 * t + 1))
                    for par in range(2):
                        last = TTo(intra[:, t, 2 * par:2 * par + 2, :],
                                   PS[:, 2 + par, 256:512].rearrange("p (a n) -> p a n", a=2),
                                   dcy[:, 2 * par:2 * par + 2, :], ALU.mult)
                    last.then_inc(mask_step.sem, 1)

                def lower(t):
                    e.wait_ge(mask_step.sem, mask_step.at(l, 4 * t + 2))
                    TTo(dcy[:, :, :], dcy[:, :, :], by_s(strict[:, :]), ALU.mult).then_inc(mask_step.sem, 1)
                    e.wait_ge(mask_step.sem, mask_step.at(l, 4 * t + 3))
                    for par in range(2):
                        last = TTo(lT[t % 2][:, 2 * par:2 * par + 2, :],
                                   PS[:, 2 + par, 0:256].rearrange("p (a n) -> p a n", a=2),
                                   dcy[:, 2 * par:2 * par + 2, :], ALU.mult)
                    last.then_inc(mask_step.sem, 1)
                    e.wait_ge(bb_mm.sem, bb_mm.at(l, t + 1))
                    e.wait_ge(mask_step.sem, mask_step.at(l, 4 * t + 4))
                    TTo(lT[t % 2][:, :, :], lT[t % 2][:, :, :], ps4(4 if t else 6), ALU.mult).then_inc(lt_done.sem, 1)

                def decayed_q(t):
                    e.wait_ge(kk_mm.sem, kk_mm.at(l, t + 1))
                    e.wait_ge(eg_done.sem, eg_done.at(l, t + 1))
                    e.tensor_copy(egl[:, t, :, :], eg[:, :, CHUNK - 1::CHUNK])
                    TTo(bp[:, 0:2, t * P:(t + 1) * P], bp[:, 0:2, t * P:(t + 1) * P], eg[:, :, :], ALU.mult)\
                        .then_inc(qe_done.sem, 1)

                def rope(i):
                    e.wait_ge(rot_mm.sem, rot_mm.at(l, i + 1))
                    TTo(sq[:, i % 2, :], PS[:, 2 + i // 4, :], sin[:, :], ALU.mult).then_inc(rot_step.sem, 1)
                    TTo(ct[i][:, :], ct[i][:, :], cos[:, :], ALU.mult).then_inc(rot_step.sem, 1)
                    e.wait_ge(rot_step.sem, rot_step.at(l, 2 * i + 2))
                    TTo(ct[i][:, :], ct[i][:, :], sq[:, i % 2, :], ALU.add).then_inc(rope_done.sem, 1)

                differences(0)
                within(0)
                lower(0)
                decayed_q(0)
                ahead(MIX + gate_unit(0))
                for t in range(TT):
                    e.wait_ge(lt_done.sem, lt_done.at(l, t + 1))

                    def blocks(lv):
                        g = 6 * t + lv
                        if g >= 1:
                            e.wait_ge(y_mm.sem, y_mm.at(l, g))
                        if lv == 1:
                            e.wait_ge(u_done.sem, u_done.at(l, 6 * t + 1))
                        TTo(cT[:, :, :], lT[t % 2][:, :, :], by_s(level_mask[:, lv, :]), ALU.mult)\
                            .then_inc(ct_done.sem, 1)

                    blocks(0)
                    e.wait_ge(ct_done.sem, ct_done.at(l, 6 * t + 1))
                    if t >= 1:
                        e.wait_ge(uw_mm.sem, uw_mm.at(l, t))
                    TTo(Um[:, :, :], by_s(ident[:, :]), cT[:, :, :], ALU.subtract).then_inc(u_done.sem, 1)
                    for lv in range(LEVELS):
                        g = 6 * t + lv
                        if lv == 0:
                            e.wait_ge(y_mm.sem, y_mm.at(l, g + 1))
                            TTo(Tm[:, :, :], by_s(ident[:, :]), ps4(7), ALU.subtract).then_inc(tm_done.sem, 1)
                        if lv < LEVELS - 1:
                            blocks(lv + 1)
                        if g % 2 == 0 and g >= 2:
                            ahead(MIX + gate_unit(g // 2))
                        if lv == LEVELS - 1 and t + 1 < TT:
                            lower(t + 1)
                        if lv >= 1:
                            e.wait_ge(z_mm.sem, z_mm.at(l, 5 * t + lv))
                            if lv < LEVELS - 1:
                                TTo(Tm[:, :, :], Tm[:, :, :], ps4(7), ALU.subtract).then_inc(tm_done.sem, 1)
                            e.wait_ge(u_done.sem, u_done.at(l, g))
                            TTo(Um[:, :, :], Um[:, :, :], ps4(6), ALU.subtract).then_inc(u_done.sem, 1)
                        if lv == 0:
                            e.wait_ge(tr_mm.sem, tr_mm.at(l, t + 1))
                            e.wait_ge(ab_v.sem, ab_v.at(l, 7))
                            TTo(slots(v_beta[:, :, :]), heads(PS[:, 4, 256:512]), per_head(16 + 4 * t), ALU.mult)
                            TTo(slots(k_beta[:, :, :]), heads(PS[:, 4, 0:256]), per_head(192 + 4 * t), ALU.mult)
                            TTo(slots(k_dec[:, t, :, :]), heads(PS[:, 4, 0:256]), per_head(160 + 4 * t), ALU.mult)\
                                .then_inc(tok_done.sem, 1)
                        if lv == 1:
                            rope(t)
                        if t + 1 < TT:
                            if lv == 2:
                                differences(t + 1)
                            if lv == 4:
                                within(t + 1)
                            if lv == 5:
                                decayed_q(t + 1)
                        elif lv == 4:
                            rope(4)
                e.memset(st[:, 0, :, :], 0.0).then_inc(st_zero.sem, 1)
                e.wait_ge(uw_done.sem, uw_done.at(l, TT))
                e.wait_ge(qe_done.sem, qe_done.at(l, TT))
                e.wait_ge(st_zero.sem, st_zero.at(l, 1))
                for n in range(NCH):
                    t, pb = n // 2, 64 * (n % 2)
                    e.wait_ge(ws_mm.sem, ws_mm.at(l, n + 1))
                    for par in range(2):
                        v = u_val[pb:pb + 64, t, 2 * par:2 * par + 2, :]
                        last = TTo(v, v, PS[pb:pb + 64, 2 + par, 0:2 * HEAD].rearrange("p (a n) -> p a n", a=2),
                                   ALU.subtract)
                    last.then_inc(vnew_done.sem, 1)
                    e.wait_ge(kv_mm.sem, kv_mm.at(l, n + 1))
                    if n >= 1:
                        e.wait_ge(st_done.sem, st_done.at(l, n))
                    for pair in range(2):
                        last = STT(out=st[:, n + 1, pair, :], in0=st[:, n, pair, :], scalar=egl[:, t, pair, n % 2:n % 2 + 1],
                                   in1=PS[:, 4 + n % 2, pair * HEAD:(pair + 1) * HEAD], op0=ALU.mult, op1=ALU.add)
                    last.then_inc(st_done.sem, 1)
                    if n % 2 == 0:
                        ahead(MIX + gate_unit(12 + n // 2))
                ahead(MIX + gate_unit(16))
                for i in range(2):
                    e.wait_ge(on_root.sem, on_root.at(l, i + 1))
                    e.reciprocal(h32[:, i, :], h32[:, i, :]).then_inc(on_step.sem, 1)
                    e.wait_ge(on_step.sem, on_step.at(l, 3 * i + 1))
                    STT(out=bp[:, 4 + i, :], in0=bp[:, 4 + i, :], scalar=small[:, 8:9], in1=h32[:, i, :],
                        op0=ALU.mult, op1=ALU.mult).then_inc(on_step.sem, 1)
                    e.wait_ge(on_step.sem, on_step.at(l, 3 * i + 2))
                    e.wait_ge(on_silu.sem, on_silu.at(l, i + 1))
                    TTo(bp[:, 4 + i, :], bp[:, 4 + i, :], bp[:, 6 + i, :], ALU.mult).then_inc(on_step.sem, 1)
                for i in range(2):
                    e.wait_ge(ob_hi.sem, ob_hi.at(l, i + 1))
                    TTo(ol[:, 2 + i, :], bp[:, 4 + i, :], oh[:, 2 + i, :], ALU.subtract).then_inc(ob_lo.sem, 1)

                n_pt = 0
                ahead(MIX + M_A)
                for t in range(TT):
                    lo = 0 if t else P
                    e.wait_ge(s_mm.sem, s_mm.at(l, t + 1))
                    if t >= 1:
                        e.wait_ge(pt_mm.sem, pt_mm.at(l, n_pt))
                    n_pt += 2 if t else 1
                    STT(out=sco[:, :, lo:256], in0=PS[:, 0:4, :].rearrange("p b (c n) -> p (b c) n", c=2)[:, :, lo:256],
                        scalar=HEAD ** -0.5, in1=c_mask[:, :].unsqueeze(1).broadcast_to([P, 8, 2 * P])[:, :, lo:256],
                        op0=ALU.mult, op1=ALU.add).then_inc(bias_done.sem, 1)
                    if t == 0:
                        ahead(MIX + M_A + 1)
                    e.wait_ge(bias_done.sem, bias_done.at(l, t + 1))
                    e.tensor_reduce(mx[:, 0:8], sco[:, :, lo:256], AX.X, ALU.max).then_inc(s_step.sem, 1)
                    e.wait_ge(s_step.sem, s_step.at(l, 5 * t + 1))
                    TTo(mx[:, 8:16], mx[:, 0:8], small[:, 16:24], ALU.max).then_inc(s_step.sem, 1)
                    e.wait_ge(s_step.sem, s_step.at(l, 5 * t + 2))
                    TS(mx[:, 16:24], mx[:, 8:16], -1.0, None, ALU.mult).then_inc(negmax_done.sem, 1)
                    TTo(mx[:, 24:32], small[:, 16:24], mx[:, 8:16], ALU.subtract).then_inc(s_step.sem, 1)
                    e.wait_ge(exp_done.sem, exp_done.at(l, t + 1))
                    TTo(mx[:, 48:56], mx[:, 32:40], mx[:, 40:48], ALU.add).then_inc(s_step.sem, 1)
                    e.wait_ge(s_step.sem, s_step.at(l, 5 * t + 4))
                    e.reciprocal(mx[:, 56:64], mx[:, 48:56]).then_inc(s_step.sem, 1)
                    e.wait_ge(s_step.sem, s_step.at(l, 5 * t + 5))
                    TTo(sco[:, :, lo:256], sco[:, :, lo:256],
                        mx[:, 56:64].unsqueeze(2).broadcast_to([P, 8, 2 * P])[:, :, lo:256], ALU.mult)\
                        .then_inc(prob_done.sem, 1)
                    for m in ((), (M_A + 2, M_A + 3), (M_A + 4, M_A + 5), (gate_unit(17), gate_unit(18)))[t]:
                        ahead(MIX + m)
                    e.wait_ge(o_hi.sem, o_hi.at(l, t + 1))
                    TTo(ol[:, 4:8, t * P:(t + 1) * P], PS[:, 6, :].rearrange("p (a n) -> p a n", a=4),
                        oh[:, 4:8, t * P:(t + 1) * P], ALU.subtract).then_inc(o_lo.sem, 1)

                e.wait_ge(bias_masked.sem, bias_masked.at(l, 1))
                sA = sco[:, :, :].rearrange("p (h a) n -> p h (a n)", a=2)
                for t in range(TT):
                    w, near = (t + 1) * P, max(t - 1, 0) * P
                    e.wait_ge(s_mm.sem, s_mm.at(l, 4 + t + 1))
                    e.wait_ge(pt_mm.sem, pt_mm.at(l, n_pt))
                    n_pt += t + 1
                    if near:
                        for h in range(4):
                            TS(sA[:, h, 0:near], PS[:, h, 0:near], HEAD ** -0.5, a_far[:, h:h + 1], ALU.mult, ALU.add)
                    STT(out=sA[:, :, near:w], in0=PS[:, 0:4, near:w], scalar=HEAD ** -0.5,
                        in1=a_bias[:, :, 256 - (w - near):256], op0=ALU.mult, op1=ALU.add).then_inc(bias_done.sem, 1)
                    e.wait_ge(bias_done.sem, bias_done.at(l, 4 + t + 1))
                    e.tensor_reduce(mx[:, 0:4], sA[:, :, 0:w], AX.X, ALU.max).then_inc(s_step.sem, 1)
                    e.wait_ge(s_step.sem, s_step.at(l, 20 + 2 * t + 1))
                    TS(mx[:, 16:20], mx[:, 0:4], -1.0, None, ALU.mult).then_inc(negmax_done.sem, 1)
                    e.wait_ge(exp_done.sem, exp_done.at(l, 4 + t + 1))
                    e.reciprocal(mx[:, 56:60], mx[:, 32:36]).then_inc(s_step.sem, 1)
                    e.wait_ge(s_step.sem, s_step.at(l, 20 + 2 * t + 2))
                    TTo(sA[:, :, 0:w], sA[:, :, 0:w], mx[:, 56:60].unsqueeze(2).broadcast_to([P, 4, w]), ALU.mult)\
                        .then_inc(prob_done.sem, 1)
                    ahead(MIX + gate_unit(19 + t))
                    if t == TT - 1:
                        ahead(MIX + gate_unit(23))
                    e.wait_ge(o_hi.sem, o_hi.at(l, 4 + t + 1))
                    TTo(ol[:, 0:2, t * P:(t + 1) * P], PS[:, 6, 0:256].rearrange("p (a n) -> p a n", a=2),
                        oh[:, 0:2, t * P:(t + 1) * P], ALU.subtract).then_inc(o_lo.sem, 1)

                def merged_lo(d):
                    e.wait_ge(mh_done.sem, mh_done.at(l, d + 1))
                    TTo(ul[:, d, :], up_m[:, 3 + d % 2, :], uh[:, d, :], ALU.subtract).then_inc(ml_done.sem, 1)

                for d in range(KD):
                    n = U_UP + d
                    if d >= 1:
                        e.wait_ge(merge_step.sem, merge_step.at(l, 2 * d))
                    ahead(n)
                    multiplied(l, n)
                    e.wait_ge(sig_done.sem, sig_done.at(l, d + 1))
                    for b in range(3):
                        last = TTo(up_m[:, b, :], g_in[d % 2][b][:, :], PS[:, 3 * (d % 2) + b, :], ALU.mult)
                    last.then_inc(mg_used.sem, 1)
                    e.wait_ge(mg_used.sem, mg_used.at(l, d + 1))
                    TTo(up_m[:, 0, :], up_m[:, 0, :], up_m[:, 1, :], ALU.add).then_inc(merge_step.sem, 1)
                    e.wait_ge(merge_step.sem, merge_step.at(l, 2 * d + 1))
                    if d >= 2:
                        e.wait_ge(ml_done.sem, ml_done.at(l, d - 1))
                    TTo(up_m[:, 3 + d % 2, :], up_m[:, 0, :], up_m[:, 2, :], ALU.add).then_inc(merge_step.sem, 1)
                    if d >= 1:
                        merged_lo(d - 1)
                merged_lo(KD - 1)
                for d in range(KD):
                    n = U_OUT + d
                    if d < KD - 1:
                        ahead(n)
                    multiplied(l, n)
                    residual(l, 1, 0, d, 6 + d % 2)
                    add_square(l, 1, d)

            for s in (lo_ready, unit_done, silu_done, h_done, x_done, in_done, mg_used):
                e.sem_inc(s.sem, s.credit)
            e.wait_ge(cond_done.sem, 1)
            for lot in range(ADA_LOTS):
                e.wait_ge(ada0_in[lot].sem, 32)
                for v in (lot, KD + lot):
                    STT(out=ada0[:, v, :], in0=ada0[:, v, :], scalar=1.0, in1=cond[:, :], op0=ALU.mult,
                        op1=ALU.mult, accum_out=ada_sum[:, v:v + 1]).then_inc(ada0_step.sem, 1)
            e.wait_ge(consts_in.sem, 16 * 6)
            e.wait_ge(ada0_step.sem, 16)
            TTo(ada_sum[:, 0:16], ada_sum[:, 0:16], ada_b[:, 0:16], ALU.add).then_inc(ada_ready.sem, 16)
            with e.Fori(0, DEPTH) as l:
                norm(l, 0, 0)
                ffn(l, 0, 0, False)
                norm(l, 1, SUB)
                mixing(l)
                norm(l, 2, 2 * SUB)
                ffn(l, 2, 2 * SUB, True)
            inverse_root(DEPTH, 0)
            e.wait_ge(rstd_mm.sem, 3 * DEPTH + 1)
            for d in range(KD):
                if d >= 2:
                    e.wait_ge(out_done[d % 2].sem, 16 * (d // 2))
                STT(out=sq[:, d % 2, :], in0=x[:, d, :], scalar=final_g[:, d:d + 1], in1=PS[:, 6, :],
                    op0=ALU.mult, op1=ALU.mult).then_inc(out_ready.sem, 1)


def _units(w, cols):
    L, K, _ = w.shape
    w = w[:, :, cols].reshape(L, K // P, P, len(cols) // P, P)
    return np.ascontiguousarray(w.transpose(0, 3, 2, 1, 4)).reshape(-1, P, K // P * P)


def _cols(v):
    v = v.reshape(v.shape[:-1] + (v.shape[-1] // P, P))
    return np.ascontiguousarray(np.moveaxis(v, -1, 0))


def _layout(i):
    f32 = np.float32
    L = DEPTH
    i = {k: np.asarray(v) for k, v in i.items()}
    o = {}
    o["x"] = _cols(i["x"].reshape(SEQ, D_MODEL)).transpose(0, 2, 1)
    o["c"] = i["c"].reshape(1, D_MODEL)
    o["ada_w"] = np.ascontiguousarray(i["ada_w"].transpose(0, 2, 1)).reshape(-1, P, D_MODEL)
    o["ada_b"] = _cols(i["ada_b"].reshape(6 * 3 * D_MODEL))
    o["norm_g"] = _cols(np.stack([i["ffn1_norm_g"], i["mix_norm_g"], i["ffn2_norm_g"]], 1).reshape(6, D_MODEL))
    o["final_g"] = _cols(i["final_norm_g"])
    F = D_FF // P
    pairs = np.stack([np.arange(D_FF).reshape(F, P), D_FF + np.arange(D_FF).reshape(F, P)], 1).reshape(-1)
    for n in ("ffn1", "ffn2"):
        o[n + "_in"] = _units(i[n + "_w_in"], pairs)
        cut = F_HALF[0] * P
        o[n + "_out0"] = _units(i[n + "_w_out"][:, :cut], np.arange(D_MODEL))
        o[n + "_out1"] = _units(i[n + "_w_out"][:, cut:], np.arange(D_MODEL))
    AQ, AK, AV, BQ, BZ, BA, BB, CQ, CK, CV, G = np.cumsum([0, 256, 256, 256, 768, 256, 4, 4, 512, 128, 128])
    r = np.arange
    cq = np.concatenate([CQ + 64 * h + r(64) for j in range(4) for h in (j, j + 4)])
    cols = np.concatenate([BQ + r(768), BZ + r(256), cq, CK + r(128), CV + r(128), G + r(2176),
                           AQ + r(256), AK + r(256), AV + r(256), G + 2176 + r(896)])
    o["mix_in"] = _units(i["mix_w_in"], cols)
    slot = np.array(HEAD_OF_SLOT)
    ab = i["mix_w_in"][:, :, np.concatenate([BA + slot, BB + slot])]
    o["w_ab"] = np.ascontiguousarray(ab.reshape(L, KD, P, 8).transpose(0, 2, 1, 3))
    up_c = i["w_up_c"][:, np.concatenate([64 * h + r(64) for j in range(4) for h in (j, j + 4)])]
    o["mix_up"] = _units(np.concatenate([i["w_up_a"], i["w_up_b"], up_c], 1), r(D_MODEL))
    o["mix_out"] = _units(i["mix_w_out"], r(D_MODEL))
    p, j = r(P)[:, None], r(2 * P)[None, :]
    rel = np.clip(P + p - j, -(CHUNK - 1), 128) + CHUNK - 1
    o["a_bias"] = np.ascontiguousarray(i["a_rel_bias"][:, :, rel].transpose(0, 2, 1, 3))
    o["a_far"] = np.ascontiguousarray(np.broadcast_to(i["a_rel_bias"][:, None, :, -1], (L, P, 4)))
    o["conv_w"] = np.ascontiguousarray(i["b_conv_w"].reshape(L, 4, 6, P).transpose(0, 3, 2, 1))
    small = np.zeros((L, P, 32), f32)
    small[:, :, 0:4] = i["b_dt_bias"][:, None, slot]
    small[:, :, 4:8] = i["b_a_log"][:, None, slot]
    small[:, 0:64, 8] = i["b_norm_g"]
    small[:, 64:128, 8] = i["b_norm_g"]
    small[:, :, 16:24] = i["c_sinks"][:, None, :]
    o["small"] = small
    q, c = r(P)[:, None], r(P)[None, :]
    same = q // CHUNK == c // CHUNK
    o["ident"] = np.eye(P, dtype=f32)
    o["ones_mean"] = np.full((P, P), 1.0 / D_MODEL, f32)
    o["eps"] = np.stack([np.full(P, EPS, f32), np.ones(P, f32)], 1)
    o["tri"] = (same & (q <= c)).astype(f32)
    o["same_chunk"] = same.astype(f32)
    o["strict"] = (q < c).astype(f32)
    o["level_mask"] = np.stack([(c // 2 ** v == q // 2 ** v + 1) & (q // 2 ** v % 2 == 0) for v in range(LEVELS)], 1).astype(f32)
    rot = np.zeros((P, P), f32)
    for h in range(2):
        for d in range(32):
            rot[64 * h + 32 + d, 64 * h + d] = -1.0
            rot[64 * h + d, 64 * h + 32 + d] = 1.0
    o["rot"] = rot
    inv = np.float32(10000.0) ** (-np.arange(32, dtype=f32) / np.float32(32))
    ang = np.arange(SEQ, dtype=f32)[None, :] * inv[:, None].astype(f32)
    o["cos"] = np.tile(np.cos(ang).astype(f32), (4, 1))
    o["sin"] = np.tile(np.sin(ang).astype(f32), (4, 1))
    kc, qc = j // CHUNK - 2, p // CHUNK
    o["c_mask"] = np.where((kc == qc) | (kc == qc - 1), 0.0, NEG).astype(f32)
    o["a_mask"] = np.where(kc <= qc, 0.0, NEG).astype(f32)
    return {k: np.ascontiguousarray(v) for k, v in o.items()}


def kernel(**inputs):
    import concourse.bacc as _bacc
    from concourse.bass_utils import run_bass_kernel_spmd as _run

    nc = _bacc.Bacc("TRN2", target_bir_lowering=False, num_devices=1)
    arrays, aps = {}, {}
    for name, v in _layout(inputs).items():
        arrays[f"in_{name}_dram"] = v
        aps[name] = nc.dram_tensor(f"in_{name}_dram", v.shape, mybir.dt.from_np(v.dtype), kind="ExternalInput").ap()
    out = nc.dram_tensor("out_dram", (P, KD, SEQ), F32, kind="ExternalOutput").ap()
    encoder_kernel(nc, aps, out)
    r = _run(nc, [arrays], core_ids=[0])
    got = r.results[0]["out_dram"]
    return np.ascontiguousarray(got.transpose(2, 1, 0)).reshape(1, SEQ, D_MODEL)
```
